# Optimizing a Trainium2 kernel written in Bass

```python
import jax, jax.numpy as jnp
from jax import lax
import numpy as np

D_MODEL = 1024
BATCH = 1
SEQ = 256
DEPTH = 2

RWKV_HEADS = 8
RWKV_HEAD_DIM = 64
RWKV_WIDTH = RWKV_HEADS * RWKV_HEAD_DIM
DECAY_LORA = 64
ICLR_LORA = 64
GATE_LORA = 128
RWKV_GN_EPS = 64e-5
GDN_HEADS = 4
GDN_HEAD_DIM = 128
GDN_WIDTH = GDN_HEADS * GDN_HEAD_DIM
CONV_WIDTH = 4
CHUNK = 64
D_FF = 2816
N_EXPERTS = 8
TOP_K = 2
NORM_EPS = 1e-6

RWKV_SPLITS = (RWKV_WIDTH, RWKV_WIDTH, RWKV_WIDTH, DECAY_LORA, ICLR_LORA, GATE_LORA)
RWKV_COLS = sum(RWKV_SPLITS)
GDN_SPLITS = (3 * GDN_WIDTH, GDN_HEADS, GDN_HEADS, GDN_WIDTH)
GDN_COLS = sum(GDN_SPLITS)
GATE_COLS = 2 * D_MODEL
IN_COLS = RWKV_COLS + GDN_COLS + GATE_COLS
N_DENSE = (DEPTH + 1) // 2
N_MOE = DEPTH // 2

kernel_name = 'hybrid_rwkv7_gdn_moe_trunk'

def _split(t, sizes):
    return jnp.split(t, np.cumsum(sizes)[:-1].tolist(), axis=-1)

def rms_norm(x, g, eps=NORM_EPS):
    xf = x.astype(jnp.float32)
    y = xf * lax.rsqrt(jnp.mean(xf * xf, axis=-1, keepdims=True) + eps)
    return (y * g.astype(jnp.float32)).astype(x.dtype)

def l2_normalize(x, eps=1e-6):
    return x * lax.rsqrt(jnp.sum(x * x, axis=-1, keepdims=True) + eps)

def causal_depthwise_conv(x, w):
    K, C = w.shape
    return lax.conv_general_dilated(x, w[:, None, :], window_strides=(1,), padding=[(K - 1, 0)],
                                    dimension_numbers=('NWC', 'WIO', 'NWC'), feature_group_count=C)

def swiglu(h, w_gate, w_up, w_down):
    return (jax.nn.silu(h @ w_gate) * (h @ w_up)) @ w_down

def rwkv7_recurrence(r, w, k, v, a, b):
    B, T, H, N = r.shape

    def step(S, inp):
        r_t, w_t, k_t, v_t, a_t, b_t = inp
        sa = jnp.einsum('bhvk,bhk->bhv', S, a_t)
        S = S * w_t[:, :, None, :] + sa[..., None] * b_t[:, :, None, :] + v_t[..., None] * k_t[:, :, None, :]
        return S, jnp.einsum('bhvk,bhk->bhv', S, r_t)

    xs = tuple(jnp.moveaxis(t, 1, 0) for t in (r, w, k, v, a, b))
    _, o = lax.scan(step, jnp.zeros((B, H, N, N), jnp.float32), xs)
    return jnp.moveaxis(o, 0, 1)

def chunked_gated_delta_rule(q, k, v, g_log, beta):
    B, T, H, dk = q.shape
    dv = v.shape[-1]
    C = CHUNK
    NC = T // C
    q = q * (dk ** -0.5)

    def to_chunks(t):
        return t.reshape(B, NC, C, H, -1).transpose(0, 3, 1, 2, 4)

    q, k, v = to_chunks(q), to_chunks(k), to_chunks(v)
    g_log = g_log.reshape(B, NC, C, H).transpose(0, 3, 1, 2)
    beta = beta.reshape(B, NC, C, H).transpose(0, 3, 1, 2)
    gc = jnp.cumsum(g_log, axis=-1)
    causal = jnp.tril(jnp.ones((C, C), dtype=bool))
    strict = jnp.tril(jnp.ones((C, C), dtype=bool), -1)
    decay = jnp.exp(jnp.where(causal, gc[..., :, None] - gc[..., None, :], -jnp.inf))
    k_beta = k * beta[..., None]
    v_beta = v * beta[..., None]
    A = jnp.where(strict, jnp.einsum('bhncd,bhnsd->bhncs', k_beta, k) * decay, 0.0)
    L = A + jnp.eye(C, dtype=A.dtype)
    rhs = jnp.concatenate([v_beta, k_beta * jnp.exp(gc)[..., None]], axis=-1)
    sol = lax.linalg.triangular_solve(L, rhs, left_side=True, lower=True, unit_diagonal=True)
    u, w = sol[..., :dv], sol[..., dv:]
    qk = jnp.einsum('bhncd,bhnsd->bhncs', q, k) * decay

    def step(S, inp):
        q_c, k_c, u_c, w_c, qk_c, gc_c = inp
        v_new = u_c - jnp.einsum('bhcd,bhde->bhce', w_c, S)
        o = (jnp.einsum('bhcd,bhde->bhce', q_c * jnp.exp(gc_c)[..., None], S)
             + jnp.einsum('bhcs,bhse->bhce', qk_c, v_new))
        g_last = gc_c[..., -1]
        S = (S * jnp.exp(g_last)[..., None, None]
             + jnp.einsum('bhcd,bhce->bhde', k_c * jnp.exp(g_last[..., None] - gc_c)[..., None], v_new))
        return S, o

    xs = tuple(jnp.moveaxis(t, 2, 0) for t in (q, k, u, w, qk, gc))
    _, o = lax.scan(step, jnp.zeros((B, H, dk, dv), jnp.float32), xs)
    return o.transpose(1, 0, 3, 2, 4).reshape(B, T, H, dv)

def rwkv7_branch(p, mu, w0, w_decay_up, a0, w_iclr_up, w_gate_up, k_k, k_a, r_k, lnx_g, lnx_b, w_pa):
    f32 = jnp.float32
    B, T, _ = p.shape
    prev = jnp.pad(p, ((0, 0), (1, 0), (0, 0)))[:, :T]
    p = p + (prev - p) * mu
    r, k, v, wl, al, gl = _split(p, RWKV_SPLITS)
    w_log = -jax.nn.softplus(-(w0 + jnp.tanh(wl) @ w_decay_up).astype(f32)) - 0.5
    decay = jnp.exp(-jnp.exp(w_log))
    a = jax.nn.sigmoid((a0 + al @ w_iclr_up).astype(f32))
    g = jax.nn.sigmoid(gl) @ w_gate_up

    def hd(t):
        return t.astype(f32).reshape(*t.shape[:-1], RWKV_HEADS, RWKV_HEAD_DIM)

    r, k, v, decay, a = hd(r), hd(k), hd(v), hd(decay), hd(a)
    kk = l2_normalize(k * hd(k_k))
    k = k * (1.0 + (a - 1.0) * hd(k_a))
    o = rwkv7_recurrence(r, decay, k, v, -kk, kk * a)
    mean = jnp.mean(o, axis=-1, keepdims=True)
    var = jnp.mean(jnp.square(o - mean), axis=-1, keepdims=True)
    o = (o - mean) * lax.rsqrt(var + RWKV_GN_EPS) * hd(lnx_g) + hd(lnx_b)
    o = o + jnp.sum(r * k * hd(r_k), axis=-1, keepdims=True) * v
    o = o.reshape(B, T, RWKV_WIDTH).astype(p.dtype) * g
    return o @ w_pa

def gated_deltanet_branch(p, conv_w, a_log, dt_bias, gdn_norm_g, w_pb):
    f32 = jnp.float32
    B, T, _ = p.shape
    qkv, a_in, b_in, z = _split(p, GDN_SPLITS)
    qkv = jax.nn.silu(causal_depthwise_conv(qkv, conv_w))
    q, k, v = [t.astype(f32).reshape(B, T, GDN_HEADS, GDN_HEAD_DIM) for t in jnp.split(qkv, 3, axis=-1)]
    q, k = l2_normalize(q), l2_normalize(k)
    beta = jax.nn.sigmoid(b_in.astype(f32))
    g_log = -jnp.exp(a_log.astype(f32)) * jax.nn.softplus(a_in.astype(f32) + dt_bias.astype(f32))
    o = chunked_gated_delta_rule(q, k, v, g_log, beta)
    o = o * lax.rsqrt(jnp.mean(o * o, axis=-1, keepdims=True) + NORM_EPS) * gdn_norm_g.astype(f32)
    o = o.reshape(B, T, GDN_WIDTH).astype(p.dtype) * jax.nn.silu(z)
    return o @ w_pb

def hybrid_mixer(h, w_in, mu, w0, w_decay_up, a0, w_iclr_up, w_gate_up, k_k, k_a, r_k, lnx_g, lnx_b,
                 w_pa, conv_w, a_log, dt_bias, gdn_norm_g, w_pb, w_out):
    proj = h @ w_in
    p_rwkv, p_gdn, p_gate = _split(proj, (RWKV_COLS, GDN_COLS, GATE_COLS))
    y_a = rwkv7_branch(p_rwkv, mu, w0, w_decay_up, a0, w_iclr_up, w_gate_up, k_k, k_a, r_k,
                       lnx_g, lnx_b, w_pa)
    y_b = gated_deltanet_branch(p_gdn, conv_w, a_log, dt_bias, gdn_norm_g, w_pb)
    g_a, g_b = jnp.split(p_gate, 2, axis=-1)
    y = jax.nn.sigmoid(g_a) * y_a + jax.nn.sigmoid(g_b) * y_b
    return y @ w_out

def moe_swiglu(h, router, w_gate, w_up, w_down):
    logits = (h @ router).astype(jnp.float32)
    top_v, top_i = lax.top_k(logits, TOP_K)
    gates = jax.nn.softmax(top_v, axis=-1)
    combine = jnp.sum(jax.nn.one_hot(top_i, N_EXPERTS, dtype=jnp.float32) * gates[..., None], axis=-2)
    combine = combine.astype(h.dtype)
    out = jnp.zeros_like(h)
    for e in range(N_EXPERTS):
        out = out + combine[..., e:e + 1] * swiglu(h, w_gate[e], w_up[e], w_down[e])
    return out

def setup_inputs(seed: int = 0) -> dict:
    key = jax.random.key(seed)
    ks = jax.random.split(key, 32)
    f32 = jnp.float32
    L, D = DEPTH, D_MODEL

    def nrm(k, shape, scale):
        return jax.random.normal(k, shape, f32) * scale

    dt = jnp.exp(jax.random.uniform(ks[17], (L, GDN_HEADS), f32, np.log(1e-3), np.log(1e-1)))
    return {
        'x': nrm(ks[0], (BATCH, SEQ, D), 1.0),
        'norm1_g': 1.0 + nrm(ks[1], (L, D), 0.02),
        'w_in': nrm(ks[2], (L, D, IN_COLS), D ** -0.5),
        'tshift_mu': jax.random.uniform(ks[3], (L, RWKV_COLS), f32),
        'w0': jax.random.uniform(ks[4], (L, RWKV_WIDTH), f32, -6.0, 1.0),
        'w_decay_up': nrm(ks[5], (L, DECAY_LORA, RWKV_WIDTH), 0.5 * DECAY_LORA ** -0.5),
        'a0': nrm(ks[6], (L, RWKV_WIDTH), 0.5),
        'w_iclr_up': nrm(ks[7], (L, ICLR_LORA, RWKV_WIDTH), ICLR_LORA ** -0.5),
        'w_gate_up': nrm(ks[8], (L, GATE_LORA, RWKV_WIDTH), GATE_LORA ** -0.5),
        'k_k': 1.0 + nrm(ks[9], (L, RWKV_WIDTH), 0.1),
        'k_a': 1.0 + nrm(ks[10], (L, RWKV_WIDTH), 0.1),
        'r_k': nrm(ks[11], (L, RWKV_WIDTH), 0.1),
        'lnx_g': 1.0 + nrm(ks[12], (L, RWKV_WIDTH), 0.02),
        'lnx_b': nrm(ks[13], (L, RWKV_WIDTH), 0.01),
        'w_pa': nrm(ks[14], (L, RWKV_WIDTH, D), RWKV_WIDTH ** -0.5),
        'conv_w': nrm(ks[15], (L, CONV_WIDTH, 3 * GDN_WIDTH), CONV_WIDTH ** -0.5),
        'a_log': jnp.log(jax.random.uniform(ks[16], (L, GDN_HEADS), f32, 1.0, 16.0)),
        'dt_bias': dt + jnp.log(-jnp.expm1(-dt)),
        'gdn_norm_g': 1.0 + nrm(ks[18], (L, GDN_HEAD_DIM), 0.02),
        'w_pb': nrm(ks[19], (L, GDN_WIDTH, D), GDN_WIDTH ** -0.5),
        'w_out': nrm(ks[20], (L, D, D), D ** -0.5),
        'norm2_g': 1.0 + nrm(ks[21], (L, D), 0.02),
        'ffn_w_gate': nrm(ks[22], (N_DENSE, D, D_FF), D ** -0.5),
        'ffn_w_up': nrm(ks[23], (N_DENSE, D, D_FF), D ** -0.5),
        'ffn_w_down': nrm(ks[24], (N_DENSE, D_FF, D), D_FF ** -0.5),
        'moe_router': nrm(ks[25], (N_MOE, D, N_EXPERTS), D ** -0.5),
        'moe_w_gate': nrm(ks[26], (N_MOE, N_EXPERTS, D, D_FF), D ** -0.5),
        'moe_w_up': nrm(ks[27], (N_MOE, N_EXPERTS, D, D_FF), D ** -0.5),
        'moe_w_down': nrm(ks[28], (N_MOE, N_EXPERTS, D_FF, D), D_FF ** -0.5),
        'final_g': 1.0 + nrm(ks[29], (D,), 0.02),
    }

def reference(x, norm1_g, w_in, tshift_mu, w0, w_decay_up, a0, w_iclr_up, w_gate_up, k_k, k_a, r_k,
              lnx_g, lnx_b, w_pa, conv_w, a_log, dt_bias, gdn_norm_g, w_pb, w_out, norm2_g,
              ffn_w_gate, ffn_w_up, ffn_w_down, moe_router, moe_w_gate, moe_w_up, moe_w_down, final_g):
    for layer in range(DEPTH):
        h = rms_norm(x, norm1_g[layer])
        x = x + hybrid_mixer(h, w_in[layer], tshift_mu[layer], w0[layer], w_decay_up[layer], a0[layer],
                             w_iclr_up[layer], w_gate_up[layer], k_k[layer], k_a[layer], r_k[layer],
                             lnx_g[layer], lnx_b[layer], w_pa[layer], conv_w[layer], a_log[layer],
                             dt_bias[layer], gdn_norm_g[layer], w_pb[layer], w_out[layer])
        h = rms_norm(x, norm2_g[layer])
        j = layer // 2
        if layer % 2 == 0:
            x = x + swiglu(h, ffn_w_gate[j], ffn_w_up[j], ffn_w_down[j])
        else:
            x = x + moe_swiglu(h, moe_router[j], moe_w_gate[j], moe_w_up[j], moe_w_down[j])
    return rms_norm(x, final_g)


_drawn_inputs = setup_inputs


def setup_inputs(seed=0):
    import zlib

    import numpy as np

    out = dict(_drawn_inputs(seed))
    spreads = {}
    factors = {}
    for name, (base, spread) in spreads.items():
        noise = np.random.default_rng([zlib.crc32(name.encode()), seed]).standard_normal(out[name].shape)
        drawn = base * np.exp(spread * noise) if base else spread * noise
        out[name] = __import__('jax').numpy.asarray(drawn.astype(out[name].dtype))
    for name, factor in factors.items():
        out[name] = (out[name] * factor).astype(out[name].dtype)
    return out
```

```python
from contextlib import ExitStack

import concourse.bass as bass
from concourse import mybir

F32 = mybir.dt.float32
BF16 = mybir.dt.bfloat16
I32 = mybir.dt.int32
U32 = mybir.dt.uint32
ALU = mybir.AluOpType
ACT = mybir.ActivationFunctionType
AX_X = mybir.AxisListType.X

P = 128
D = 1024
T = 256
DEPTH = 2
KT = D // P
RW = 512
NT = RW // P
HD = 64
GH = 4
RWKV_COLS = 1792
GDN_BASE = RWKV_COLS
AB_BASE = GDN_BASE + 3 * RW
Z_BASE = AB_BASE + 2 * GH
GATE_BASE = Z_BASE + RW
F = 2816
NE = 8
NORM_EPS = 1e-6
GN_EPS = 64e-5
DECAY_C = 0.6065306597126334

SLAB = 2048
COLS = SLAB // KT
FC = F // COLS
MIX_RING = 3
FFN_RING = 11
IN_SLABS = ([1536] + [512, 768, 0, 256, 1024, 1280] + [GDN_BASE + COLS * i for i in range(6)]
            + [Z_BASE, Z_BASE + COLS] + [GATE_BASE + COLS * i for i in range(8)])
N_IN = len(IN_SLABS)
N_CONV = 13
N_MIX = N_IN + 8
N_FFN = 3 * FC

V_MU, V_W0, V_A0, V_KK, V_KA, V_RK, V_LG, V_LB, V_CONV, V_N1, V_N2, V_GN = (
    0, 14, 18, 22, 26, 30, 34, 38, 42, 90, 98, 106)
N_VEC = 107
VEC_BANK = (6, 0)

MIX0 = MIX_RING * SLAB


def ffn_order():
    order = [("g", 0), ("u", 0)]
    for j in range(1, FC):
        order += [("g", j), ("u", j), ("d", j - 1)]
    return order + [("d", FC - 1)]


FFN_ORDER = ffn_order()
AT = {key: n for n, key in enumerate(FFN_ORDER)}

R_STEPS = ["pair", "dT", "sq", "gen1", "gen2", "last1", "gT", "m", "gen3", "gen4", "last2",
           "z0", "u0", "s", "z1", "u1", "o"]
G_STEPS = [s for s in R_STEPS if s != "z0"]
R_AT = {s: n + 1 for n, s in enumerate(R_STEPS)}
G_AT = {s: n + 1 for n, s in enumerate(G_STEPS)}
R_COPIES = ["dT", "sq", "sqT", "gen1", "gen1T", "gen2", "gen2T", "gT", "m", "mT", "gen3", "gen3T", "gen4", "gen4T",
            "z0", "u0", "s", "z1", "u1"]
G_COPIES = [s for s in R_COPIES if s not in ("z0", "z1")]
RC_AT = {s: n + 1 for n, s in enumerate(R_COPIES)}
GC_AT = {s: n + 1 for n, s in enumerate(G_COPIES)}
R_SUMS = ["d", "masked", "gen1", "gen2", "last1", "gen3", "gen4", "last2", "o"]
G_SUMS = ["d", "masked", "gen1", "gen2", "last1", "gen3", "gen4", "last2", "z1", "o"]
RS_AT = {s: n + 1 for n, s in enumerate(R_SUMS)}
GS_AT = {s: n + 1 for n, s in enumerate(G_SUMS)}


class Chain:

    def __init__(self, eng, sem):
        self.eng, self.sem, self.n = eng, sem, 0

    def mark(self, ins):
        self.n += 1
        ins.then_inc(self.sem, 1)

    def __call__(self, ins):
        self.mark(ins)
        self.eng.wait_ge(self.sem, self.n)


def trunk(nc, x, norm1_g, w_in, tshift_mu, w0, w_decay_up, a0, w_iclr_up, w_gate_up, k_k, k_a, r_k, lnx_g, lnx_b,
          w_pa, conv_w, a_log, dt_bias, gdn_norm_g, w_pb, w_out, norm2_g, ffn_w_gate, ffn_w_up, ffn_w_down,
          moe_router, moe_w_gate, moe_w_up, moe_w_down, final_g, out, dbg=None):
    with ExitStack() as ctx:
        def sb(name, shape, dt=F32):
            return ctx.enter_context(nc.sbuf_tensor(name, shape, dt))

        def sem(name):
            return ctx.enter_context(nc.semaphore(name))

        ps = ctx.enter_context(nc.psum_tensor("ps", [P, 8, 512], F32))

        xT = sb("xT", [P, KT, T])
        hT = sb("hT", [P, KT, T])
        ident = sb("ident", [P, P])
        ones = sb("ones", [P, P])
        head_ones = sb("head_ones", [P, P])
        later = sb("later", [P, 2, P])
        later_neg = sb("later_neg", [P, 2, P])
        blocks16 = sb("blocks16", [P, P])
        sel = sb("sel", [GH, GH, P])
        restart = sb("restart", [P, 8 * 129], BF16)
        slots = sb("slots", [P, P])
        vec_rows = sb("vec_rows", [P, P])
        vec = sb("vec", [P, DEPTH, N_VEC])
        one_less_mu = sb("one_less_mu", [P, DEPTH, 14])
        head_raw = sb("head_raw", [GH, 2, DEPTH])
        minus_a = sb("minus_a", [GH, DEPTH])
        lora_up = sb("lora_up", [P, RW])
        gate_up = sb("gate_up", [P, RW])
        w_ab = sb("w_ab", [P, KT, 2 * GH])
        eps_b = sb("eps_b", [P, 4])
        arena = sb("arena", [P, 44800])

        at = [MIX0]

        def take(n):
            at[0] += n
            return at[0] - n

        def view(off, n, rows=P):
            return arena[0:rows, off:off + n]

        o_R, o_K = take(1024), take(1024)
        o_V = take(1024)
        o_LO, o_LC, o_EP, o_EM, o_A = take(512), take(1032), take(1032), take(1032), take(1024)
        o_KK, o_AR, o_BH, o_KH, o_SQ, o_G = take(1024), take(2048), take(1024), take(1024), take(1024), take(1024)
        o_TV, o_TB, o_TK, o_QKV, o_KBQ = take(1024), take(512), take(512), take(3072), take(2048)
        o_Z, o_TVB, o_TKN, o_GB, o_GATES = take(1024), take(1024), take(512), take(512), take(4096)
        R3 = view(o_R, 1024).rearrange("p (t n) -> p t n", t=NT)
        K3_flat = view(o_K, 1024)
        K3 = view(o_K, 1024).rearrange("p (t n) -> p t n", t=NT)
        V3 = view(o_V, 1024).rearrange("p (t n) -> p t n", t=NT)
        LO = view(o_LO, 512)
        LC = view(o_LC, 1032).rearrange("p (q n) -> p q n", q=8)
        EP = view(o_EP, 1032).rearrange("p (q n) -> p q n", q=8)
        EM = view(o_EM, 1032).rearrange("p (q n) -> p q n", q=8)
        A3 = view(o_A, 1024).rearrange("p (t n) -> p t n", t=NT)
        KK = view(o_KK, 1024)
        AR = view(o_AR, 2048).rearrange("p (q s n) -> p q s n", q=8, s=2)
        BH = view(o_BH, 1024).rearrange("p (q n) -> p q n", q=8)
        KH = view(o_KH, 1024).rearrange("p (q n) -> p q n", q=8)
        SQ = view(o_SQ, 1024)
        G = view(o_G, 1024)
        TV = view(o_TV, 1024).rearrange("p (c n) -> p c n", c=2)
        TB = view(o_TB, 512)
        TK = view(o_TK, 512)
        QKV = view(o_QKV, 3072)
        Q1, K1, V1 = view(o_QKV, 1024), view(o_QKV + 1024, 1024), view(o_QKV + 2048, 1024)
        KBQ = view(o_KBQ, 2048).rearrange("p (q s n) -> p q s n", q=8, s=2)
        Z = view(o_Z, 1024)
        TVB = view(o_TVB, 1024).rearrange("p (c n) -> p c n", c=2)
        TKN = view(o_TKN, 512)
        GB = view(o_GB, 512, GH)
        GATES = view(o_GATES, 4096)
        KG = view(o_QKV, 512)
        QG = view(o_QKV + 512, 512)
        OG = V1
        BG = view(o_LC, 1024).rearrange("p (h n) -> p h n", h=GH)
        EG = view(o_A, 1024).rearrange("p (h n) -> p h n", h=GH)
        BB = view(o_EM, 1024).rearrange("p (h n) -> p h n", h=GH)
        DD = view(o_EP, 1024).rearrange("p (q n) -> p q n", q=8)
        DM = view(o_K, 2048).rearrange("p (q s n) -> p q s n", q=8, s=2)
        x_tok_in = view(o_QKV, 2048).rearrange("p (a n) -> p a n", a=2)
        YT = view(o_KBQ, 2048)
        XSQ = view(o_KBQ, 2048)
        RSTD = view(o_TVB, 256)
        small = sb("small", [P, 64])
        mid = small[:, 0:8]
        scol = small[:, 8:12]
        gcol = small[:, 12:20].rearrange("p (c h) -> p c h", c=2)
        kdec = small[:, 20:24]

        MQ, MK, DG, DT, ZB, UB, SB = [], [], [], [], [], [], []
        for s in range(2):
            o = take(1024)
            MQ.append(view(o, 1024).rearrange("p (q n) -> p q n", q=4))
            o = take(1024)
            MK.append(view(o, 1024).rearrange("p (q n) -> p q n", q=4))
            o = take(1024)
            DG.append(view(o, 1024).rearrange("p (q n) -> p q n", q=4))
            o = take(512)
            DT.append(view(o, 512).rearrange("p (q n) -> p q n", q=4))
            o = take(256)
            ZB.append(view(o, 256).rearrange("p (q n) -> p q n", q=2))
            o = take(512)
            UB.append(view(o, 512).rearrange("p (q n) -> p q n", q=4))
            o = take(256)
            SB.append(view(o, 256).rearrange("p (q n) -> p q n", q=2))
        assert at[0] <= 44800, at[0]
        o = at[0] - 4608
        g4 = view(o, 1280, GH).rearrange("p (i n) -> p i n", i=5)
        KSQ = MQ[0]
        QSQ = view(o_TVB, 1024)

        at[0] = FFN_RING * SLAB
        o = take(2 * 512)
        FG = view(o, 1024).rearrange("p (b n) -> p b n", b=2)
        o = take(2 * 512)
        FH = view(o, 1024).rearrange("p (b n) -> p b n", b=2)
        o = take(2048)
        h_tok = view(o, 2048).rearrange("p (a n) -> p a n", a=2)
        o = take(2048)
        x_tok = view(o, 2048).rearrange("p (a n) -> p a n", a=2)
        o = take(1024)
        XS = view(o, 1024).rearrange("p (k n) -> p k n", k=KT)
        o = take(256)
        PT = view(o, 256).rearrange("p (a n) -> p a n", a=2)
        o = take(256)
        PTC = view(o, 256).rearrange("p (a n) -> p a n", a=2)
        o = take(256)
        PC = view(o, 256)
        o = take(1024)
        YE = view(o, 1024)
        o = take(64)
        w_router = view(o, 64).rearrange("p (k n) -> p k n", k=KT)
        o = take(256)
        rt = view(o, 256)
        logits = rt[:, 0:16].rearrange("p (a n) -> p a n", a=2)
        top = rt[:, 16:32].rearrange("p (a n) -> p a n", a=2)
        topi_f = rt[:, 32:48].rearrange("p (a n) -> p a n", a=2)
        hot1 = rt[:, 48:64].rearrange("p (a n) -> p a n", a=2)
        hot2 = rt[:, 64:80].rearrange("p (a n) -> p a n", a=2)
        chosen = rt[:, 80:96].rearrange("p (a n) -> p a n", a=2)
        combine = rt[:, 96:112].rearrange("p (a n) -> p a n", a=2)
        pos = rt[:, 112:128].rearrange("p (a n) -> p a n", a=2)
        g_diff, g_exp = rt[:, 128:130], rt[:, 130:132]
        g_first, g_second = rt[:, 132:134], rt[:, 134:136]
        most = rt[:, 136:137]
        xsum = rt[:, 138:140]
        topi = sb("topi", [P, 2, 8], U32)
        over = sb("over", [P, 1], I32)
        o = take(2048)
        x_sq = view(o, 2048).rearrange("p (a n) -> p a n", a=2)
        o = take(1024)
        fin_g = view(o, 1024)
        x_tok_out = h_tok
        assert at[0] <= 44800, at[0]

        slab_in = [sem(f"slab_in{i}") for i in range(FFN_RING)]
        slab_done = sem("slab_done")
        consts_made = sem("consts_made")
        x_in = sem("x_in")
        rows_in = [sem(f"rows_in{L}") for L in range(DEPTH)]
        small_in = [sem(f"small_in{L}") for L in range(DEPTH)]
        head_in = sem("head_in")
        router_in = sem("router_in")
        fin_in = sem("fin_in")
        vec_turned, vec_kept = sem("vec_turned"), sem("vec_kept")
        x_turned, x_kept = sem("x_turned"), sem("x_kept")
        squared, summed, rooted, normed = sem("squared"), sem("summed"), sem("rooted"), sem("normed")
        proj_act, proj_dve = sem("proj_act"), sem("proj_dve")
        lora_acted, lora_done = sem("lora_acted"), sem("lora_done")
        decay_sig, rate_sig, gate_kept = sem("decay_sig"), sem("rate_sig"), sem("gate_kept")
        kk_made, kk_squared, kk_summed, kk_rooted = sem("kk_made"), sem("kk_squared"), sem("kk_summed"), sem("kk_rooted")
        log_decay, decays = sem("log_decay"), sem("decays")
        rw_ready, rk_ready, rk_summed, bonus_made = sem("rw_ready"), sem("rk_ready"), sem("rk_summed"), sem("bonus_made")
        silu_done, qk_squared, qk_summed = sem("silu_done"), sem("qk_squared"), sem("qk_summed")
        qk_rooted, qk_normed = sem("qk_rooted"), sem("qk_normed")
        ab_done, ab_dve, ab_act = sem("ab_done"), sem("ab_dve"), sem("ab_act")
        spread, spread_kept, cols_turned, cols_kept = sem("spread"), sem("spread_kept"), sem("cols_turned"), sem("cols_kept")
        kdec_arg, kdec_made, dd_made, dd_exp = sem("kdec_arg"), sem("kdec_made"), sem("dd_made"), sem("dd_exp")
        vb_made, gdn_ready = sem("vb_made"), sem("gdn_ready")
        rw_turned, rw_kept = sem("rw_turned"), sem("rw_kept")
        gdn_turned, gdn_kept, gdn_keyed = sem("gdn_turned"), sem("gdn_kept"), sem("gdn_keyed")
        mat_done = [sem(f"mat_done{s}") for s in range(2)]
        mat_copied = [sem(f"mat_copied{s}") for s in range(2)]
        mat_summed = [sem(f"mat_summed{s}") for s in range(2)]
        hn_summed, hn_act, hn_dve = sem("hn_summed"), sem("hn_act"), sem("hn_dve")
        merged, mixed = sem("merged"), sem("mixed")
        ffn_act, ffn_dve, ffn_added = sem("ffn_act"), sem("ffn_dve"), sem("ffn_added")
        tok_turned, tok_kept = sem("tok_turned"), sem("tok_kept")
        routed, logits_done, diff_made, exp_made, pos_done, over_made = (
            sem("routed"), sem("logits_done"), sem("diff_made"), sem("exp_made"), sem("pos_done"), sem("over_made"))
        hot_made, gathered, gather_kept = sem("hot_made"), sem("gathered"), sem("gather_kept")
        hot_turned, hot_kept = sem("hot_turned"), sem("hot_kept")
        e_act, e_dve, e_out, e_kept = sem("e_act"), sem("e_dve"), sem("e_out"), sem("e_kept")
        scattered, added = sem("scattered"), sem("added")
        pos_moved = sem("pos_moved")
        moe_added, fin_sq, fin_root, fin_made, stored = (
            sem("moe_added"), sem("fin_sq"), sem("fin_root"), sem("fin_made"), sem("stored"))
        act_steps, dve_steps, pool_steps = sem("act_steps"), sem("dve_steps"), sem("pool_steps")

        first = {("mix", 0): 0, ("ffn", 0): N_MIX, ("mix", 1): N_MIX + N_FFN, ("moe", 1): 2 * N_MIX + N_FFN}
        place, landed, before = {}, {}, {}
        uses, last_user = [0] * FFN_RING, [None] * FFN_RING
        for phase, n, ring in ((("mix", 0), N_MIX, MIX_RING), (("ffn", 0), N_FFN, FFN_RING),
                               (("mix", 1), N_MIX, MIX_RING), (("moe", 1), N_FFN, FFN_RING)):
            for i in range(n):
                slot, s = i % ring, first[phase] + i
                uses[slot] += 1
                place[s], landed[s], before[s] = slot, 16 * uses[slot], last_user[slot]
                last_user[slot] = s
        E_LAPS = N_FFN // FFN_RING

        def slab(slot):
            return arena[:, slot * SLAB:(slot + 1) * SLAB]

        def by_k(ap, n):
            return ap.rearrange("(k p) n -> p k n", p=P)

        def mix_source(L, i):
            if i < N_IN:
                return by_k(w_in[L, :, IN_SLABS[i]:IN_SLABS[i] + COLS], COLS), KT
            i -= N_IN
            if i < 4:
                w = (w_pb, w_pb, w_pa, w_pa)[i]
                return by_k(w[L, :, 512 * (i % 2):512 * (i % 2) + 512], 512), NT
            i -= 4
            return by_k(w_out[L, :, COLS * i:COLS * i + COLS], COLS), KT

        def ffn_source(wg, wu, wd, kind, j):
            if kind == "d":
                return by_k(wd[COLS * j:COLS * (j + 1), :], D), 2
            return by_k((wg if kind == "g" else wu)[:, COLS * j:COLS * (j + 1)], COLS), KT

        block = ctx.enter_context(nc.Block())

        @block.sync
        def _(sp):
            xv = x.rearrange("b (a p) d -> p (b a) d", p=P)
            sp.dma_start(x_tok_in, xv).then_inc(x_in, 16)

            def static(s, src, k):
                if before[s] is not None:
                    sp.wait_ge(slab_done, before[s] + 1)
                dst = slab(place[s]).rearrange("p (k n) -> p k n", k=k)
                sp.dma_start(dst, src).then_inc(slab_in[place[s]], 16)

            for L in range(DEPTH):
                for i in range(N_MIX):
                    static(first["mix", L] + i, *mix_source(L, i))
                if L == 0:
                    for i, (kind, j) in enumerate(FFN_ORDER):
                        if i == MIX_RING:
                            sp.wait_ge(mixed, 4 * (L + 1))
                        static(first["ffn", 0] + i, *ffn_source(ffn_w_gate[0], ffn_w_up[0], ffn_w_down[0], kind, j))

            def experts(lap):
                s0 = first["moe", 1]
                with sp.Fori(0, NE) as e:
                    for i, (kind, j) in enumerate(FFN_ORDER):
                        slot = i % FFN_RING
                        sp.wait_ge(slab_done, e * N_FFN + (s0 + lap * NE * N_FFN + i - FFN_RING + 1))
                        src, k = ffn_source(moe_w_gate[0, e], moe_w_up[0, e], moe_w_down[0, e], kind, j)
                        sp.dma_start(slab(slot).rearrange("p (k n) -> p k n", k=k), src).then_inc(slab_in[slot], 16)

            sp.wait_ge(mixed, 8)
            experts(0)
            sp.wait_ge(over_made, 1)
            more = sp.value_load(over[0:1, 0:1])
            with sp.If(more > 0):
                experts(1)

            sp.wait_ge(fin_made, 2)
            ov = out.rearrange("b (a p) d -> p (b a) d", p=P)
            sp.dma_start(ov, x_tok_out).then_inc(stored, 16)
            sp.wait_ge(stored, 16)

        @block.gpsimd
        def _(pool):
            step = Chain(pool, pool_steps)
            for t in (ident, ones, head_ones, later, later_neg, blocks16, sel, eps_b):
                step(nc.gpsimd.memset(t[:], 0.0 if t in (head_ones,) else 1.0))
            step(nc.gpsimd.memset(restart[:], 1.0))
            step(nc.gpsimd.iota(slots[:], pattern=[[1, P]], base=0, channel_multiplier=0,
                                allow_small_or_imprecise_dtypes=True))
            keep = nc.gpsimd.affine_select
            step(keep(out=ident[:], in_=ident[:], pattern=[[-1, P]], compare_op=ALU.is_equal, fill=0.0,
                           base=0, channel_multiplier=1))
            for tab, value in ((later, 1.0), (later_neg, -1.0)):
                step(nc.gpsimd.memset(tab[:, 0, :], value))
                step(keep(out=tab[:, 0, :], in_=tab[:, 0, :], pattern=[[1, P]], compare_op=ALU.is_gt, fill=0.0,
                               base=0, channel_multiplier=-1))
                step(keep(out=tab[:, 1, :], in_=tab[:, 1, :], pattern=[[1, P]], compare_op=ALU.is_ge, fill=0.0,
                               base=0, channel_multiplier=-1))
            b16 = blocks16[:].rearrange("p (b n) -> p b n", n=16)
            step(keep(out=b16, in_=b16, pattern=[[-16, 8], [0, 16]], compare_op=ALU.is_ge, fill=0.0,
                      base=0, channel_multiplier=1))
            step(keep(out=b16, in_=b16, pattern=[[16, 8], [0, 16]], compare_op=ALU.is_ge, fill=0.0,
                           base=15, channel_multiplier=-1))
            step(keep(out=sel[:], in_=sel[:], pattern=[[-1, GH], [0, P]], compare_op=ALU.is_equal, fill=0.0,
                           base=0, channel_multiplier=1))
            r3 = restart[:].rearrange("p (q n) -> p q n", q=8)
            step(nc.gpsimd.memset(r3[:, :, 0:1], 0.0))
            for hh in range(2):
                step(nc.gpsimd.memset(head_ones[64 * hh:64 * hh + 64, 64 * hh:64 * hh + 64], 1.0))
            for i, value in enumerate((NORM_EPS, P * 1e-6, GN_EPS, 1.0)):
                step(nc.gpsimd.memset(eps_b[:, i:i + 1], value))
            nc.gpsimd.memset(small[:], 0.0).then_inc(consts_made, 1)

            for L in range(DEPTH):
                if L:
                    pool.wait_ge(vec_turned, L)
                rows = [(V_MU, tshift_mu[L], 14), (V_W0, w0[L], 4), (V_A0, a0[L], 4), (V_KK, k_k[L], 4),
                        (V_KA, k_a[L], 4), (V_RK, r_k[L], 4), (V_LG, lnx_g[L], 4), (V_LB, lnx_b[L], 4),
                        (V_N1, norm1_g[L], 8), (V_N2, norm2_g[L], 8), (V_GN, gdn_norm_g[L], 1)]
                for r, src, n in rows:
                    pool.dma_start(vec_rows[r:r + n, :], src.rearrange("(t p) -> t p", p=P)).then_inc(rows_in[L], 16)
                pool.dma_start(vec_rows[V_CONV:V_CONV + 48, :],
                               conv_w[L].rearrange("j (t p) -> (j t) p", p=P)).then_inc(rows_in[L], 16)
                if L == 0:
                    for i, src in enumerate((a_log, dt_bias)):
                        for l in range(DEPTH):
                            pool.dma_start(head_raw[:, i, l:l + 1],
                                           src[l].rearrange("(h a) -> h a", a=1)).then_inc(head_in, 16)
                else:
                    pool.wait_ge(lora_done, 3 * L)
                    pool.wait_ge(ab_done, L)
                pool.dma_start(lora_up[0:64, :], w_decay_up[L]).then_inc(small_in[L], 16)
                pool.dma_start(lora_up[64:128, :], w_iclr_up[L]).then_inc(small_in[L], 16)
                pool.dma_start(gate_up[:], w_gate_up[L]).then_inc(small_in[L], 16)
                pool.dma_start(w_ab[:], by_k(w_in[L, :, AB_BASE:AB_BASE + 2 * GH], 2 * GH)).then_inc(small_in[L], 16)
            pool.wait_ge(mixed, 8)
            pool.dma_start(w_router, by_k(moe_router[0], NE)).then_inc(router_in, 16)
            pool.dma_start(fin_g, final_g.rearrange("(a n) -> a n", a=1).broadcast_to([P, D])).then_inc(fin_in, 16)

        @block.tensor
        def _(pe):
            def mm(out, lhsT, rhs, start=True, stop=True, **kw):
                return nc.tensor.matmul(out, lhsT, rhs, start=start, stop=stop, **kw)

            def turn(out, src):
                n = src.shape[0]
                return nc.tensor.transpose(out, src, ident[0:n, 0:n])

            def arrived(s):
                pe.wait_ge(slab_in[place[s]], landed[s])
                return slab(place[s])

            def norm(n):
                pe.wait_ge(squared, n + 1)
                for k in range(KT):
                    last = mm(ps[:, 7, 0:T], ones[:], XSQ[:, k * T:(k + 1) * T], k == 0, k == KT - 1)
                last.then_inc(summed, 1)
                pe.wait_ge(normed, n + 1)

            def in_slab(L, o):
                if o >= 4:
                    if o - 4 < N_CONV:
                        pe.wait_ge(proj_dve, N_CONV * L + o - 3)
                    else:
                        pe.wait_ge(proj_act, N_IN * L + o - 3)
                w = arrived(first["mix", L] + o).rearrange("p (k n) -> p k n", k=KT)
                for m in range(2):
                    for k in range(KT):
                        last = mm(ps[:, o % 4, m * T:(m + 1) * T], w[:, k, m * P:(m + 1) * P], hT[:, k, :],
                                  k == 0, k == KT - 1)
                last.then_inc(slab_done, 1)

            def head_sums(table, src, bank):
                for i in range(2):
                    last = mm(ps[:, bank + i, :], table[:], src[:, i * 512:(i + 1) * 512])
                return last

            def project(L):
                norm(2 * L)
                pe.wait_ge(small_in[L], 64)
                for o in range(9):
                    in_slab(L, o)
                pe.wait_ge(lora_acted, 2 * (L + 1))
                for lo, bank in ((0, 4), (64, 6)):
                    for t in range(NT):
                        last = mm(ps[:, bank + t // 2, (t % 2) * T:(t % 2 + 1) * T],
                                  lora_up[lo:lo + 64, t * P:(t + 1) * P], LO[lo:lo + 64, 0:T])
                    last.then_inc(lora_done, 1)
                in_slab(L, 9)
                in_slab(L, 10)
                pe.wait_ge(kk_squared, L + 1)
                pe.wait_ge(decay_sig, L + 1)
                head_sums(head_ones, SQ, 4).then_inc(kk_summed, 1)
                in_slab(L, 11)
                in_slab(L, 12)
                pe.wait_ge(rate_sig, L + 1)
                for t in range(NT):
                    last = mm(ps[:, 6 + t // 2, (t % 2) * T:(t % 2 + 1) * T],
                              gate_up[:, t * P:(t + 1) * P], LO[:, T:2 * T])
                last.then_inc(lora_done, 1)
                pe.wait_ge(kk_rooted, L + 1)
                for i in range(2):
                    for k in range(KT):
                        last = mm(ps[0:GH, 4, i * T:(i + 1) * T], w_ab[:, k, i * GH:(i + 1) * GH], hT[:, k, :],
                                  k == 0, k == KT - 1)
                last.then_inc(ab_done, 1)
                for o in range(13, 17):
                    in_slab(L, o)
                pe.wait_ge(rk_ready, L + 1)
                pe.wait_ge(gate_kept, L + 1)
                head_sums(head_ones, SQ, 6).then_inc(rk_summed, 1)
                in_slab(L, 17)
                pe.wait_ge(qk_squared, 2 * L + 1)
                pe.wait_ge(ab_act, 3 * L + 3)
                pe.wait_ge(ab_dve, 3 * L + 1)
                head_sums(ones, QSQ, 4).then_inc(qk_summed, 1)
                in_slab(L, 18)
                pe.wait_ge(qk_squared, 2 * L + 2)
                pe.wait_ge(bonus_made, L + 1)
                for i in range(2):
                    last = mm(ps[:, 6 + i, :], ones[:], KSQ[:, 2 * i:2 * i + 2, :])
                last.then_inc(qk_summed, 1)
                in_slab(L, 19)
                in_slab(L, 20)
                pe.wait_ge(qk_rooted, 2 * L + 2)
                pe.wait_ge(ab_dve, 3 * L + 3)
                for h in range(GH):
                    last = mm(ps[:, 4 + h, :], sel[:, h, :], GB)
                last.then_inc(spread, 1)
                in_slab(L, 21)
                in_slab(L, 22)
                pe.wait_ge(spread_kept, L + 1)
                for c in range(2):
                    last = mm(ps[:, 4, c * GH:(c + 1) * GH], GB[:, c * P:(c + 1) * P], ident[0:GH, 0:GH])
                last.then_inc(cols_turned, 1)

            def turn_tokens(L):
                pe.wait_ge(proj_act, N_IN * (L + 1))
                pe.wait_ge(rw_ready, L + 1)
                for c in range(2):
                    for t in range(NT):
                        turn(ps[:, c, t * P:(t + 1) * P], V3[:, t, c * P:(c + 1) * P])
                for bank, src in ((2, BH), (3, KH)):
                    for t in range(NT):
                        last = turn(ps[:, bank, t * P:(t + 1) * P], src[:, 2 * t, :])
                last.then_inc(rw_turned, 1)
                pe.wait_ge(vb_made, L + 1)
                for c in range(2):
                    for h in range(GH):
                        turn(ps[:, 5 + c, h * P:(h + 1) * P], V1[:, h * T + c * P:h * T + (c + 1) * P])
                for h in range(GH):
                    last = turn(ps[:, 7, h * P:(h + 1) * P], K1[:, h * T:h * T + P])
                last.then_inc(gdn_turned, 1)
                pe.wait_ge(rw_kept, L + 1)
                pe.wait_ge(gdn_kept, L + 1)
                pe.wait_ge(gdn_keyed, L + 1)
                pe.wait_ge(cols_kept, L + 1)
                pe.wait_ge(gdn_ready, L + 1)

            def groups(L):
                for pair in range(3):
                    rw = pair < 2
                    base = L * (2 * len(R_STEPS) + len(G_STEPS)) + pair * len(R_STEPS)
                    cbase = L * (2 * len(R_COPIES) + len(G_COPIES)) + pair * len(R_COPIES)
                    sbase = L * (2 * len(R_SUMS) + len(G_SUMS)) + pair * len(R_SUMS)
                    copies, sums = (RC_AT, RS_AT) if rw else (GC_AT, GS_AT)

                    def copied(s, what):
                        pe.wait_ge(mat_copied[s], cbase + copies[what])

                    def summed_(s, what):
                        pe.wait_ge(mat_summed[s], sbase + sums[what])

                    def products(s, bank, lhs, rhs):
                        for q in range(4):
                            last = mm(ps[:, 4 * s + bank, q * P:(q + 1) * P], lhs(q), rhs(q))
                        return last

                    def doubling(s, left, add):
                        A = lambda q: DG[s][:, q, 0:P]
                        At = lambda q: DT[s][:, q, :]
                        Gm = lambda q: DG[s][:, q, P:2 * P]
                        if left:
                            products(s, 1, At, A)
                            last = products(s, 2, A, At)
                        if add:
                            last = products(s, 3, At, Gm)
                        last.then_inc(mat_done[s], 1)

                    for s in range(2):
                        g = 2 * pair + s
                        if pair:
                            pbase = sbase - (len(R_SUMS))
                            pe.wait_ge(mat_summed[s], pbase + RS_AT["o"])
                        for q in range(4):
                            hh, c = q // 2, q % 2
                            dst = ps[:, 4 * s + q // 2, (q % 2) * T:(q % 2 + 1) * T]
                            if rw:
                                r = slice(64 * hh, 64 * hh + 64)
                                last = mm(dst, BH[r, 2 * g + c, :], AR[r, 2 * g + c, :, :])
                                last = mm(ps[:, 4 * s + 2 + q // 2, (q % 2) * T:(q % 2 + 1) * T],
                                          KH[r, 2 * g + c, :], AR[r, 2 * g + c, :, :])
                            else:
                                h = 2 * (g - 4) + hh
                                last = mm(dst, K1[:, h * T + c * P:h * T + (c + 1) * P], KBQ[:, 2 * h + c, :, :])
                        last.then_inc(mat_done[s], 1)
                    for s in range(2):
                        summed_(s, "d")
                        for q in range(4):
                            last = turn(ps[:, 4 * s, q * P:(q + 1) * P], DG[s][:, q, 0:P])
                        last.then_inc(mat_done[s], 1)
                    for s in range(2):
                        copied(s, "dT")
                        summed_(s, "masked")
                        doubling(s, True, False)
                    for s in range(2):
                        copied(s, "sqT")
                        doubling(s, True, True)
                    for s in range(2):
                        copied(s, "gen1T")
                        summed_(s, "gen1")
                        doubling(s, True, True)
                    for s in range(2):
                        copied(s, "gen2T")
                        summed_(s, "gen2")
                        doubling(s, False, True)
                    for s in range(2):
                        summed_(s, "last1")
                        for q in range(4):
                            last = turn(ps[:, 4 * s, q * P:(q + 1) * P], DG[s][:, q, P:2 * P])
                        last.then_inc(mat_done[s], 1)
                    for s in range(2):
                        copied(s, "gT")
                        products(s, 1, lambda q: DT[s][:, q, :], lambda q: MQ[s][:, q, 0:P])
                        products(s, 2, lambda q: MQ[s][:, q, 0:P], lambda q: DT[s][:, q, :]).then_inc(mat_done[s], 1)
                    for s in range(2):
                        copied(s, "mT")
                        doubling(s, True, True)
                    for s in range(2):
                        copied(s, "gen3T")
                        summed_(s, "gen3")
                        doubling(s, True, True)
                    for s in range(2):
                        copied(s, "gen4T")
                        summed_(s, "gen4")
                        doubling(s, False, True)

                    def heads(s):
                        g = 2 * pair + s
                        for hh in range(2):
                            if rw:
                                yield hh, slice(g * P + HD * hh, g * P + HD * (hh + 1)), slice(HD * hh, HD * (hh + 1)), HD
                            else:
                                h = 2 * (g - 4) + hh
                                yield hh, slice(h * P, (h + 1) * P), slice(0, P), P

                    def solve(s, c, rhs, what):
                        for hh, cols, rows, n in heads(s):
                            last = mm(ps[:, 4 * s + 1, hh * P:hh * P + n], DG[s][:, 2 * hh + c, P:2 * P], rhs(hh, cols, n))
                        last.then_inc(mat_done[s], 1)

                    if rw:
                        for s in range(2):
                            for hh, cols, rows, n in heads(s):
                                last = mm(ps[:, 4 * s + 2 * hh, 0:n], MK[s][:, 2 * hh, 0:P], TV[:, 0, cols])
                            last.then_inc(mat_done[s], 1)
                    for s in range(2):
                        summed_(s, "last2")
                        if rw:
                            copied(s, "z0")
                            solve(s, 0, lambda hh, cols, n: ZB[s][:, hh, 0:n], "u0")
                        else:
                            solve(s, 0, lambda hh, cols, n: TVB[:, 0, cols], "u0")
                    for s in range(2):
                        copied(s, "u0")
                        for hh, cols, rows, n in heads(s):
                            if rw:
                                dst = ps[rows, 4 * s + 2, 0:n]
                                mm(dst, TB[:, cols], UB[s][:, 2 * hh, 0:n], True, False)
                                last = mm(dst, TK[:, cols], TV[:, 0, cols], False, True)
                            else:
                                last = mm(ps[:, 4 * s + 2, hh * P:(hh + 1) * P], TKN[:, cols], UB[s][:, 2 * hh, :])
                        last.then_inc(mat_done[s], 1)
                    for s in range(2):
                        g = 2 * pair + s
                        copied(s, "s")
                        for hh, cols, rows, n in heads(s):
                            dst = ps[:, 4 * s + 2 * hh, 0:n] if rw else ps[:, 4 * s, hh * P:hh * P + n]
                            if rw:
                                mm(dst, AR[rows, 2 * g + 1, 0, :], SB[s][rows, 0, 0:n], True, False)
                                last = mm(dst, MK[s][:, 2 * hh + 1, 0:P], TV[:, 1, cols], False, True)
                            else:
                                last = mm(dst, KG[:, cols], SB[s][:, hh, :])
                        last.then_inc(mat_done[s], 1)
                    for s in range(2):
                        if rw:
                            copied(s, "z1")
                        else:
                            summed_(s, "z1")
                        solve(s, 1, lambda hh, cols, n: ZB[s][:, hh, 0:n], "u1")
                    for s in range(2):
                        g = 2 * pair + s
                        copied(s, "u1")
                        for hh, cols, rows, n in heads(s):
                            for c in range(2):
                                q = 2 * hh + c
                                dst = ps[rows, 4 * s + 3, c * P:(c + 1) * P] if rw else \
                                    ps[:, 4 * s + 3, q * P:(q + 1) * P]
                                mm(dst, UB[s][:, q, 0:n], MQ[s][:, q, P:2 * P], True, not rw and c == 0)
                                if rw:
                                    mm(dst, TV[:, c, cols], MK[s][:, q, P:2 * P], False, c == 0)
                                if c == 1:
                                    if rw:
                                        last = mm(dst, SB[s][rows, 0, 0:n], AR[rows, 2 * g + 1, 1, :], False, True)
                                    else:
                                        last = mm(dst, SB[s][:, hh, :], QG[:, cols], False, True)
                        last.then_inc(mat_done[s], 1)

            def finish_mixer(L):
                ends = [(L + 1) * (2 * len(R_SUMS) + len(G_SUMS))] * 2
                for s in range(2):
                    pe.wait_ge(mat_summed[s], ends[s])
                head_sums(head_ones, KK, 0).then_inc(hn_summed, 1)
                pe.wait_ge(hn_act, 4 * L + 1)
                head_sums(ones, QSQ, 4).then_inc(hn_summed, 1)
                pe.wait_ge(hn_act, 4 * L + 3)
                head_sums(head_ones, SQ, 2).then_inc(hn_summed, 1)
                pe.wait_ge(hn_dve, 3 * L + 2)
                for i, src, bank in ((0, OG, 4), (1, OG, 6), (2, KK, 0), (3, KK, 2)):
                    w = arrived(first["mix", L] + N_IN + i).rearrange("p (k n) -> p k n", k=NT)
                    if i == 2:
                        pe.wait_ge(hn_dve, 3 * L + 3)
                    for m in range(4):
                        for k in range(NT):
                            last = mm(ps[:, bank + m // 2, (m % 2) * T:(m % 2 + 1) * T], w[:, k, m * P:(m + 1) * P],
                                      src[:, k * T:(k + 1) * T], k == 0, k == NT - 1)
                    last.then_inc(slab_done, 1)
                pe.wait_ge(merged, L + 1)
                for j in range(4):
                    w = arrived(first["mix", L] + N_IN + 4 + j).rearrange("p (k n) -> p k n", k=KT)
                    for m in range(2):
                        for k in range(KT):
                            last = mm(ps[:, j, m * T:(m + 1) * T], w[:, k, m * P:(m + 1) * P],
                                      YT[:, k * T:(k + 1) * T], k == 0, k == KT - 1)
                    last.then_inc(slab_done, 1)

            def dense(L):
                norm(2 * L + 1)
                s0 = first["ffn", L]
                for i, (kind, j) in enumerate(FFN_ORDER):
                    w = arrived(s0 + i)
                    if kind in "gu":
                        if j >= 2:
                            pe.wait_ge(ffn_dve, j - 1)
                        wk = w.rearrange("p (k n) -> p k n", k=KT)
                        for m in range(2):
                            for k in range(KT):
                                last = mm(ps[:, 2 * (j % 2) + (kind == "u"), m * T:(m + 1) * T],
                                          wk[:, k, m * P:(m + 1) * P], hT[:, k, :], k == 0, k == KT - 1)
                    else:
                        pe.wait_ge(ffn_dve, j + 1)
                        wk = w.rearrange("p (k n) -> p k n", k=2)
                        for m in range(KT):
                            for k in range(2):
                                last = mm(ps[:, 4 + m // 2, (m % 2) * T:(m % 2 + 1) * T], wk[:, k, m * P:(m + 1) * P],
                                          FH[:, j % 2, k * T:(k + 1) * T], j == 0 and k == 0 and m % 2 == 0,
                                          j == FC - 1 and k == 1, skip_group_check=True)
                    last.then_inc(slab_done, 1)

            def experts(lap):
                s0 = first["moe", 1] + lap * NE * N_FFN
                with pe.Fori(0, NE) as e:
                    pe.wait_ge(hot_made, e + (lap * NE + 1))
                    for k in range(KT):
                        for a in range(2):
                            last = mm(ps[:, 4 + k // 4, (k % 4) * P:(k % 4 + 1) * P],
                                      h_tok[:, a, k * P:(k + 1) * P], PT[:, a, :], a == 0, a == 1)
                    last.then_inc(gathered, 1)
                    for a in range(2):
                        last = turn(ps[:, 6, a * P:(a + 1) * P], PTC[:, a, :])
                    last.then_inc(hot_turned, 1)
                    pe.wait_ge(gather_kept, e + (lap * NE + 1))
                    for i, (kind, j) in enumerate(FFN_ORDER):
                        slot = i % FFN_RING
                        pe.wait_ge(slab_in[slot], e * (16 * E_LAPS)
                                   + (16 * (uses[slot] - E_LAPS + i // FFN_RING + 1 + lap * NE * E_LAPS)))
                        w = slab(slot)
                        if kind in "gu":
                            if kind == "g" and j >= 2:
                                pe.wait_ge(e_dve, e * FC + (lap * NE * FC + j - 1))
                            wk = w.rearrange("p (k n) -> p k n", k=KT)
                            for m in range(2):
                                for k in range(KT):
                                    last = mm(ps[:, j % 2 + 4 * (kind == "u"), m * P:(m + 1) * P], wk[:, k, m * P:(m + 1) * P], XS[:, k, :],
                                              k == 0, k == KT - 1)
                        else:
                            pe.wait_ge(e_dve, e * FC + (lap * NE * FC + j + 1))
                            wk = w.rearrange("p (k n) -> p k n", k=2)
                            for k in range(2):
                                for n in range(2):
                                    last = mm(ps[:, 2 + n, :], FH[:, j % 2, k * P:(k + 1) * P],
                                              wk[:, k, n * 512:(n + 1) * 512],
                                              j == 0 and k == 0, j == FC - 1 and k == 1)
                        last.then_inc(slab_done, 1)
                    pe.wait_ge(hot_kept, e + (lap * NE + 1))
                    pe.wait_ge(e_kept, e + (lap * NE + 1))
                    for a in range(2):
                        if a == 1:
                            pe.wait_ge(added, 2 * e + (2 * lap * NE + 1))
                        for n in range(2):
                            last = mm(ps[:, 6 + n, :], PC[:, a * P:(a + 1) * P], YE[:, n * 512:(n + 1) * 512])
                        last.then_inc(scattered, 1)
                    pe.wait_ge(added, 2 * e + (2 * lap * NE + 2))

            pe.wait_ge(consts_made, 1)
            pe.wait_ge(x_in, 16)
            for k in range(KT):
                for a in range(2):
                    last = turn(ps[:, k // 2, (k % 2) * T + a * P:(k % 2) * T + (a + 1) * P],
                                x_tok_in[:, a, k * P:(k + 1) * P])
            last.then_inc(x_turned, 1)
            for L in range(DEPTH):
                pe.wait_ge(rows_in[L], 16 * 12)
                turn(ps[:, VEC_BANK[L], 0:N_VEC], vec_rows[0:N_VEC, :]).then_inc(vec_turned, 1)
                project(L)
                turn_tokens(L)
                groups(L)
                finish_mixer(L)
                if L == 0:
                    dense(L)
            norm(3)
            for i, src in enumerate((hT, xT)):
                for k in range(KT):
                    for a in range(2):
                        last = turn(ps[:, 4 * i + 2 * a + k // 4, (k % 4) * P:(k % 4 + 1) * P],
                                    src[:, k, a * P:(a + 1) * P])
                last.then_inc(tok_turned, 1)
            pe.wait_ge(tok_kept, 2)
            pe.wait_ge(router_in, 16)
            for a in range(2):
                for k in range(KT):
                    last = mm(ps[:, 0, a * NE:(a + 1) * NE], hT[:, k, a * P:(a + 1) * P], w_router[:, k, :],
                              k == 0, k == KT - 1)
            last.then_inc(logits_done, 1)
            pe.wait_ge(routed, 1)
            mm(ps[:, 1, 0:NE], later[:, 0, :], chosen[:, 0, :])
            mm(ps[:, 1, NE:2 * NE], later[:, 0, :], chosen[:, 1, :], True, False)
            mm(ps[:, 1, NE:2 * NE], ones[:], chosen[:, 0, :], False, True)
            mm(ps[:, 1, 2 * NE:3 * NE], ones[:], chosen[:, 0, :], True, False)
            mm(ps[:, 1, 2 * NE:3 * NE], ones[:], chosen[:, 1, :], False, True).then_inc(pos_done, 1)
            experts(0)
            pe.wait_ge(over_made, 1)
            more = pe.value_load(over[0:1, 0:1])
            with pe.If(more > 0):
                experts(1)

        def banks(a, n):
            return ps[:, a:a + (n + 511) // 512, :].rearrange("p b n -> p (b n)")[:, 0:n]

        def group_bases(L, pair):
            return (L * (2 * len(R_STEPS) + len(G_STEPS)) + pair * len(R_STEPS),
                    L * (2 * len(R_COPIES) + len(G_COPIES)) + pair * len(R_COPIES),
                    L * (2 * len(R_SUMS) + len(G_SUMS)) + pair * len(R_SUMS))

        @block.scalar
        def _(act):
            step = Chain(act, act_steps)
            run = nc.scalar.activation

            def norm(n):
                run(XSQ, xT[:].rearrange("p k n -> p (k n)"), ACT.Square).then_inc(squared, 1)
                act.wait_ge(summed, n + 1)
                run(RSTD, ps[:, 7, 0:T], ACT.Sqrt, bias=eps_b[:, 0:1], scale=1.0 / D).then_inc(rooted, 1)

            def in_slab(L, o):
                act.wait_ge(slab_done, first["mix", L] + o + 1)
                src = ps[:, o % 4, :]
                if o < N_CONV:
                    for m in range(2):
                        if o < 7:
                            t = IN_SLABS[o] // P + m
                            dst, scale = shifted(t), one_less_mu[:, L, t:t + 1]
                        else:
                            i = 2 * (o - 7) + m
                            dst, scale = QKV[:, i * T:(i + 1) * T], vec[:, L, V_CONV + 36 + i:V_CONV + 37 + i]
                        last = run(dst, src[:, m * T:(m + 1) * T], ACT.Copy, scale=scale)
                elif o < 15:
                    last = run(Z[:, (o - 13) * 512:(o - 12) * 512], src, ACT.Silu)
                else:
                    last = run(GATES[:, (o - 15) * 512:(o - 14) * 512], src, ACT.Sigmoid)
                last.then_inc(proj_act, 1)

            def project(L):
                norm(2 * L)
                for o in range(3):
                    in_slab(L, o)
                act.wait_ge(proj_dve, N_CONV * L + 1)
                run(LO[0:64, 0:T], LO[0:64, 0:T], ACT.Tanh).then_inc(lora_acted, 1)
                run(LO[:, T:2 * T], LO[:, T:2 * T], ACT.Sigmoid).then_inc(lora_acted, 1)
                for o in range(3, 9):
                    in_slab(L, o)
                act.wait_ge(lora_done, 3 * L + 1)
                for t in range(NT):
                    src = ps[:, 4 + t // 2, (t % 2) * T:(t % 2 + 1) * T].rearrange("p (c n) -> p c n", c=2)
                    last = run(LC[:, 2 * t:2 * t + 2, 1:129], src, ACT.Sigmoid, bias=vec[:, L, V_W0 + t:V_W0 + t + 1])
                last.then_inc(decay_sig, 1)
                act.wait_ge(lora_done, 3 * L + 2)
                for t in range(NT):
                    last = run(A3[:, t, :], ps[:, 6 + t // 2, (t % 2) * T:(t % 2 + 1) * T], ACT.Sigmoid,
                               bias=vec[:, L, V_A0 + t:V_A0 + t + 1])
                last.then_inc(rate_sig, 1)
                act.wait_ge(kk_made, L + 1)
                run(SQ, KK, ACT.Square).then_inc(kk_squared, 1)
                in_slab(L, 9)
                in_slab(L, 10)
                act.wait_ge(log_decay, L + 1)
                run(view(o_EP, 1032), view(o_LC, 1032), ACT.Exp, scale=-DECAY_C).then_inc(decays, 1)
                run(view(o_EM, 1032), view(o_LC, 1032), ACT.Exp, scale=DECAY_C).then_inc(decays, 1)
                act.wait_ge(kk_summed, L + 1)
                run(SQ, banks(4, 1024), ACT.Sqrt, bias=eps_b[:, 0:1]).then_inc(kk_rooted, 1)
                in_slab(L, 11)
                in_slab(L, 12)
                act.wait_ge(lora_done, 3 * L + 3)
                run(G, banks(6, 1024), ACT.Copy).then_inc(gate_kept, 1)
                act.wait_ge(ab_dve, 3 * L + 1)
                step(run(g4[:, 1, :], g4[:, 0, :], ACT.Abs))
                run(g4[:, 1, :], g4[:, 1, :], ACT.Exp, scale=-1.0).then_inc(ab_act, 1)
                act.wait_ge(ab_dve, 3 * L + 2)
                run(g4[:, 3, :], g4[:, 2, :], ACT.Ln).then_inc(ab_act, 1)
                run(GB[:, T:2 * T], ps[0:GH, 4, T:2 * T], ACT.Sigmoid).then_inc(ab_act, 1)
                act.wait_ge(proj_dve, N_CONV * (L + 1))
                for i in range(3):
                    last = run(QKV[:, i * 1024:(i + 1) * 1024], QKV[:, i * 1024:(i + 1) * 1024], ACT.Silu)
                    last.then_inc(silu_done, 1)
                in_slab(L, 13)
                in_slab(L, 14)
                act.wait_ge(silu_done, 3 * L + 2)
                run(QSQ, Q1, ACT.Square).then_inc(qk_squared, 1)
                run(KSQ, K1.rearrange("p (q n) -> p q n", q=4), ACT.Square).then_inc(qk_squared, 1)
                in_slab(L, 15)
                in_slab(L, 16)
                in_slab(L, 17)
                act.wait_ge(qk_summed, 2 * L + 1)
                run(QSQ, banks(4, 1024), ACT.Sqrt, bias=eps_b[:, 1:2], scale=float(P)).then_inc(qk_rooted, 1)
                in_slab(L, 18)
                act.wait_ge(qk_summed, 2 * L + 2)
                run(KSQ.rearrange("p q n -> p (q n)"), banks(6, 1024), ACT.Sqrt,
                    bias=eps_b[:, 0:1]).then_inc(qk_rooted, 1)
                in_slab(L, 19)
                in_slab(L, 20)
                act.wait_ge(spread, L + 1)
                act.wait_ge(rw_ready, L + 1)
                step(run(BG, ps[:, 4:8, 0:T], ACT.Copy))
                run(BB, ps[:, 4:8, T:2 * T], ACT.Copy).then_inc(spread_kept, 1)
                in_slab(L, 21)
                in_slab(L, 22)
                run(EG, BG, ACT.Exp).then_inc(kdec_made, 1)
                act.wait_ge(kdec_arg, L + 1)
                run(kdec, kdec, ACT.Exp).then_inc(kdec_made, 1)
                act.wait_ge(dd_made, L + 1)
                run(DD, DD, ACT.Exp).then_inc(dd_exp, 1)

            def turn_tokens(L):
                act.wait_ge(rw_turned, L + 1)
                run(TV, ps[:, 0:2, :], ACT.Copy)
                run(TB, ps[:, 2, :], ACT.Copy)
                run(TK, ps[:, 3, :], ACT.Copy).then_inc(rw_kept, 1)
                act.wait_ge(gdn_turned, L + 1)
                run(TVB, ps[:, 5:7, :], ACT.Copy).then_inc(gdn_kept, 1)

            def groups(L):
                for pair in range(3):
                    rw = pair < 2
                    base, _, _ = group_bases(L, pair)
                    steps = R_AT if rw else G_AT

                    def copy(s, what, dst, src, scale=None):
                        act.wait_ge(mat_done[s], base + steps[what])
                        if scale is None:
                            run(dst, src, ACT.Copy).then_inc(mat_copied[s], 1)
                        else:
                            run(dst, src, ACT.Copy, scale=scale).then_inc(mat_copied[s], 1)

                    def bank(s, b):
                        return ps[:, 4 * s + b, :].rearrange("p (q n) -> p q n", q=4)

                    def turned(s, what):
                        copy(s, what, DT[s], bank(s, 0))

                    def both(s, what):
                        copy(s, what, DG[s][:, :, 0:P], bank(s, 1))
                        copy(s, what, DT[s], bank(s, 2))

                    for what in ("dT", "sq", "gen1", "gen2", "gT", "m", "gen3", "gen4"):
                        for s in range(2):
                            (turned if what in ("dT", "gT") else both)(s, what)
                    n = HD if rw else P

                    def narrow(s, b):
                        return ps[:, 4 * s + b, 0:2 * P].rearrange("p (q n) -> p q n", q=2)[:, :, 0:n]

                    if rw:
                        for s in range(2):
                            copy(s, "z0", ZB[s][:, :, 0:n], ps[:, 4 * s:4 * s + 3:2, 0:n])
                    for s in range(2):
                        copy(s, "u0", UB[s].rearrange("p (h c) n -> p h c n", c=2)[:, :, 0, 0:n], narrow(s, 1))
                    for s in range(2):
                        if rw:
                            g = 2 * pair + s
                            copy(s, "s", SB[s][:, 0, 0:HD], ps[:, 4 * s + 2, 0:HD], scol[:, g:g + 1])
                        else:
                            copy(s, "s", SB[s], narrow(s, 2))
                    if rw:
                        for s in range(2):
                            copy(s, "z1", ZB[s][:, :, 0:n], ps[:, 4 * s:4 * s + 3:2, 0:n])
                    for s in range(2):
                        copy(s, "u1", UB[s].rearrange("p (h c) n -> p h c n", c=2)[:, :, 1, 0:n], narrow(s, 1))

            def finish_mixer(L):
                sums = (L + 1) * (2 * len(R_SUMS) + len(G_SUMS))
                act.wait_ge(mat_summed[0], sums)
                act.wait_ge(mat_summed[1], sums)
                run(QSQ, OG, ACT.Square).then_inc(hn_act, 1)
                act.wait_ge(hn_summed, 3 * L + 2)
                run(QSQ, banks(4, 1024), ACT.Sqrt, bias=eps_b[:, 0:1], scale=1.0 / P).then_inc(hn_act, 1)
                act.wait_ge(hn_dve, 3 * L + 1)
                run(SQ, KK, ACT.Square).then_inc(hn_act, 1)
                act.wait_ge(hn_summed, 3 * L + 3)
                run(SQ, banks(2, 1024), ACT.Sqrt, bias=eps_b[:, 2:3], scale=1.0 / HD).then_inc(hn_act, 1)

            def dense(L):
                act.wait_ge(mixed, 4 * (L + 1))
                norm(2 * L + 1)
                s0 = first["ffn", L]
                for j in range(FC):
                    act.wait_ge(slab_done, s0 + AT["g", j] + 1)
                    if j >= 2:
                        act.wait_ge(ffn_dve, j - 1)
                    run(FG[:, j % 2, :], ps[:, 2 * (j % 2), :], ACT.Silu).then_inc(ffn_act, 1)

            def experts(lap):
                s0 = first["moe", 1] + lap * NE * N_FFN
                with act.Fori(0, NE) as e:
                    act.wait_ge(gathered, e + (lap * NE + 1))
                    run(XS, ps[:, 4:6, :].rearrange("p b (k n) -> p (b k) n", n=P), ACT.Copy).then_inc(gather_kept, 1)
                    act.wait_ge(hot_turned, e + (lap * NE + 1))
                    run(PC, ps[:, 6, 0:2 * P], ACT.Copy).then_inc(hot_kept, 1)
                    for j in range(FC):
                        act.wait_ge(slab_done, e * N_FFN + (s0 + AT["g", j] + 1))
                        if j >= 2:
                            act.wait_ge(e_dve, e * FC + (lap * NE * FC + j - 1))
                        run(FG[:, j % 2, 0:T], ps[:, j % 2, 0:T], ACT.Silu).then_inc(e_act, 1)
                    act.wait_ge(slab_done, e * N_FFN + (s0 + N_FFN))
                    run(YE, banks(2, 1024), ACT.Copy).then_inc(e_kept, 1)

            def shifted(t):
                if t >= 12:
                    return LO[:, (t - 12) * T:(t - 11) * T]
                return (R3, K3, V3)[t // NT][:, t % NT, :]

            act.wait_ge(x_turned, 1)
            run(xT[:].rearrange("p k n -> p (k n)"), banks(0, 2048), ACT.Copy).then_inc(x_kept, 1)
            act.wait_ge(x_kept, 1)
            for L in range(DEPTH):
                act.wait_ge(vec_turned, L + 1)
                run(vec[:, L, :], ps[:, VEC_BANK[L], 0:N_VEC], ACT.Copy).then_inc(vec_kept, 1)
                act.wait_ge(vec_kept, 2 * L + 2)
                if L == 0:
                    act.wait_ge(head_in, 16 * 2 * DEPTH)
                    step(run(minus_a[:], head_raw[:, 0, :], ACT.Exp))
                    run(minus_a[:], minus_a[:], ACT.Copy, scale=-1.0)
                if L:
                    act.wait_ge(ffn_added, 4)
                project(L)
                turn_tokens(L)
                groups(L)
                finish_mixer(L)
                if L == 0:
                    dense(L)
            act.wait_ge(mixed, 8)
            norm(3)
            for i, dst in enumerate((h_tok, x_tok)):
                act.wait_ge(tok_turned, i + 1)
                run(dst.rearrange("p a n -> p (a n)"), banks(4 * i, 2048), ACT.Copy).then_inc(tok_kept, 1)
            act.wait_ge(diff_made, 1)
            run(g_exp, g_diff, ACT.Exp).then_inc(exp_made, 1)
            experts(0)
            act.wait_ge(over_made, 1)
            more = act.value_load(over[0:1, 0:1])
            with act.If(more > 0):
                experts(1)
            act.wait_ge(moe_added, 1)
            for a in range(2):
                step(run(x_sq[:, a, :], x_tok[:, a, :], ACT.Square, accum_out=xsum[:, a:a + 1]))
            run(xsum, xsum, ACT.Sqrt, bias=eps_b[:, 0:1], scale=1.0 / D).then_inc(fin_root, 1)

        @block.vector
        def _(dve):
            step = Chain(dve, dve_steps)
            tt, ts, stt = nc.vector.tensor_tensor, nc.vector.tensor_scalar, nc.vector.scalar_tensor_tensor

            def v_at(L, at_, n=1):
                return vec[:, L, at_:at_ + n]

            def per_tile(L, at_):
                return vec[:, L, at_:at_ + NT].unsqueeze(2).broadcast_to([P, NT, T])

            def by_tile(ap):
                return ap.rearrange("p (t n) -> p t n", t=NT)

            def by_chunk(ap):
                return ap.rearrange("p (q n) -> p q n", q=8)

            def norm(n, at_):
                dve.wait_ge(rooted, n + 1)
                step(nc.vector.reciprocal(RSTD, RSTD))
                for k in range(KT):
                    g = vec[:, n // 2, at_ + k:at_ + k + 1]
                    last = stt(hT[:, k, :], xT[:, k, :], g, RSTD, ALU.mult, ALU.mult)
                last.then_inc(normed, 1)

            def in_slab(L, o):
                dve.wait_ge(proj_act, N_IN * L + o + 1)
                for m in range(2):
                    src = ps[:, o % 4, m * T:(m + 1) * T]
                    if o < 7:
                        t = IN_SLABS[o] // P + m
                        dst = (LO[:, (t - 12) * T:(t - 11) * T] if t >= 12 else (R3, K3, V3)[t // NT][:, t % NT, :])
                        last = stt(dst[:, 1:T], src[:, 0:T - 1], v_at(L, V_MU + t), dst[:, 1:T], ALU.mult, ALU.add)
                if o >= 7:
                    for back in range(1, 4):
                        for m in range(2):
                            src = ps[:, o % 4, m * T:(m + 1) * T]
                            i = 2 * (o - 7) + m
                            dst = QKV[:, i * T + back:(i + 1) * T]
                            last = stt(dst, src[:, 0:T - back], v_at(L, V_CONV + (3 - back) * 12 + i), dst,
                                       ALU.mult, ALU.add)
                            if back < 3:
                                step.mark(last)
                        if back < 3:
                            dve.wait_ge(dve_steps, step.n)
                last.then_inc(proj_dve, 1)

            def project(L):
                norm(2 * L, V_N1)
                step.mark(nc.vector.memset(LC[:, :, 0:1], 0.0))
                for o in range(7):
                    in_slab(L, o)
                dve.wait_ge(proj_dve, N_CONV * L + 7)
                tt(by_tile(KK), K3, per_tile(L, V_KK), ALU.mult).then_inc(kk_made, 1)
                in_slab(L, 7)
                in_slab(L, 8)
                dve.wait_ge(decay_sig, L + 1)
                flat = view(o_LC, 1032)
                step(nc.vector.tensor_tensor_scan(flat, restart[:], flat, 0.0, ALU.mult, ALU.add))
                step(nc.vector.tensor_copy(mid, LC[:, :, 64]))
                tt(LC, LC, mid.unsqueeze(2).broadcast_to([P, 8, 129]), ALU.subtract).then_inc(log_decay, 1)
                in_slab(L, 9)
                in_slab(L, 10)
                dve.wait_ge(kk_rooted, L + 1)
                step(nc.vector.reciprocal(SQ, SQ))
                step(tt(KK, KK, SQ, ALU.mult))
                in_slab(L, 11)
                in_slab(L, 12)
                dve.wait_ge(rate_sig, L + 1)
                for t in range(NT):
                    last = ts(SQ[:, t * T:(t + 1) * T], A3[:, t, :], -1.0, v_at(L, V_KA + t), ALU.add, ALU.mult)
                step(last)
                step.mark(stt(by_tile(K3_flat), by_tile(SQ), 1.0, K3, ALU.add, ALU.mult))
                dve.wait_ge(decays, 2 * L + 2)
                stt(AR[:, :, 0, :], by_chunk(KK), -1.0, EP[:, :, 0:P], ALU.mult, ALU.mult)
                tt(AR[:, :, 1, :], by_chunk(view(o_R, 1024)), EP[:, :, 1:129], ALU.mult)
                step(tt(BH, by_chunk(KK), by_chunk(view(o_A, 1024)), ALU.mult))
                tt(scol, EP[:, 0::2, P], EM[:, 1::2, 0], ALU.mult)
                tt(BH, BH, EM[:, :, 1:129], ALU.mult)
                tt(KH, by_chunk(K3_flat), EM[:, :, 1:129], ALU.mult).then_inc(rw_ready, 1)
                step(tt(SQ, view(o_R, 1024), K3_flat, ALU.mult))
                tt(by_tile(SQ), by_tile(SQ), per_tile(L, V_RK), ALU.mult).then_inc(rk_ready, 1)
                dve.wait_ge(ab_done, L + 1)
                dve.wait_ge(head_in, 16 * 2 * DEPTH)
                ts(g4[:, 0, :], ps[0:GH, 4, 0:T], head_raw[:, 1, L:L + 1], None, ALU.add).then_inc(ab_dve, 1)
                dve.wait_ge(ab_act, 3 * L + 1)
                ts(g4[:, 2, :], g4[:, 1, :], 1.0, None, ALU.add).then_inc(ab_dve, 1)
                dve.wait_ge(ab_dve, 3 * L + 2)
                step.mark(nc.vector.reciprocal(g4[:, 4, :], g4[:, 2, :]))
                dve.wait_ge(ab_act, 3 * L + 2)
                step(ts(g4[:, 2, :], g4[:, 2, :], -1.0, None, ALU.add))
                step(tt(g4[:, 2, :], g4[:, 1, :], g4[:, 2, :], ALU.subtract))
                step(tt(g4[:, 2, :], g4[:, 2, :], g4[:, 4, :], ALU.mult))
                step(tt(g4[:, 2, :], g4[:, 2, :], g4[:, 3, :], ALU.add))
                step(stt(g4[:, 2, :], g4[:, 0, :], 0.0, g4[:, 2, :], ALU.max, ALU.add))
                step(ts(g4[:, 2, :], g4[:, 2, :], minus_a[:, L:L + 1], None, ALU.mult))
                for c in range(2):
                    last = nc.vector.tensor_tensor_scan(GB[:, c * P:(c + 1) * P], ones[0:GH, :],
                                                        g4[:, 2, c * P:(c + 1) * P], 0.0, ALU.mult, ALU.add)
                last.then_inc(ab_dve, 1)
                dve.wait_ge(rk_summed, L + 1)
                tt(view(o_R, 1024), banks(6, 1024), view(o_V, 1024), ALU.mult).then_inc(bonus_made, 1)
                dve.wait_ge(qk_rooted, 2 * L + 1)
                step(nc.vector.reciprocal(QSQ, QSQ))
                tt(KBQ[:, :, 1, :], by_chunk(Q1), by_chunk(QSQ), ALU.mult)
                dve.wait_ge(qk_rooted, 2 * L + 2)
                ksq = KSQ.rearrange("p q n -> p (q n)")
                step(nc.vector.reciprocal(ksq, ksq))
                step(tt(K1, K1, ksq, ALU.mult))
                dve.wait_ge(spread_kept, L + 1)
                tt(KBQ[:, :, 0, :], by_chunk(K1), by_chunk(view(o_EM, 1024)), ALU.mult)
                dve.wait_ge(silu_done, 3 * L + 3)
                tt(V1, V1, view(o_EM, 1024), ALU.mult).then_inc(vb_made, 1)
                dve.wait_ge(cols_turned, L + 1)
                nc.vector.tensor_copy(gcol, ps[:, 4, 0:2 * GH].rearrange("p (c h) -> p c h", c=2)).then_inc(cols_kept, 1)
                dve.wait_ge(cols_kept, L + 1)
                tt(kdec, BG[:, :, P - 1], gcol[:, 0, :], ALU.subtract).then_inc(kdec_arg, 1)
                for h in range(GH):
                    for c in range(2):
                        last = ts(DD[:, 2 * h + c, :], BG[:, h, c * P:(c + 1) * P], gcol[:, c, h:h + 1], 0.0,
                                  ALU.subtract, ALU.min)
                last.then_inc(dd_made, 1)

            def turn_tokens(L):
                dve.wait_ge(kdec_made, 2 * L + 2)
                dve.wait_ge(gdn_turned, L + 1)
                src = ps[:, 7, :].rearrange("p (h n) -> p h n", h=GH)
                tt(TKN.rearrange("p (h n) -> p h n", h=GH), src, kdec.unsqueeze(2).broadcast_to([P, GH, P]),
                   ALU.mult).then_inc(gdn_keyed, 1)
                late = slice(P, 2 * P)
                kb = KBQ.rearrange("p (h c) s n -> p h c s n", c=2)
                stt(KG.rearrange("p (h n) -> p h n", h=GH), kb[:, :, 1, 0, :], -1.0, EG[:, :, late], ALU.mult, ALU.mult)
                tt(QG.rearrange("p (h n) -> p h n", h=GH), kb[:, :, 1, 1, :], EG[:, :, late], ALU.mult)
                dve.wait_ge(dd_exp, L + 1)
                dve.wait_ge(rw_turned, L + 1)
                tt(DM, DD.unsqueeze(2).broadcast_to([P, 8, 2, P]),
                   later_neg[:].unsqueeze(1).broadcast_to([P, 8, 2, P]), ALU.mult).then_inc(gdn_ready, 1)

            def groups(L):
                for pair in range(3):
                    rw = pair < 2
                    base, _, _ = group_bases(L, pair)
                    steps = R_AT if rw else G_AT
                    if pair == 2:
                        dve.wait_ge(gdn_ready, L + 1)
                    flat_mask = later[:].rearrange("p s n -> p (s n)")

                    def masked(s, dst, b):
                        g = 2 * pair + s
                        src = ps[:, 4 * s + b:4 * s + b + 2, :].rearrange("p b (q n) -> p (b q) n", q=2)
                        if rw:
                            mask = flat_mask.unsqueeze(1).broadcast_to([P, 4, 2 * P])
                        else:
                            mask = DM[:, 4 * (g - 4):4 * (g - 4) + 4, :, :].rearrange("p q s n -> p q (s n)")
                        return tt(dst, src, mask, ALU.mult)

                    for s in range(2):
                        dve.wait_ge(mat_done[s], base + 1)
                        Q, A, Gm = MQ[s][:, :, 0:P], DG[s][:, :, 0:P], DG[s][:, :, P:2 * P]
                        step(masked(s, MQ[s], 0))
                        tt(A, Q, blocks16[:].unsqueeze(1).broadcast_to([P, 4, P]), ALU.mult).then_inc(mat_summed[s], 1)
                        sums = L * (2 * len(R_SUMS) + len(G_SUMS)) + pair * len(R_SUMS)
                        if rw:
                            step.mark(masked(s, MK[s], 2))
                        dve.wait_ge(mat_summed[s], sums + 1)
                        step.mark(tt(Gm, A, ident[:].unsqueeze(1).broadcast_to([P, 4, P]), ALU.add))
                        tt(Q, Q, A, ALU.subtract).then_inc(mat_summed[s], 1)
                    for what in ("gen1", "gen2", "last1", "gen3", "gen4", "last2"):
                        for s in range(2):
                            Gm = DG[s][:, :, P:2 * P]
                            dve.wait_ge(mat_done[s], base + steps[what])
                            tt(Gm, ps[:, 4 * s + 3, :].rearrange("p (q n) -> p q n", q=4), Gm,
                               ALU.add).then_inc(mat_summed[s], 1)
                    if not rw:
                        for s in range(2):
                            g = 2 * pair + s
                            dve.wait_ge(mat_done[s], base + steps["z1"])
                            src = ps[:, 4 * s, 0:2 * P]
                            vb = TVB[:, 1, 2 * (g - 4) * P:(2 * (g - 4) + 2) * P]
                            tt(ZB[s].rearrange("p q n -> p (q n)"), src, vb, ALU.add).then_inc(mat_summed[s], 1)
                    for s in range(2):
                        g = 2 * pair + s
                        dve.wait_ge(mat_done[s], base + steps["o"])
                        if rw:
                            last = nc.vector.tensor_copy(KK[:, g * T:(g + 1) * T], ps[:, 4 * s + 3, 0:T])
                        else:
                            last = nc.vector.tensor_copy(OG[:, (g - 4) * 512:(g - 3) * 512], ps[:, 4 * s + 3, :])
                        last.then_inc(mat_summed[s], 1)

            def finish_mixer(L):
                dve.wait_ge(hn_summed, 3 * L + 1)
                sums = (L + 1) * (2 * len(R_SUMS) + len(G_SUMS))
                dve.wait_ge(mat_summed[0], sums)
                dve.wait_ge(mat_summed[1], sums)
                stt(KK, banks(0, 1024), -1.0 / HD, KK, ALU.mult, ALU.add).then_inc(hn_dve, 1)
                dve.wait_ge(hn_act, 4 * L + 2)
                step(nc.vector.reciprocal(QSQ, QSQ))
                step(tt(OG, OG, QSQ, ALU.mult))
                stt(OG, OG, v_at(L, V_GN), Z, ALU.mult, ALU.mult).then_inc(hn_dve, 1)
                dve.wait_ge(hn_act, 4 * L + 4)
                step(nc.vector.reciprocal(SQ, SQ))
                step(tt(KK, KK, SQ, ALU.mult))
                for t in range(NT):
                    cut = slice(t * T, (t + 1) * T)
                    last = ts(KK[:, cut], KK[:, cut], v_at(L, V_LG + t), v_at(L, V_LB + t), ALU.mult, ALU.add)
                step(last)
                step(tt(KK, KK, view(o_R, 1024), ALU.add))
                tt(KK, KK, G, ALU.mult).then_inc(hn_dve, 1)
                for i in range(2):
                    dve.wait_ge(slab_done, first["mix", L] + N_IN + i + 1)
                    step.mark(tt(YT[:, i * 1024:(i + 1) * 1024], banks(4 + 2 * i, 1024),
                                 GATES[:, 2048 + i * 1024:2048 + (i + 1) * 1024], ALU.mult))
                for i in range(2):
                    dve.wait_ge(slab_done, first["mix", L] + N_IN + i + 3)
                    ya = GATES[:, i * 1024:(i + 1) * 1024]
                    step(tt(ya, banks(2 * i, 1024), ya, ALU.mult))
                    last = tt(YT[:, i * 1024:(i + 1) * 1024], YT[:, i * 1024:(i + 1) * 1024], ya, ALU.add)
                last.then_inc(merged, 1)
                for j in range(4):
                    dve.wait_ge(slab_done, first["mix", L] + N_IN + 4 + j + 1)
                    xs = xT[:, 2 * j:2 * j + 2, :].rearrange("p k n -> p (k n)")
                    tt(xs, ps[:, j, :], xs, ALU.add).then_inc(mixed, 1)

            def dense(L):
                norm(2 * L + 1, V_N2)
                s0 = first["ffn", L]
                for j in range(FC):
                    dve.wait_ge(ffn_act, j + 1)
                    dve.wait_ge(slab_done, s0 + AT["u", j] + 1)
                    if j >= 2:
                        dve.wait_ge(slab_done, s0 + AT["d", j - 2] + 1)
                    tt(FH[:, j % 2, :], ps[:, 2 * (j % 2) + 1, :], FG[:, j % 2, :], ALU.mult).then_inc(ffn_dve, 1)
                dve.wait_ge(slab_done, s0 + N_FFN)
                for j in range(4):
                    xs = xT[:, 2 * j:2 * j + 2, :].rearrange("p k n -> p (k n)")
                    tt(xs, ps[:, 4 + j, :], xs, ALU.add).then_inc(ffn_added, 1)

            def route():
                dve.wait_ge(logits_done, 1)
                step(nc.vector.tensor_copy(logits, ps[:, 0, 0:2 * NE].rearrange("p (a n) -> p a n", a=2)))
                for a in range(2):
                    step(nc.vector.max(top[:, a, :], logits[:, a, :]))
                    step(nc.vector.max_index(topi[:, a, :], top[:, a, :], logits[:, a, :]))
                step(nc.vector.tensor_copy(topi_f, topi[:]))
                tt(g_diff, top[:, :, 1], top[:, :, 0], ALU.subtract).then_inc(diff_made, 1)
                dve.wait_ge(exp_made, 1)
                step(ts(g_first, g_exp, 1.0, None, ALU.add))
                step(nc.vector.reciprocal(g_first, g_first))
                step(tt(g_second, g_exp, g_first, ALU.mult))
                for a in range(2):
                    step.mark(ts(hot1[:, a, :], slots[:, 0:NE], topi_f[:, a, 0:1], None, ALU.is_equal))
                    step(ts(hot2[:, a, :], slots[:, 0:NE], topi_f[:, a, 1:2], None, ALU.is_equal))
                tt(chosen, hot1, hot2, ALU.add).then_inc(routed, 1)
                dve.wait_ge(routed, 1)
                for a in range(2):
                    step.mark(ts(hot1[:, a, :], hot1[:, a, :], g_first[:, a:a + 1], None, ALU.mult))
                    step(ts(hot2[:, a, :], hot2[:, a, :], g_second[:, a:a + 1], None, ALU.mult))
                step.mark(tt(combine, hot1, hot2, ALU.add))
                dve.wait_ge(pos_done, 1)
                step(nc.vector.tensor_copy(pos, ps[:, 1, 0:2 * NE].rearrange("p (a n) -> p a n", a=2)))
                step(nc.vector.reduce_max(most, ps[:, 1, 2 * NE:3 * NE], AX_X))
                ts(over[:], most, float(P), None, ALU.is_gt).then_inc(over_made, 1)

            def experts(lap):
                s0 = first["moe", 1] + lap * NE * N_FFN
                if lap:
                    ts(pos, pos, -float(P), None, ALU.add).then_inc(pos_moved, 1)
                    dve.wait_ge(pos_moved, 1)
                with dve.Fori(0, NE) as e:
                    for a in range(2):
                        p_col = pos[:, a, bass.ds(e, 1)]
                        ts(PT[:, a, :], slots[:], p_col, chosen[:, a, bass.ds(e, 1)], ALU.is_equal, ALU.mult)
                        last = ts(PTC[:, a, :], slots[:], p_col, combine[:, a, bass.ds(e, 1)], ALU.is_equal, ALU.mult)
                    last.then_inc(hot_made, 1)
                    for j in range(FC):
                        dve.wait_ge(e_act, e * FC + (lap * NE * FC + j + 1))
                        dve.wait_ge(slab_done, e * N_FFN + (s0 + AT["u", j] + 1))
                        if j >= 2:
                            dve.wait_ge(slab_done, e * N_FFN + (s0 + AT["d", j - 2] + 1))
                        tt(FH[:, j % 2, 0:T], ps[:, 4 + j % 2, 0:T], FG[:, j % 2, 0:T], ALU.mult).then_inc(e_dve, 1)
                    for a in range(2):
                        dve.wait_ge(scattered, 2 * e + (2 * lap * NE + a + 1))
                        tt(x_tok[:, a, :], banks(6, 1024), x_tok[:, a, :], ALU.add).then_inc(added, 1)

            dve.wait_ge(consts_made, 1)
            dve.wait_ge(x_kept, 1)
            for L in range(DEPTH):
                dve.wait_ge(vec_kept, 2 * L + 1)
                ts(one_less_mu[:, L, :], vec[:, L, V_MU:V_MU + 14], -1.0, 1.0, ALU.mult, ALU.add).then_inc(vec_kept, 1)
                project(L)
                turn_tokens(L)
                groups(L)
                finish_mixer(L)
                if L == 0:
                    dense(L)
            norm(3, V_N2)
            route()
            experts(0)
            more = dve.value_load(over[0:1, 0:1])
            with dve.If(more > 0):
                experts(1)
            nc.vector.memset(most, 0.0).then_inc(moe_added, 1)
            dve.wait_ge(fin_in, 16)
            dve.wait_ge(fin_root, 1)
            step(nc.vector.reciprocal(xsum, xsum))
            for a in range(2):
                stt(x_tok_out[:, a, :], x_tok[:, a, :], xsum[:, a:a + 1], fin_g, ALU.mult, ALU.mult).then_inc(fin_made, 1)


_INS = ['x', 'norm1_g', 'w_in', 'tshift_mu', 'w0', 'w_decay_up', 'a0', 'w_iclr_up', 'w_gate_up', 'k_k', 'k_a', 'r_k',
        'lnx_g', 'lnx_b', 'w_pa', 'conv_w', 'a_log', 'dt_bias', 'gdn_norm_g', 'w_pb', 'w_out', 'norm2_g',
        'ffn_w_gate', 'ffn_w_up', 'ffn_w_down', 'moe_router', 'moe_w_gate', 'moe_w_up', 'moe_w_down', 'final_g']
_OUTS = [((1, T, D), 'float32')]


def kernel(**inputs):
    import numpy as _np
    import concourse.bacc as _bacc
    from concourse import mybir as _mybir
    from concourse.bass_utils import run_bass_kernel_spmd as _run

    nc = _bacc.Bacc("TRN2", target_bir_lowering=False, num_devices=1)
    arrays, args = {}, []
    for name in _INS:
        a = _np.ascontiguousarray(inputs[name])
        arrays[f"in_{name}_dram"] = a
        args.append(nc.dram_tensor(f"in_{name}_dram", a.shape, _mybir.dt.from_np(a.dtype), kind="ExternalInput").ap())
    for i, (shape, dtype) in enumerate(_OUTS):
        dt = _mybir.dt.from_np(_np.dtype(dtype))
        args.append(nc.dram_tensor(f"out_{i}_dram", shape, dt, kind="ExternalOutput").ap())
    trunk(nc, *args)
    r = _run(nc, [arrays], core_ids=[0])
    return r.results[0]["out_0_dram"]
```

```python
from contextlib import ExitStack

import concourse.bass as bass
from concourse import mybir

F32 = mybir.dt.float32
F32R = mybir.dt.float32r
BF16 = mybir.dt.bfloat16
I32 = mybir.dt.int32
U32 = mybir.dt.uint32
ALU = mybir.AluOpType
ACT = mybir.ActivationFunctionType
AX_X = mybir.AxisListType.X

P = 128
D = 1024
T = 256
DEPTH = 2
KT = D // P
RW = 512
NT = RW // P
HD = 64
GH = 4
RWKV_COLS = 1792
GDN_BASE = RWKV_COLS
AB_BASE = GDN_BASE + 3 * RW
Z_BASE = AB_BASE + 2 * GH
GATE_BASE = Z_BASE + RW
F = 2816
NE = 8
NORM_EPS = 1e-6
GN_EPS = 64e-5
DECAY_C = 0.6065306597126334

SLAB = 2048
COLS = SLAB // KT
FC = F // COLS
MIX_RING = 3
FFN_RING = 11
HIGHS = 3
IN_SLABS = ([1536] + [512, 768, 0, 256, 1024, 1280] + [GDN_BASE + COLS * i for i in range(6)]
            + [Z_BASE, Z_BASE + COLS] + [GATE_BASE + COLS * i for i in range(8)])
N_IN = len(IN_SLABS)
N_CONV = 13
N_MIX = N_IN + 8
N_FFN = 3 * FC

V_MU, V_W0, V_A0, V_KK, V_KA, V_RK, V_LG, V_LB, V_CONV, V_N1, V_N2, V_GN = (
    0, 14, 18, 22, 26, 30, 34, 38, 42, 90, 98, 106)
N_VEC = 107
VEC_BANK = (6, 0)

MIX0 = MIX_RING * SLAB


def ffn_order():
    order = [("g", 0), ("u", 0)]
    for j in range(1, FC):
        order += [("g", j), ("u", j), ("d", j - 1)]
    return order + [("d", FC - 1)]


FFN_ORDER = ffn_order()
AT = {key: n for n, key in enumerate(FFN_ORDER)}

R_STEPS = ["pair", "dT", "sq", "gen1", "gen2", "last1", "gT", "m", "gen3", "gen4", "last2",
           "z0", "u0", "s", "z1", "u1", "o"]
G_STEPS = [s for s in R_STEPS if s != "z0"]
R_AT = {s: n + 1 for n, s in enumerate(R_STEPS)}
G_AT = {s: n + 1 for n, s in enumerate(G_STEPS)}
R_COPIES = ["dT", "sq", "sqT", "gen1", "gen1T", "gen2", "gen2T", "gT", "m", "mT", "gen3", "gen3T", "gen4", "gen4T",
            "z0", "u0", "s", "z1", "u1"]
G_COPIES = [s for s in R_COPIES if s not in ("z0", "z1")]
RC_AT = {s: n + 1 for n, s in enumerate(R_COPIES)}
GC_AT = {s: n + 1 for n, s in enumerate(G_COPIES)}
R_SUMS = ["d", "masked", "gen1", "gen2", "last1", "gen3", "gen4", "last2", "o"]
G_SUMS = ["d", "masked", "gen1", "gen2", "last1", "gen3", "gen4", "last2", "z1", "o"]
RS_AT = {s: n + 1 for n, s in enumerate(R_SUMS)}
GS_AT = {s: n + 1 for n, s in enumerate(G_SUMS)}


class Chain:

    def __init__(self, eng, sem):
        self.eng, self.sem, self.n = eng, sem, 0

    def mark(self, ins):
        self.n += 1
        ins.then_inc(self.sem, 1)

    def __call__(self, ins):
        self.mark(ins)
        self.eng.wait_ge(self.sem, self.n)


def trunk(nc, x, norm1_g, w_in, tshift_mu, w0, w_decay_up, a0, w_iclr_up, w_gate_up, k_k, k_a, r_k, lnx_g, lnx_b,
          w_pa, conv_w, a_log, dt_bias, gdn_norm_g, w_pb, w_out, norm2_g, ffn_w_gate, ffn_w_up, ffn_w_down,
          moe_router, moe_w_gate, moe_w_up, moe_w_down, final_g, out, dbg=None):
    with ExitStack() as ctx:
        def sb(name, shape, dt=F32):
            return ctx.enter_context(nc.sbuf_tensor(name, shape, dt))

        def sem(name):
            return ctx.enter_context(nc.semaphore(name))

        ps = ctx.enter_context(nc.psum_tensor("ps", [P, 8, 512], F32))

        xT = sb("xT", [P, KT, T])
        hT = sb("hT", [P, KT, T])
        hT_at = nc.sbuf_base - 4 * KT * T
        ident = sb("ident", [P, P])
        ones = sb("ones", [P, P])
        head_ones = sb("head_ones", [P, P])
        later = sb("later", [P, 2, P])
        later_neg = sb("later_neg", [P, 2, P])
        blocks16 = sb("blocks16", [P, P])
        sel = sb("sel", [GH, GH, P])
        restart = sb("restart", [P, 8 * 129], BF16)
        slots = sb("slots", [P, P])
        vec_rows = sb("vec_rows", [P, P])
        vec = sb("vec", [P, DEPTH, N_VEC])
        one_less_mu = sb("one_less_mu", [P, DEPTH, 14])
        head_raw = sb("head_raw", [GH, 2, DEPTH])
        minus_a = sb("minus_a", [GH, DEPTH])
        lora_up = sb("lora_up", [P, RW])
        gate_up = sb("gate_up", [P, RW])
        w_ab = sb("w_ab", [P, KT, 2 * GH])
        w_ab_high = sb("w_ab_high", [P, KT, 2 * GH], F32R)
        w_ab_low = sb("w_ab_low", [P, KT, 2 * GH], F32R)
        eps_b = sb("eps_b", [P, 4])
        arena = sb("arena", [P, 44800])
        arena_at = nc.sbuf_base - 4 * 44800

        at = [MIX0]

        def take(n):
            at[0] += n
            return at[0] - n

        def view(off, n, rows=P):
            return arena[0:rows, off:off + n]

        def rounded(name, off, n):
            return nc.alloc_sbuf_tensor_at(name, [P, n], F32R, offset=arena_at + 4 * off)[:]

        o_R, o_K = take(1024), take(1024)
        o_V = take(1024)
        o_LO, o_LC, o_EP, o_EM, o_A = take(512), take(1032), take(1032), take(1032), take(1024)
        o_KK, o_AR, o_BH, o_KH, o_SQ, o_G = take(1024), take(2048), take(1024), take(1024), take(1024), take(1024)
        o_TV, o_TB, o_TK, o_QKV, o_KBQ = take(1024), take(512), take(512), take(3072), take(2048)
        o_Z, o_TVB, o_TKN, o_GB, o_GATES = take(1024), take(1024), take(512), take(512), take(4096)
        R3 = view(o_R, 1024).rearrange("p (t n) -> p t n", t=NT)
        K3_flat = view(o_K, 1024)
        K3 = view(o_K, 1024).rearrange("p (t n) -> p t n", t=NT)
        V3 = view(o_V, 1024).rearrange("p (t n) -> p t n", t=NT)
        LO = view(o_LO, 512)
        LC = view(o_LC, 1032).rearrange("p (q n) -> p q n", q=8)
        EP = view(o_EP, 1032).rearrange("p (q n) -> p q n", q=8)
        EM = view(o_EM, 1032).rearrange("p (q n) -> p q n", q=8)
        A3 = view(o_A, 1024).rearrange("p (t n) -> p t n", t=NT)
        KK = view(o_KK, 1024)
        AR = view(o_AR, 2048).rearrange("p (q s n) -> p q s n", q=8, s=2)
        BH = view(o_BH, 1024).rearrange("p (q n) -> p q n", q=8)
        KH = view(o_KH, 1024).rearrange("p (q n) -> p q n", q=8)
        SQ = view(o_SQ, 1024)
        G = view(o_G, 1024)
        TV = view(o_TV, 1024).rearrange("p (c n) -> p c n", c=2)
        TB = view(o_TB, 512)
        TK = view(o_TK, 512)
        QKV = view(o_QKV, 3072)
        Q1, K1, V1 = view(o_QKV, 1024), view(o_QKV + 1024, 1024), view(o_QKV + 2048, 1024)
        KBQ = view(o_KBQ, 2048).rearrange("p (q s n) -> p q s n", q=8, s=2)
        Z = view(o_Z, 1024)
        TVB = view(o_TVB, 1024).rearrange("p (c n) -> p c n", c=2)
        TKN = view(o_TKN, 512)
        GB = view(o_GB, 512, GH)
        GATES = view(o_GATES, 4096)
        KG = view(o_QKV, 512)
        QG = view(o_QKV + 512, 512)
        OG = V1
        BG = view(o_LC, 1024).rearrange("p (h n) -> p h n", h=GH)
        EG = view(o_A, 1024).rearrange("p (h n) -> p h n", h=GH)
        BB = view(o_EM, 1024).rearrange("p (h n) -> p h n", h=GH)
        DD = view(o_EP, 1024).rearrange("p (q n) -> p q n", q=8)
        DM = view(o_K, 2048).rearrange("p (q s n) -> p q s n", q=8, s=2)
        x_tok_in = view(o_QKV, 2048).rearrange("p (a n) -> p a n", a=2)
        YT = view(o_KBQ, 2048)
        XSQ = view(o_KBQ, 2048)
        RSTD = view(o_TVB, 256)
        small = sb("small", [P, 64])
        mid = small[:, 0:8]
        scol = small[:, 8:12]
        gcol = small[:, 12:20].rearrange("p (c h) -> p c h", c=2)
        kdec = small[:, 20:24]

        o = at[0]
        KSQ = view(o, 1024).rearrange("p (q n) -> p q n", q=4)
        g4 = view(o + 1024, 1280, GH).rearrange("p (i n) -> p i n", i=5)
        mix_norm_high = rounded("mix_norm_high", o + 2304, 2048).rearrange("p (k n) -> p k n", k=KT)
        mix_norm_low = nc.alloc_sbuf_tensor_at("mix_norm_low", [P, KT, T], F32R, offset=hT_at)[:]
        mix_high = [rounded(f"mix_high{i}", place_, SLAB) for i, place_ in enumerate((o_TV, o + 4352, o + 6400))]
        mix_low = [rounded(f"mix_low{i}", i * SLAB, SLAB) for i in range(MIX_RING)]

        MQ, MK, DG, DT, ZB, UB, SB = [], [], [], [], [], [], []
        for s in range(2):
            o = take(1024)
            MQ.append(view(o, 1024).rearrange("p (q n) -> p q n", q=4))
            o = take(1024)
            MK.append(view(o, 1024).rearrange("p (q n) -> p q n", q=4))
            o = take(1024)
            DG.append(view(o, 1024).rearrange("p (q n) -> p q n", q=4))
            o = take(512)
            DT.append(view(o, 512).rearrange("p (q n) -> p q n", q=4))
            o = take(256)
            ZB.append(view(o, 256).rearrange("p (q n) -> p q n", q=2))
            o = take(512)
            UB.append(view(o, 512).rearrange("p (q n) -> p q n", q=4))
            o = take(256)
            SB.append(view(o, 256).rearrange("p (q n) -> p q n", q=2))
        assert at[0] <= 44800, at[0]
        QSQ = view(o_TVB, 1024)

        at[0] = FFN_RING * SLAB
        low = [rounded(f"low{i}", i * SLAB, SLAB) for i in range(FFN_RING)]
        high = [rounded(f"high{i}", take(SLAB), SLAB) for i in range(HIGHS)]
        XSQ_ffn = view(at[0], 2048)
        RSTD_ffn = view(at[0] + 2048, 256)
        FG = view(take(2 * 512), 1024).rearrange("p (b n) -> p b n", b=2)
        FH = view(take(512), 512)
        FH_high = rounded("FH_high", take(1024), 1024).rearrange("p (b n) -> p b n", b=2)
        FH_low = rounded("FH_low", take(1024), 1024).rearrange("p (b n) -> p b n", b=2)
        o = take(4096)
        hT_high = rounded("hT_high", o, 2048).rearrange("p (k n) -> p k n", k=KT)
        hT_low = rounded("hT_low", o + 2048, 2048).rearrange("p (k n) -> p k n", k=KT)
        h_tok_high = rounded("h_tok_high", o, 2048).rearrange("p (a n) -> p a n", a=2)
        h_tok_low = rounded("h_tok_low", o + 2048, 2048).rearrange("p (a n) -> p a n", a=2)
        x_tok_out = view(o, 2048).rearrange("p (a n) -> p a n", a=2)
        x_tok = view(take(2048), 2048).rearrange("p (a n) -> p a n", a=2)
        XS_high = rounded("XS_high", take(1024), 1024).rearrange("p (k n) -> p k n", k=KT)
        XS_low = rounded("XS_low", take(1024), 1024).rearrange("p (k n) -> p k n", k=KT)
        PT = rounded("PT", take(256), 256).rearrange("p (a n) -> p a n", a=2)
        PTC = view(take(256), 256).rearrange("p (a n) -> p a n", a=2)
        PC = view(take(256), 256)
        YE = view(take(1024), 1024)
        w_router = view(take(64), 64).rearrange("p (k n) -> p k n", k=KT)
        rt = view(take(256), 256)
        logits = rt[:, 0:16].rearrange("p (a n) -> p a n", a=2)
        top = rt[:, 16:32].rearrange("p (a n) -> p a n", a=2)
        topi_f = rt[:, 32:48].rearrange("p (a n) -> p a n", a=2)
        hot1 = rt[:, 48:64].rearrange("p (a n) -> p a n", a=2)
        hot2 = rt[:, 64:80].rearrange("p (a n) -> p a n", a=2)
        chosen9 = rt[:, 144:162].rearrange("p (a n) -> p a n", a=2)
        pos9 = rt[:, 162:180].rearrange("p (a n) -> p a n", a=2)
        chosen, pos = chosen9[:, :, 0:NE], pos9[:, :, 0:NE]
        combine = rt[:, 96:112].rearrange("p (a n) -> p a n", a=2)
        g_diff, g_exp = rt[:, 128:130], rt[:, 130:132]
        g_first, g_second = rt[:, 132:134], rt[:, 134:136]
        most = rt[:, 136:137]
        xsum = rt[:, 138:140]
        topi = sb("topi", [P, 2, 8], U32)
        over = sb("over", [P, 1], I32)
        fin_g = view(take(1024), 1024)
        x_sq = XSQ_ffn.rearrange("p (a n) -> p a n", a=2)
        assert at[0] <= 44800, at[0]

        slab_in = [sem(f"slab_in{i}") for i in range(FFN_RING)]
        slab_done = sem("slab_done")
        consts_made = sem("consts_made")
        x_in = sem("x_in")
        rows_in = [sem(f"rows_in{L}") for L in range(DEPTH)]
        small_in = [sem(f"small_in{L}") for L in range(DEPTH)]
        head_in = sem("head_in")
        router_in = sem("router_in")
        fin_in = sem("fin_in")
        vec_turned, vec_kept = sem("vec_turned"), sem("vec_kept")
        x_turned, x_kept = sem("x_turned"), sem("x_kept")
        squared, summed, rooted, normed = sem("squared"), sem("summed"), sem("rooted"), sem("normed")
        proj_act, proj_dve = sem("proj_act"), sem("proj_dve")
        lora_acted, lora_done = sem("lora_acted"), sem("lora_done")
        decay_sig, rate_sig, gate_kept = sem("decay_sig"), sem("rate_sig"), sem("gate_kept")
        kk_made, kk_squared, kk_summed, kk_rooted = sem("kk_made"), sem("kk_squared"), sem("kk_summed"), sem("kk_rooted")
        log_decay, decays = sem("log_decay"), sem("decays")
        rw_ready, rk_ready, rk_summed, bonus_made = sem("rw_ready"), sem("rk_ready"), sem("rk_summed"), sem("bonus_made")
        silu_done, qk_squared, qk_summed = sem("silu_done"), sem("qk_squared"), sem("qk_summed")
        qk_rooted, qk_normed = sem("qk_rooted"), sem("qk_normed")
        ab_split = sem("ab_split")
        ab_done, ab_dve, ab_act = sem("ab_done"), sem("ab_dve"), sem("ab_act")
        spread, spread_kept, cols_turned, cols_kept = sem("spread"), sem("spread_kept"), sem("cols_turned"), sem("cols_kept")
        kdec_arg, kdec_made, dd_made, dd_exp = sem("kdec_arg"), sem("kdec_made"), sem("dd_made"), sem("dd_exp")
        vb_made, gdn_ready = sem("vb_made"), sem("gdn_ready")
        rw_turned, rw_kept = sem("rw_turned"), sem("rw_kept")
        gdn_turned, gdn_kept, gdn_keyed = sem("gdn_turned"), sem("gdn_kept"), sem("gdn_keyed")
        mat_done = [sem(f"mat_done{s}") for s in range(2)]
        mat_copied = [sem(f"mat_copied{s}") for s in range(2)]
        mat_summed = [sem(f"mat_summed{s}") for s in range(2)]
        hn_summed, hn_act, hn_dve = sem("hn_summed"), sem("hn_act"), sem("hn_dve")
        merged, mixed = sem("merged"), sem("mixed")
        slab_high, slab_split = sem("slab_high"), sem("slab_split")
        norm_high, norm_split = sem("norm_high"), sem("norm_split")
        ffn_act, ffn_dve, ffn_added = sem("ffn_act"), sem("ffn_dve"), sem("ffn_added")
        ffn_high, ffn_split = sem("ffn_high"), sem("ffn_split")
        tok_turned, tok_kept = sem("tok_turned"), sem("tok_kept")
        routed, logits_done, diff_made, exp_made, pos_done, over_made = (
            sem("routed"), sem("logits_done"), sem("diff_made"), sem("exp_made"), sem("pos_done"), sem("over_made"))
        hot_made, gathered, gather_kept = sem("hot_made"), sem("gathered"), sem("gather_kept")
        gather_split, weights_made = sem("gather_split"), sem("weights_made")
        hot_turned, hot_kept = sem("hot_turned"), sem("hot_kept")
        e_turned, e_high, e_split = sem("e_turned"), sem("e_high"), sem("e_split")
        e_act, e_dve, e_out, e_kept = sem("e_act"), sem("e_dve"), sem("e_out"), sem("e_kept")
        scattered, added = sem("scattered"), sem("added")
        zeroed, zero_put = sem("zeroed"), sem("zero_put")
        pos_moved = sem("pos_moved")
        moe_added, fin_sq, fin_root, fin_made, stored = (
            sem("moe_added"), sem("fin_sq"), sem("fin_root"), sem("fin_made"), sem("stored"))
        act_steps, dve_steps, pool_steps = sem("act_steps"), sem("dve_steps"), sem("pool_steps")

        first = {("mix", 0): 0, ("ffn", 0): N_MIX, ("mix", 1): N_MIX + N_FFN, ("moe", 1): 2 * N_MIX + N_FFN}
        place, landed, before = {}, {}, {}
        uses, last_user = [0] * FFN_RING, [None] * FFN_RING
        for phase, n, ring in ((("mix", 0), N_MIX, MIX_RING), (("ffn", 0), N_FFN, FFN_RING),
                               (("mix", 1), N_MIX, MIX_RING), (("moe", 1), N_FFN, FFN_RING)):
            for i in range(n):
                slot, s = i % ring, first[phase] + i
                uses[slot] += 1
                place[s], landed[s], before[s] = slot, 16 * uses[slot], last_user[slot]
                last_user[slot] = s
        E_LAPS = N_FFN // FFN_RING

        split_before = {("mix", 0): 0, ("ffn", 0): N_IN, ("mix", 1): N_IN + N_FFN, ("moe", 1): 2 * N_IN + N_FFN}

        def slab(slot):
            return arena[:, slot * SLAB:(slot + 1) * SLAB]

        def by_k(ap, n):
            return ap.rearrange("(k p) n -> p k n", p=P)

        def mix_source(L, i):
            if i < N_IN:
                return by_k(w_in[L, :, IN_SLABS[i]:IN_SLABS[i] + COLS], COLS), KT
            i -= N_IN
            if i < 4:
                w = (w_pb, w_pb, w_pa, w_pa)[i]
                return by_k(w[L, :, 512 * (i % 2):512 * (i % 2) + 512], 512), NT
            i -= 4
            return by_k(w_out[L, :, COLS * i:COLS * i + COLS], COLS), KT

        def ffn_source(wg, wu, wd, kind, j):
            if kind == "d":
                return by_k(wd[COLS * j:COLS * (j + 1), :], D), 2
            return by_k((wg if kind == "g" else wu)[:, COLS * j:COLS * (j + 1)], COLS), KT

        block = ctx.enter_context(nc.Block())

        @block.sync
        def _(sp):
            xv = x.rearrange("b (a p) d -> p (b a) d", p=P)
            sp.dma_start(x_tok_in, xv).then_inc(x_in, 16)

            def static(s, src, k):
                if before[s] is not None:
                    sp.wait_ge(slab_done, before[s] + 1)
                dst = slab(place[s]).rearrange("p (k n) -> p k n", k=k)
                sp.dma_start(dst, src).then_inc(slab_in[place[s]], 16)

            for L in range(DEPTH):
                for i in range(N_MIX):
                    static(first["mix", L] + i, *mix_source(L, i))
                if L == 0:
                    for i, (kind, j) in enumerate(FFN_ORDER):
                        if i == MIX_RING:
                            sp.wait_ge(mixed, 4 * (L + 1))
                        static(first["ffn", 0] + i, *ffn_source(ffn_w_gate[0], ffn_w_up[0], ffn_w_down[0], kind, j))

            def experts(lap):
                s0 = first["moe", 1]
                with sp.Fori(0, NE) as e:
                    for i, (kind, j) in enumerate(FFN_ORDER):
                        slot = i % FFN_RING
                        sp.wait_ge(slab_done, e * N_FFN + (s0 + lap * NE * N_FFN + i - FFN_RING + 1))
                        src, k = ffn_source(moe_w_gate[0, e], moe_w_up[0, e], moe_w_down[0, e], kind, j)
                        sp.dma_start(slab(slot).rearrange("p (k n) -> p k n", k=k), src).then_inc(slab_in[slot], 16)

            sp.wait_ge(mixed, 8)
            experts(0)
            sp.wait_ge(over_made, 1)
            more = sp.value_load(over[0:1, 0:1])
            with sp.If(more > 0):
                experts(1)

            sp.wait_ge(fin_made, 2)
            ov = out.rearrange("b (a p) d -> p (b a) d", p=P)
            sp.dma_start(ov, x_tok_out).then_inc(stored, 16)
            sp.wait_ge(stored, 16)

        @block.gpsimd
        def _(pool):
            step = Chain(pool, pool_steps)
            for t in (ident, ones, head_ones, later, later_neg, blocks16, sel, eps_b):
                step(nc.gpsimd.memset(t[:], 0.0 if t in (head_ones,) else 1.0))
            step(nc.gpsimd.memset(restart[:], 1.0))
            step(nc.gpsimd.iota(slots[:], pattern=[[1, P]], base=0, channel_multiplier=0,
                                allow_small_or_imprecise_dtypes=True))
            keep = nc.gpsimd.affine_select
            step(keep(out=ident[:], in_=ident[:], pattern=[[-1, P]], compare_op=ALU.is_equal, fill=0.0,
                           base=0, channel_multiplier=1))
            for tab, value in ((later, 1.0), (later_neg, -1.0)):
                step(nc.gpsimd.memset(tab[:, 0, :], value))
                step(keep(out=tab[:, 0, :], in_=tab[:, 0, :], pattern=[[1, P]], compare_op=ALU.is_gt, fill=0.0,
                               base=0, channel_multiplier=-1))
                step(keep(out=tab[:, 1, :], in_=tab[:, 1, :], pattern=[[1, P]], compare_op=ALU.is_ge, fill=0.0,
                               base=0, channel_multiplier=-1))
            b16 = blocks16[:].rearrange("p (b n) -> p b n", n=16)
            step(keep(out=b16, in_=b16, pattern=[[-16, 8], [0, 16]], compare_op=ALU.is_ge, fill=0.0,
                      base=0, channel_multiplier=1))
            step(keep(out=b16, in_=b16, pattern=[[16, 8], [0, 16]], compare_op=ALU.is_ge, fill=0.0,
                           base=15, channel_multiplier=-1))
            step(keep(out=sel[:], in_=sel[:], pattern=[[-1, GH], [0, P]], compare_op=ALU.is_equal, fill=0.0,
                           base=0, channel_multiplier=1))
            r3 = restart[:].rearrange("p (q n) -> p q n", q=8)
            step(nc.gpsimd.memset(r3[:, :, 0:1], 0.0))
            for hh in range(2):
                step(nc.gpsimd.memset(head_ones[64 * hh:64 * hh + 64, 64 * hh:64 * hh + 64], 1.0))
            for i, value in enumerate((NORM_EPS, P * 1e-6, GN_EPS, 1.0)):
                step(nc.gpsimd.memset(eps_b[:, i:i + 1], value))
            nc.gpsimd.memset(small[:], 0.0).then_inc(consts_made, 1)

            for L in range(DEPTH):
                if L:
                    pool.wait_ge(vec_turned, L)
                rows = [(V_MU, tshift_mu[L], 14), (V_W0, w0[L], 4), (V_A0, a0[L], 4), (V_KK, k_k[L], 4),
                        (V_KA, k_a[L], 4), (V_RK, r_k[L], 4), (V_LG, lnx_g[L], 4), (V_LB, lnx_b[L], 4),
                        (V_N1, norm1_g[L], 8), (V_N2, norm2_g[L], 8), (V_GN, gdn_norm_g[L], 1)]
                for r, src, n in rows:
                    pool.dma_start(vec_rows[r:r + n, :], src.rearrange("(t p) -> t p", p=P)).then_inc(rows_in[L], 16)
                pool.dma_start(vec_rows[V_CONV:V_CONV + 48, :],
                               conv_w[L].rearrange("j (t p) -> (j t) p", p=P)).then_inc(rows_in[L], 16)
                if L == 0:
                    for i, src in enumerate((a_log, dt_bias)):
                        for l in range(DEPTH):
                            pool.dma_start(head_raw[:, i, l:l + 1],
                                           src[l].rearrange("(h a) -> h a", a=1)).then_inc(head_in, 16)
                else:
                    pool.wait_ge(lora_done, 3 * L)
                    pool.wait_ge(ab_split, 2 * L)
                pool.dma_start(lora_up[0:64, :], w_decay_up[L]).then_inc(small_in[L], 16)
                pool.dma_start(lora_up[64:128, :], w_iclr_up[L]).then_inc(small_in[L], 16)
                pool.dma_start(gate_up[:], w_gate_up[L]).then_inc(small_in[L], 16)
                pool.dma_start(w_ab[:], by_k(w_in[L, :, AB_BASE:AB_BASE + 2 * GH], 2 * GH)).then_inc(small_in[L], 16)
            pool.wait_ge(mixed, 8)
            pool.dma_start(w_router, by_k(moe_router[0], NE)).then_inc(router_in, 16)
            pool.dma_start(fin_g, final_g.rearrange("(a n) -> a n", a=1).broadcast_to([P, D])).then_inc(fin_in, 16)

        @block.tensor
        def _(pe):
            def mm(out, lhsT, rhs, start=True, stop=True, **kw):
                return nc.tensor.matmul(out, lhsT, rhs, start=start, stop=stop, **kw)

            def turn(out, src):
                n = src.shape[0]
                return nc.tensor.transpose(out, src, ident[0:n, 0:n])

            def arrived(s):
                pe.wait_ge(slab_in[place[s]], landed[s])
                return slab(place[s])

            def split_mm(out, w_high, w_low, x_high, x_low, start=True, stop=True, **kw):
                mm(out, w_high, x_high, start, False, **kw)
                mm(out, w_high, x_low, False, False, **kw)
                return mm(out, w_low, x_high, False, stop, **kw)

            def norm(n):
                pe.wait_ge(squared, n + 1)
                squares = XSQ_ffn if n % 2 else XSQ
                for k in range(KT):
                    last = mm(ps[:, 7, 0:T], ones[:], squares[:, k * T:(k + 1) * T], k == 0, k == KT - 1)
                last.then_inc(summed, 1)
                if n == 3:
                    pe.wait_ge(normed, n + 1)

            def in_slab(L, o):
                if o >= 4:
                    if o - 4 < N_CONV:
                        pe.wait_ge(proj_dve, N_CONV * L + o - 3)
                    else:
                        pe.wait_ge(proj_act, N_IN * L + o - 3)
                pe.wait_ge(slab_split, split_before["mix", L] + o + 1)
                wh, wl = (w.rearrange("p (k n) -> p k n", k=KT) for w in (mix_high[o % 3], mix_low[o % 3]))
                for m in range(2):
                    cut = slice(m * P, (m + 1) * P)
                    for k in range(KT):
                        if o == 0 and m == 0 and k % 4 == 0:
                            pe.wait_ge(norm_split, 4 * L + k // 4 + 1)
                        last = split_mm(ps[:, o % 4, m * T:(m + 1) * T], wh[:, k, cut], wl[:, k, cut],
                                        mix_norm_high[:, k, :], mix_norm_low[:, k, :], k == 0, k == KT - 1)
                last.then_inc(slab_done, 1)

            def head_sums(table, src, bank):
                for i in range(2):
                    last = mm(ps[:, bank + i, :], table[:], src[:, i * 512:(i + 1) * 512])
                return last

            def project(L):
                norm(2 * L)
                pe.wait_ge(small_in[L], 64)
                for o in range(9):
                    in_slab(L, o)
                pe.wait_ge(lora_acted, 2 * (L + 1))
                for lo, bank in ((0, 4), (64, 6)):
                    for t in range(NT):
                        last = mm(ps[:, bank + t // 2, (t % 2) * T:(t % 2 + 1) * T],
                                  lora_up[lo:lo + 64, t * P:(t + 1) * P], LO[lo:lo + 64, 0:T])
                    last.then_inc(lora_done, 1)
                in_slab(L, 9)
                in_slab(L, 10)
                pe.wait_ge(kk_squared, L + 1)
                pe.wait_ge(decay_sig, L + 1)
                head_sums(head_ones, SQ, 4).then_inc(kk_summed, 1)
                in_slab(L, 11)
                in_slab(L, 12)
                pe.wait_ge(rate_sig, L + 1)
                for t in range(NT):
                    last = mm(ps[:, 6 + t // 2, (t % 2) * T:(t % 2 + 1) * T],
                              gate_up[:, t * P:(t + 1) * P], LO[:, T:2 * T])
                last.then_inc(lora_done, 1)
                pe.wait_ge(kk_rooted, L + 1)
                pe.wait_ge(ab_split, 2 * (L + 1))
                for i in range(2):
                    for k in range(KT):
                        last = split_mm(ps[0:GH, 4, i * T:(i + 1) * T], w_ab_high[:, k, i * GH:(i + 1) * GH],
                                        w_ab_low[:, k, i * GH:(i + 1) * GH], mix_norm_high[:, k, :],
                                        mix_norm_low[:, k, :], k == 0, k == KT - 1)
                last.then_inc(ab_done, 1)
                for o in range(13, 17):
                    in_slab(L, o)
                pe.wait_ge(rk_ready, L + 1)
                pe.wait_ge(gate_kept, L + 1)
                head_sums(head_ones, SQ, 6).then_inc(rk_summed, 1)
                in_slab(L, 17)
                pe.wait_ge(qk_squared, 2 * L + 1)
                pe.wait_ge(ab_act, 3 * L + 3)
                pe.wait_ge(ab_dve, 3 * L + 1)
                head_sums(ones, QSQ, 4).then_inc(qk_summed, 1)
                in_slab(L, 18)
                pe.wait_ge(qk_squared, 2 * L + 2)
                pe.wait_ge(bonus_made, L + 1)
                for i in range(2):
                    last = mm(ps[:, 6 + i, :], ones[:], KSQ[:, 2 * i:2 * i + 2, :])
                last.then_inc(qk_summed, 1)
                in_slab(L, 19)
                in_slab(L, 20)
                pe.wait_ge(qk_rooted, 2 * L + 2)
                pe.wait_ge(ab_dve, 3 * L + 3)
                for h in range(GH):
                    last = mm(ps[:, 4 + h, :], sel[:, h, :], GB)
                last.then_inc(spread, 1)
                in_slab(L, 21)
                in_slab(L, 22)
                pe.wait_ge(spread_kept, L + 1)
                for c in range(2):
                    last = mm(ps[:, 4, c * GH:(c + 1) * GH], GB[:, c * P:(c + 1) * P], ident[0:GH, 0:GH])
                last.then_inc(cols_turned, 1)

            def turn_tokens(L):
                pe.wait_ge(proj_act, N_IN * (L + 1))
                pe.wait_ge(rw_ready, L + 1)
                for c in range(2):
                    for t in range(NT):
                        turn(ps[:, c, t * P:(t + 1) * P], V3[:, t, c * P:(c + 1) * P])
                for bank, src in ((2, BH), (3, KH)):
                    for t in range(NT):
                        last = turn(ps[:, bank, t * P:(t + 1) * P], src[:, 2 * t, :])
                last.then_inc(rw_turned, 1)
                pe.wait_ge(vb_made, L + 1)
                for c in range(2):
                    for h in range(GH):
                        turn(ps[:, 5 + c, h * P:(h + 1) * P], V1[:, h * T + c * P:h * T + (c + 1) * P])
                for h in range(GH):
                    last = turn(ps[:, 7, h * P:(h + 1) * P], K1[:, h * T:h * T + P])
                last.then_inc(gdn_turned, 1)
                pe.wait_ge(rw_kept, L + 1)
                pe.wait_ge(gdn_kept, L + 1)
                pe.wait_ge(gdn_keyed, L + 1)
                pe.wait_ge(cols_kept, L + 1)
                pe.wait_ge(gdn_ready, L + 1)

            def groups(L):
                for pair in range(3):
                    rw = pair < 2
                    base = L * (2 * len(R_STEPS) + len(G_STEPS)) + pair * len(R_STEPS)
                    cbase = L * (2 * len(R_COPIES) + len(G_COPIES)) + pair * len(R_COPIES)
                    sbase = L * (2 * len(R_SUMS) + len(G_SUMS)) + pair * len(R_SUMS)
                    copies, sums = (RC_AT, RS_AT) if rw else (GC_AT, GS_AT)

                    def copied(s, what):
                        pe.wait_ge(mat_copied[s], cbase + copies[what])

                    def summed_(s, what):
                        pe.wait_ge(mat_summed[s], sbase + sums[what])

                    def products(s, bank, lhs, rhs):
                        for q in range(4):
                            last = mm(ps[:, 4 * s + bank, q * P:(q + 1) * P], lhs(q), rhs(q))
                        return last

                    def doubling(s, left, add):
                        A = lambda q: DG[s][:, q, 0:P]
                        At = lambda q: DT[s][:, q, :]
                        Gm = lambda q: DG[s][:, q, P:2 * P]
                        if left:
                            products(s, 1, At, A)
                            last = products(s, 2, A, At)
                        if add:
                            last = products(s, 3, At, Gm)
                        last.then_inc(mat_done[s], 1)

                    for s in range(2):
                        g = 2 * pair + s
                        if pair:
                            pbase = sbase - (len(R_SUMS))
                            pe.wait_ge(mat_summed[s], pbase + RS_AT["o"])
                        for q in range(4):
                            hh, c = q // 2, q % 2
                            dst = ps[:, 4 * s + q // 2, (q % 2) * T:(q % 2 + 1) * T]
                            if rw:
                                r = slice(64 * hh, 64 * hh + 64)
                                last = mm(dst, BH[r, 2 * g + c, :], AR[r, 2 * g + c, :, :])
                                last = mm(ps[:, 4 * s + 2 + q // 2, (q % 2) * T:(q % 2 + 1) * T],
                                          KH[r, 2 * g + c, :], AR[r, 2 * g + c, :, :])
                            else:
                                h = 2 * (g - 4) + hh
                                last = mm(dst, K1[:, h * T + c * P:h * T + (c + 1) * P], KBQ[:, 2 * h + c, :, :])
                        last.then_inc(mat_done[s], 1)
                    for s in range(2):
                        summed_(s, "d")
                        for q in range(4):
                            last = turn(ps[:, 4 * s, q * P:(q + 1) * P], DG[s][:, q, 0:P])
                        last.then_inc(mat_done[s], 1)
                    for s in range(2):
                        copied(s, "dT")
                        summed_(s, "masked")
                        doubling(s, True, False)
                    for s in range(2):
                        copied(s, "sqT")
                        doubling(s, True, True)
                    for s in range(2):
                        copied(s, "gen1T")
                        summed_(s, "gen1")
                        doubling(s, True, True)
                    for s in range(2):
                        copied(s, "gen2T")
                        summed_(s, "gen2")
                        doubling(s, False, True)
                    for s in range(2):
                        summed_(s, "last1")
                        for q in range(4):
                            last = turn(ps[:, 4 * s, q * P:(q + 1) * P], DG[s][:, q, P:2 * P])
                        last.then_inc(mat_done[s], 1)
                    for s in range(2):
                        copied(s, "gT")
                        products(s, 1, lambda q: DT[s][:, q, :], lambda q: MQ[s][:, q, 0:P])
                        products(s, 2, lambda q: MQ[s][:, q, 0:P], lambda q: DT[s][:, q, :]).then_inc(mat_done[s], 1)
                    for s in range(2):
                        copied(s, "mT")
                        doubling(s, True, True)
                    for s in range(2):
                        copied(s, "gen3T")
                        summed_(s, "gen3")
                        doubling(s, True, True)
                    for s in range(2):
                        copied(s, "gen4T")
                        summed_(s, "gen4")
                        doubling(s, False, True)

                    def heads(s):
                        g = 2 * pair + s
                        for hh in range(2):
                            if rw:
                                yield hh, slice(g * P + HD * hh, g * P + HD * (hh + 1)), slice(HD * hh, HD * (hh + 1)), HD
                            else:
                                h = 2 * (g - 4) + hh
                                yield hh, slice(h * P, (h + 1) * P), slice(0, P), P

                    def solve(s, c, rhs, what):
                        for hh, cols, rows, n in heads(s):
                            last = mm(ps[:, 4 * s + 1, hh * P:hh * P + n], DG[s][:, 2 * hh + c, P:2 * P], rhs(hh, cols, n))
                        last.then_inc(mat_done[s], 1)

                    if rw:
                        for s in range(2):
                            for hh, cols, rows, n in heads(s):
                                last = mm(ps[:, 4 * s + 2 * hh, 0:n], MK[s][:, 2 * hh, 0:P], TV[:, 0, cols])
                            last.then_inc(mat_done[s], 1)
                    for s in range(2):
                        summed_(s, "last2")
                        if rw:
                            copied(s, "z0")
                            solve(s, 0, lambda hh, cols, n: ZB[s][:, hh, 0:n], "u0")
                        else:
                            solve(s, 0, lambda hh, cols, n: TVB[:, 0, cols], "u0")
                    for s in range(2):
                        copied(s, "u0")
                        for hh, cols, rows, n in heads(s):
                            if rw:
                                dst = ps[rows, 4 * s + 2, 0:n]
                                mm(dst, TB[:, cols], UB[s][:, 2 * hh, 0:n], True, False)
                                last = mm(dst, TK[:, cols], TV[:, 0, cols], False, True)
                            else:
                                last = mm(ps[:, 4 * s + 2, hh * P:(hh + 1) * P], TKN[:, cols], UB[s][:, 2 * hh, :])
                        last.then_inc(mat_done[s], 1)
                    for s in range(2):
                        g = 2 * pair + s
                        copied(s, "s")
                        for hh, cols, rows, n in heads(s):
                            dst = ps[:, 4 * s + 2 * hh, 0:n] if rw else ps[:, 4 * s, hh * P:hh * P + n]
                            if rw:
                                mm(dst, AR[rows, 2 * g + 1, 0, :], SB[s][rows, 0, 0:n], True, False)
                                last = mm(dst, MK[s][:, 2 * hh + 1, 0:P], TV[:, 1, cols], False, True)
                            else:
                                last = mm(dst, KG[:, cols], SB[s][:, hh, :])
                        last.then_inc(mat_done[s], 1)
                    for s in range(2):
                        if rw:
                            copied(s, "z1")
                        else:
                            summed_(s, "z1")
                        solve(s, 1, lambda hh, cols, n: ZB[s][:, hh, 0:n], "u1")
                    for s in range(2):
                        g = 2 * pair + s
                        copied(s, "u1")
                        for hh, cols, rows, n in heads(s):
                            for c in range(2):
                                q = 2 * hh + c
                                dst = ps[rows, 4 * s + 3, c * P:(c + 1) * P] if rw else \
                                    ps[:, 4 * s + 3, q * P:(q + 1) * P]
                                mm(dst, UB[s][:, q, 0:n], MQ[s][:, q, P:2 * P], True, not rw and c == 0)
                                if rw:
                                    mm(dst, TV[:, c, cols], MK[s][:, q, P:2 * P], False, c == 0)
                                if c == 1:
                                    if rw:
                                        last = mm(dst, SB[s][rows, 0, 0:n], AR[rows, 2 * g + 1, 1, :], False, True)
                                    else:
                                        last = mm(dst, SB[s][:, hh, :], QG[:, cols], False, True)
                        last.then_inc(mat_done[s], 1)

            def finish_mixer(L):
                ends = [(L + 1) * (2 * len(R_SUMS) + len(G_SUMS))] * 2
                for s in range(2):
                    pe.wait_ge(mat_summed[s], ends[s])
                head_sums(head_ones, KK, 0).then_inc(hn_summed, 1)
                pe.wait_ge(hn_act, 4 * L + 1)
                head_sums(ones, QSQ, 4).then_inc(hn_summed, 1)
                pe.wait_ge(hn_act, 4 * L + 3)
                head_sums(head_ones, SQ, 2).then_inc(hn_summed, 1)
                pe.wait_ge(hn_dve, 3 * L + 2)
                for i, src, bank in ((0, OG, 4), (1, OG, 6), (2, KK, 0), (3, KK, 2)):
                    w = arrived(first["mix", L] + N_IN + i).rearrange("p (k n) -> p k n", k=NT)
                    if i == 2:
                        pe.wait_ge(hn_dve, 3 * L + 3)
                    for m in range(4):
                        for k in range(NT):
                            last = mm(ps[:, bank + m // 2, (m % 2) * T:(m % 2 + 1) * T], w[:, k, m * P:(m + 1) * P],
                                      src[:, k * T:(k + 1) * T], k == 0, k == NT - 1)
                    last.then_inc(slab_done, 1)
                pe.wait_ge(merged, L + 1)
                for j in range(4):
                    w = arrived(first["mix", L] + N_IN + 4 + j).rearrange("p (k n) -> p k n", k=KT)
                    for m in range(2):
                        for k in range(KT):
                            last = mm(ps[:, j, m * T:(m + 1) * T], w[:, k, m * P:(m + 1) * P],
                                      YT[:, k * T:(k + 1) * T], k == 0, k == KT - 1)
                    last.then_inc(slab_done, 1)

            def dense(L):
                norm(2 * L + 1)
                s0 = first["ffn", L]
                for i, (kind, j) in enumerate(FFN_ORDER):
                    pe.wait_ge(slab_split, split_before["ffn", L] + i + 1)
                    wh, wl = high[i % HIGHS], low[i % FFN_RING]
                    if kind in "gu":
                        if j >= 2:
                            pe.wait_ge(ffn_dve, j - 1)
                        wh, wl = (w.rearrange("p (k n) -> p k n", k=KT) for w in (wh, wl))
                        for m in range(2):
                            cut = slice(m * P, (m + 1) * P)
                            for k in range(KT):
                                if i == 0 and m == 0 and k % 4 == 0:
                                    pe.wait_ge(norm_split, 4 * L + 2 + k // 4 + 1)
                                last = split_mm(ps[:, 2 * (j % 2) + (kind == "u"), m * T:(m + 1) * T],
                                                wh[:, k, cut], wl[:, k, cut], hT_high[:, k, :], hT_low[:, k, :],
                                                k == 0, k == KT - 1)
                    else:
                        pe.wait_ge(ffn_split, j + 1)
                        wh, wl = (w.rearrange("p (k n) -> p k n", k=2) for w in (wh, wl))
                        for m in range(KT):
                            cut = slice(m * P, (m + 1) * P)
                            for k in range(2):
                                tok = slice(k * T, (k + 1) * T)
                                last = split_mm(ps[:, 4 + m // 2, (m % 2) * T:(m % 2 + 1) * T],
                                                wh[:, k, cut], wl[:, k, cut], FH_high[:, j % 2, tok], FH_low[:, j % 2, tok],
                                                j == 0 and k == 0 and m % 2 == 0,
                                                j == FC - 1 and k == 1, skip_group_check=True)
                    last.then_inc(slab_done, 1)

            def gather():
                for k in range(KT):
                    for a in range(2):
                        for part in (h_tok_high, h_tok_low):
                            first_, last_ = a == 0 and part is h_tok_high, a == 1 and part is h_tok_low
                            last = mm(ps[:, k // 4, (k % 4) * P:(k % 4 + 1) * P],
                                      part[:, a, k * P:(k + 1) * P], PT[:, a, :], first_, last_)
                last.then_inc(gathered, 1)

            def scatter():
                for a in range(2):
                    for n in range(2):
                        last = mm(ps[:, 4 + 2 * a + n, :], PC[:, a * P:(a + 1) * P], YE[:, n * 512:(n + 1) * 512])
                    last.then_inc(scattered, 1)

            def turn_h(j):
                for m in range(2):
                    last = turn(ps[:, 6 + j % 2, m * P:(m + 1) * P], FH[:, m * P:(m + 1) * P])
                last.then_inc(e_turned, 1)

            def experts(lap):
                s0 = first["moe", 1] + lap * NE * N_FFN
                pe.wait_ge(hot_made, lap * (NE + 1) + 1)
                gather()
                pe.wait_ge(zeroed, lap + 1)
                for n in range(2):
                    last = mm(ps[:, 2 + n, :], ones[:], YE[:, n * 512:(n + 1) * 512])
                last.then_inc(zero_put, 1)
                with pe.Fori(0, NE) as e:
                    n_e = e + lap * NE
                    chunks = e * FC + lap * NE * FC
                    pe.wait_ge(gather_split, e + (lap * (NE + 1) + 1))
                    for i, (kind, j) in enumerate(FFN_ORDER):
                        if (kind, j) == ("u", 0):
                            pe.wait_ge(e_kept, e + (lap * (NE + 1) + 1))
                            scatter()
                            pe.wait_ge(added, 2 * e + (2 * lap * (NE + 1) + 1))
                        elif kind == "u":
                            if j == 1:
                                pe.wait_ge(weights_made, n_e + 1)
                                pe.wait_ge(added, 2 * e + (2 * lap * (NE + 1) + 2))
                                for a in range(2):
                                    last = turn(ps[:, 7, a * P:(a + 1) * P], PTC[:, a, :])
                                last.then_inc(hot_turned, 1)
                            if j == 2:
                                pe.wait_ge(hot_kept, n_e + 1)
                            pe.wait_ge(e_dve, chunks + j)
                            turn_h(j - 1)
                        elif (kind, j) == ("d", FC - 2):
                            pe.wait_ge(hot_made, e + (lap * (NE + 1) + 2))
                            pe.wait_ge(e_act, chunks + FC)
                            gather()
                            pe.wait_ge(e_dve, chunks + FC)
                            turn_h(FC - 1)
                        pe.wait_ge(slab_split, e * N_FFN + (split_before["moe", 1] + lap * NE * N_FFN + i + 1))
                        wh, wl = high[i % HIGHS], low[i % FFN_RING]
                        if kind in "gu":
                            if kind == "g" and j >= 2:
                                pe.wait_ge(e_dve, chunks + (j - 1))
                            wh, wl = (w.rearrange("p (k n) -> p k n", k=KT) for w in (wh, wl))
                            for k in range(KT):
                                last = split_mm(ps[:, j % 2 + 4 * (kind == "u"), 0:COLS],
                                                XS_high[:, k, :], XS_low[:, k, :], wh[:, k, :], wl[:, k, :],
                                                k == 0, k == KT - 1)
                        else:
                            pe.wait_ge(e_split, chunks + (j + 1))
                            wh, wl = (w.rearrange("p (k n) -> p k n", k=2) for w in (wh, wl))
                            for k in range(2):
                                hcut = slice(k * P, (k + 1) * P)
                                for n in range(2):
                                    cut = slice(n * 512, (n + 1) * 512)
                                    last = split_mm(ps[:, 2 + n, :], FH_high[:, j % 2, hcut], FH_low[:, j % 2, hcut],
                                                    wh[:, k, cut], wl[:, k, cut],
                                                    j == 0 and k == 0, j == FC - 1 and k == 1)
                        last.then_inc(slab_done, 1)
                pe.wait_ge(e_kept, (lap + 1) * (NE + 1))
                scatter()

            pe.wait_ge(consts_made, 1)
            pe.wait_ge(x_in, 16)
            for k in range(KT):
                for a in range(2):
                    last = turn(ps[:, k // 2, (k % 2) * T + a * P:(k % 2) * T + (a + 1) * P],
                                x_tok_in[:, a, k * P:(k + 1) * P])
            last.then_inc(x_turned, 1)
            for L in range(DEPTH):
                pe.wait_ge(rows_in[L], 16 * 12)
                turn(ps[:, VEC_BANK[L], 0:N_VEC], vec_rows[0:N_VEC, :]).then_inc(vec_turned, 1)
                project(L)
                turn_tokens(L)
                groups(L)
                finish_mixer(L)
                if L == 0:
                    dense(L)
            norm(3)
            for i, src in enumerate((hT, xT)):
                for k in range(KT):
                    for a in range(2):
                        last = turn(ps[:, 4 * i + 2 * a + k // 4, (k % 4) * P:(k % 4 + 1) * P],
                                    src[:, k, a * P:(a + 1) * P])
                last.then_inc(tok_turned, 1)
            pe.wait_ge(tok_kept, 2)
            pe.wait_ge(norm_split, 7)
            pe.wait_ge(router_in, 16)
            for a in range(2):
                for k in range(KT):
                    last = mm(ps[:, 0, a * NE:(a + 1) * NE], hT[:, k, a * P:(a + 1) * P], w_router[:, k, :],
                              k == 0, k == KT - 1)
            last.then_inc(logits_done, 1)
            pe.wait_ge(routed, 1)
            mm(ps[:, 1, 0:NE], later[:, 0, :], chosen[:, 0, :])
            mm(ps[:, 1, NE:2 * NE], later[:, 0, :], chosen[:, 1, :], True, False)
            mm(ps[:, 1, NE:2 * NE], ones[:], chosen[:, 0, :], False, True)
            mm(ps[:, 1, 2 * NE:3 * NE], ones[:], chosen[:, 0, :], True, False)
            mm(ps[:, 1, 2 * NE:3 * NE], ones[:], chosen[:, 1, :], False, True).then_inc(pos_done, 1)
            experts(0)
            pe.wait_ge(over_made, 1)
            more = pe.value_load(over[0:1, 0:1])
            with pe.If(more > 0):
                experts(1)

        def banks(a, n):
            return ps[:, a:a + (n + 511) // 512, :].rearrange("p b n -> p (b n)")[:, 0:n]

        def group_bases(L, pair):
            return (L * (2 * len(R_STEPS) + len(G_STEPS)) + pair * len(R_STEPS),
                    L * (2 * len(R_COPIES) + len(G_COPIES)) + pair * len(R_COPIES),
                    L * (2 * len(R_SUMS) + len(G_SUMS)) + pair * len(R_SUMS))

        @block.scalar
        def _(act):
            step = Chain(act, act_steps)
            run = nc.scalar.activation

            def norm(n):
                run(XSQ_ffn if n % 2 else XSQ, xT[:].rearrange("p k n -> p (k n)"), ACT.Square).then_inc(squared, 1)
                act.wait_ge(summed, n + 1)
                run(RSTD_ffn if n % 2 else RSTD, ps[:, 7, 0:T], ACT.Sqrt, bias=eps_b[:, 0:1], scale=1.0 / D).then_inc(rooted, 1)

            def high_norm():
                for half in range(2):
                    cut = slice(4 * half, 4 * half + 4)
                    run(mix_norm_high[:, cut, :], hT[:, cut, :], ACT.Copy).then_inc(norm_high, 1)

            def high_in(L, i):
                s = first["mix", L] + i
                act.wait_ge(slab_in[place[s]], landed[s])
                if i >= 3:
                    act.wait_ge(slab_done, s - 3 + 1)
                run(mix_high[i % 3], slab(place[s]), ACT.Copy).then_inc(slab_high, 1)

            def in_slab(L, o):
                act.wait_ge(slab_done, first["mix", L] + o + 1)
                src = ps[:, o % 4, :]
                if o < N_CONV:
                    for m in range(2):
                        if o < 7:
                            t = IN_SLABS[o] // P + m
                            dst, scale = shifted(t), one_less_mu[:, L, t:t + 1]
                        else:
                            i = 2 * (o - 7) + m
                            dst, scale = QKV[:, i * T:(i + 1) * T], vec[:, L, V_CONV + 36 + i:V_CONV + 37 + i]
                        last = run(dst, src[:, m * T:(m + 1) * T], ACT.Copy, scale=scale)
                elif o < 15:
                    last = run(Z[:, (o - 13) * 512:(o - 12) * 512], src, ACT.Silu)
                else:
                    last = run(GATES[:, (o - 15) * 512:(o - 14) * 512], src, ACT.Sigmoid)
                last.then_inc(proj_act, 1)
                if o + 3 < N_IN:
                    high_in(L, o + 3)

            def project(L):
                norm(2 * L)
                high_in(L, 0)
                act.wait_ge(normed, 2 * L + 1)
                high_norm()
                high_in(L, 1)
                high_in(L, 2)
                act.wait_ge(small_in[L], 64)
                run(w_ab_high[:], w_ab[:], ACT.Copy).then_inc(ab_split, 1)
                for o in range(3):
                    in_slab(L, o)
                act.wait_ge(proj_dve, N_CONV * L + 1)
                run(LO[0:64, 0:T], LO[0:64, 0:T], ACT.Tanh).then_inc(lora_acted, 1)
                run(LO[:, T:2 * T], LO[:, T:2 * T], ACT.Sigmoid).then_inc(lora_acted, 1)
                for o in range(3, 9):
                    in_slab(L, o)
                act.wait_ge(lora_done, 3 * L + 1)
                for t in range(NT):
                    src = ps[:, 4 + t // 2, (t % 2) * T:(t % 2 + 1) * T].rearrange("p (c n) -> p c n", c=2)
                    last = run(LC[:, 2 * t:2 * t + 2, 1:129], src, ACT.Sigmoid, bias=vec[:, L, V_W0 + t:V_W0 + t + 1])
                last.then_inc(decay_sig, 1)
                act.wait_ge(lora_done, 3 * L + 2)
                for t in range(NT):
                    last = run(A3[:, t, :], ps[:, 6 + t // 2, (t % 2) * T:(t % 2 + 1) * T], ACT.Sigmoid,
                               bias=vec[:, L, V_A0 + t:V_A0 + t + 1])
                last.then_inc(rate_sig, 1)
                act.wait_ge(kk_made, L + 1)
                run(SQ, KK, ACT.Square).then_inc(kk_squared, 1)
                in_slab(L, 9)
                in_slab(L, 10)
                act.wait_ge(log_decay, L + 1)
                run(view(o_EP, 1032), view(o_LC, 1032), ACT.Exp, scale=-DECAY_C).then_inc(decays, 1)
                run(view(o_EM, 1032), view(o_LC, 1032), ACT.Exp, scale=DECAY_C).then_inc(decays, 1)
                act.wait_ge(kk_summed, L + 1)
                run(SQ, banks(4, 1024), ACT.Sqrt, bias=eps_b[:, 0:1]).then_inc(kk_rooted, 1)
                in_slab(L, 11)
                in_slab(L, 12)
                act.wait_ge(lora_done, 3 * L + 3)
                run(G, banks(6, 1024), ACT.Copy).then_inc(gate_kept, 1)
                in_slab(L, 13)
                act.wait_ge(proj_dve, N_CONV * (L + 1))
                for i in range(3):
                    last = run(QKV[:, i * 1024:(i + 1) * 1024], QKV[:, i * 1024:(i + 1) * 1024], ACT.Silu)
                    last.then_inc(silu_done, 1)
                in_slab(L, 14)
                act.wait_ge(ab_dve, 3 * L + 1)
                step(run(g4[:, 1, :], g4[:, 0, :], ACT.Abs))
                run(g4[:, 1, :], g4[:, 1, :], ACT.Exp, scale=-1.0).then_inc(ab_act, 1)
                act.wait_ge(ab_dve, 3 * L + 2)
                run(g4[:, 3, :], g4[:, 2, :], ACT.Ln).then_inc(ab_act, 1)
                run(GB[:, T:2 * T], ps[0:GH, 4, T:2 * T], ACT.Sigmoid).then_inc(ab_act, 1)
                act.wait_ge(silu_done, 3 * L + 2)
                run(QSQ, Q1, ACT.Square).then_inc(qk_squared, 1)
                run(KSQ, K1.rearrange("p (q n) -> p q n", q=4), ACT.Square).then_inc(qk_squared, 1)
                in_slab(L, 15)
                in_slab(L, 16)
                in_slab(L, 17)
                act.wait_ge(qk_summed, 2 * L + 1)
                run(QSQ, banks(4, 1024), ACT.Sqrt, bias=eps_b[:, 1:2], scale=float(P)).then_inc(qk_rooted, 1)
                in_slab(L, 18)
                act.wait_ge(qk_summed, 2 * L + 2)
                run(KSQ.rearrange("p q n -> p (q n)"), banks(6, 1024), ACT.Sqrt,
                    bias=eps_b[:, 0:1]).then_inc(qk_rooted, 1)
                in_slab(L, 19)
                in_slab(L, 20)
                act.wait_ge(spread, L + 1)
                act.wait_ge(rw_ready, L + 1)
                step(run(BG, ps[:, 4:8, 0:T], ACT.Copy))
                run(BB, ps[:, 4:8, T:2 * T], ACT.Copy).then_inc(spread_kept, 1)
                in_slab(L, 21)
                in_slab(L, 22)
                run(EG, BG, ACT.Exp).then_inc(kdec_made, 1)
                act.wait_ge(kdec_arg, L + 1)
                run(kdec, kdec, ACT.Exp).then_inc(kdec_made, 1)
                act.wait_ge(dd_made, L + 1)
                run(DD, DD, ACT.Exp).then_inc(dd_exp, 1)

            def turn_tokens(L):
                act.wait_ge(rw_turned, L + 1)
                run(TV, ps[:, 0:2, :], ACT.Copy)
                run(TB, ps[:, 2, :], ACT.Copy)
                run(TK, ps[:, 3, :], ACT.Copy).then_inc(rw_kept, 1)
                act.wait_ge(gdn_turned, L + 1)
                run(TVB, ps[:, 5:7, :], ACT.Copy).then_inc(gdn_kept, 1)

            def groups(L):
                for pair in range(3):
                    rw = pair < 2
                    base, _, _ = group_bases(L, pair)
                    steps = R_AT if rw else G_AT

                    def copy(s, what, dst, src, scale=None):
                        act.wait_ge(mat_done[s], base + steps[what])
                        if scale is None:
                            run(dst, src, ACT.Copy).then_inc(mat_copied[s], 1)
                        else:
                            run(dst, src, ACT.Copy, scale=scale).then_inc(mat_copied[s], 1)

                    def bank(s, b):
                        return ps[:, 4 * s + b, :].rearrange("p (q n) -> p q n", q=4)

                    def turned(s, what):
                        copy(s, what, DT[s], bank(s, 0))

                    def both(s, what):
                        copy(s, what, DG[s][:, :, 0:P], bank(s, 1))
                        copy(s, what, DT[s], bank(s, 2))

                    for what in ("dT", "sq", "gen1", "gen2", "gT", "m", "gen3", "gen4"):
                        for s in range(2):
                            (turned if what in ("dT", "gT") else both)(s, what)
                    n = HD if rw else P

                    def narrow(s, b):
                        return ps[:, 4 * s + b, 0:2 * P].rearrange("p (q n) -> p q n", q=2)[:, :, 0:n]

                    if rw:
                        for s in range(2):
                            copy(s, "z0", ZB[s][:, :, 0:n], ps[:, 4 * s:4 * s + 3:2, 0:n])
                    for s in range(2):
                        copy(s, "u0", UB[s].rearrange("p (h c) n -> p h c n", c=2)[:, :, 0, 0:n], narrow(s, 1))
                    for s in range(2):
                        if rw:
                            g = 2 * pair + s
                            copy(s, "s", SB[s][:, 0, 0:HD], ps[:, 4 * s + 2, 0:HD], scol[:, g:g + 1])
                        else:
                            copy(s, "s", SB[s], narrow(s, 2))
                    if rw:
                        for s in range(2):
                            copy(s, "z1", ZB[s][:, :, 0:n], ps[:, 4 * s:4 * s + 3:2, 0:n])
                    for s in range(2):
                        copy(s, "u1", UB[s].rearrange("p (h c) n -> p h c n", c=2)[:, :, 1, 0:n], narrow(s, 1))

            def finish_mixer(L):
                sums = (L + 1) * (2 * len(R_SUMS) + len(G_SUMS))
                act.wait_ge(mat_summed[0], sums)
                act.wait_ge(mat_summed[1], sums)
                run(QSQ, OG, ACT.Square).then_inc(hn_act, 1)
                act.wait_ge(hn_summed, 3 * L + 2)
                run(QSQ, banks(4, 1024), ACT.Sqrt, bias=eps_b[:, 0:1], scale=1.0 / P).then_inc(hn_act, 1)
                act.wait_ge(hn_dve, 3 * L + 1)
                run(SQ, KK, ACT.Square).then_inc(hn_act, 1)
                act.wait_ge(hn_summed, 3 * L + 3)
                run(SQ, banks(2, 1024), ACT.Sqrt, bias=eps_b[:, 2:3], scale=1.0 / HD).then_inc(hn_act, 1)

            def dense(L):
                act.wait_ge(mixed, 4 * (L + 1))
                norm(2 * L + 1)
                s0 = first["ffn", L]

                def make_high(i):
                    act.wait_ge(slab_in[place[s0 + i]], landed[s0 + i])
                    if i >= HIGHS:
                        act.wait_ge(slab_done, s0 + i - HIGHS + 1)
                    run(high[i % HIGHS], slab(place[s0 + i]), ACT.Copy).then_inc(slab_high, 1)

                make_high(0)
                act.wait_ge(normed, 2 * L + 2)
                for half in range(2):
                    run(hT_high[:, 4 * half:4 * half + 4, :], hT[:, 4 * half:4 * half + 4, :],
                        ACT.Copy).then_inc(norm_high, 1)
                make_high(1)
                make_high(2)
                for i, (kind, j) in enumerate(FFN_ORDER):
                    if kind == "g":
                        act.wait_ge(slab_done, s0 + i + 1)
                        if j >= 2:
                            act.wait_ge(ffn_dve, j - 1)
                        run(FG[:, j % 2, :], ps[:, 2 * (j % 2), :], ACT.Silu).then_inc(ffn_act, 1)
                    if i + HIGHS < N_FFN:
                        make_high(i + HIGHS)
                    if kind == "u":
                        act.wait_ge(ffn_dve, j + 1)
                        run(FH_high[:, j % 2, :], FH, ACT.Copy).then_inc(ffn_high, 1)

            def experts(lap):
                s0 = first["moe", 1] + lap * NE * N_FFN

                def keep_tokens(e):
                    act.wait_ge(gathered, e + (lap * (NE + 1) + 1))
                    run(XS_high, ps[:, 0:2, :].rearrange("p b (k n) -> p (b k) n", n=P), ACT.Copy).then_inc(gather_kept, 1)

                keep_tokens(0)
                act.wait_ge(zero_put, lap + 1)
                with act.Fori(0, NE) as e:
                    n_e = e + lap * NE
                    chunks = e * FC + lap * NE * FC

                    def make_high(i):
                        slot = i % FFN_RING
                        act.wait_ge(slab_in[slot], e * (16 * E_LAPS)
                                    + (16 * (uses[slot] - E_LAPS + i // FFN_RING + 1 + lap * NE * E_LAPS)))
                        act.wait_ge(slab_done, e * N_FFN + (s0 + i - HIGHS + 1))
                        run(high[i % HIGHS], slab(slot), ACT.Copy).then_inc(slab_high, 1)

                    def keep_h(j):
                        act.wait_ge(e_turned, chunks + (j + 1))
                        run(FH_high[:, j % 2, 0:T], ps[:, 6 + j % 2, 0:T], ACT.Copy).then_inc(e_high, 1)

                    make_high(0)
                    make_high(1)
                    act.wait_ge(slab_done, e * N_FFN + s0)
                    run(YE, banks(2, 1024), ACT.Copy).then_inc(e_kept, 1)
                    make_high(2)
                    for i, (kind, j) in enumerate(FFN_ORDER):
                        if kind == "g":
                            act.wait_ge(slab_done, e * N_FFN + (s0 + i + 1))
                            if j >= 2:
                                act.wait_ge(e_dve, chunks + (j - 1))
                            run(FG[:, j % 2, 0:T], ps[:, j % 2, 0:T], ACT.Silu).then_inc(e_act, 1)
                            if j:
                                keep_h(j - 1)
                        if i + HIGHS < N_FFN:
                            make_high(i + HIGHS)
                        if (kind, j) == ("g", 1):
                            act.wait_ge(hot_turned, n_e + 1)
                            run(PC, ps[:, 7, 0:2 * P], ACT.Copy).then_inc(hot_kept, 1)
                    keep_tokens(e + 1)
                    keep_h(FC - 1)
                act.wait_ge(slab_done, s0 + NE * N_FFN)
                run(YE, banks(2, 1024), ACT.Copy).then_inc(e_kept, 1)

            def shifted(t):
                if t >= 12:
                    return LO[:, (t - 12) * T:(t - 11) * T]
                return (R3, K3, V3)[t // NT][:, t % NT, :]

            act.wait_ge(x_turned, 1)
            run(xT[:].rearrange("p k n -> p (k n)"), banks(0, 2048), ACT.Copy).then_inc(x_kept, 1)
            act.wait_ge(x_kept, 1)
            for L in range(DEPTH):
                act.wait_ge(vec_turned, L + 1)
                run(vec[:, L, :], ps[:, VEC_BANK[L], 0:N_VEC], ACT.Copy).then_inc(vec_kept, 1)
                act.wait_ge(vec_kept, 2 * L + 2)
                if L == 0:
                    act.wait_ge(head_in, 16 * 2 * DEPTH)
                    step(run(minus_a[:], head_raw[:, 0, :], ACT.Exp))
                    run(minus_a[:], minus_a[:], ACT.Copy, scale=-1.0)
                if L:
                    act.wait_ge(ffn_added, 4)
                project(L)
                turn_tokens(L)
                groups(L)
                finish_mixer(L)
                if L == 0:
                    dense(L)
            act.wait_ge(mixed, 8)
            norm(3)
            for i, dst in enumerate((h_tok_high, x_tok)):
                act.wait_ge(tok_turned, i + 1)
                run(dst.rearrange("p a n -> p (a n)"), banks(4 * i, 2048), ACT.Copy).then_inc(tok_kept, 1)
            act.wait_ge(diff_made, 1)
            run(g_exp, g_diff, ACT.Exp).then_inc(exp_made, 1)
            experts(0)
            act.wait_ge(over_made, 1)
            more = act.value_load(over[0:1, 0:1])
            with act.If(more > 0):
                experts(1)
            act.wait_ge(moe_added, 1)
            for a in range(2):
                step(run(x_sq[:, a, :], x_tok[:, a, :], ACT.Square, accum_out=xsum[:, a:a + 1]))
            run(xsum, xsum, ACT.Sqrt, bias=eps_b[:, 0:1], scale=1.0 / D).then_inc(fin_root, 1)

        @block.vector
        def _(dve):
            step = Chain(dve, dve_steps)
            tt, ts, stt = nc.vector.tensor_tensor, nc.vector.tensor_scalar, nc.vector.scalar_tensor_tensor

            def v_at(L, at_, n=1):
                return vec[:, L, at_:at_ + n]

            def per_tile(L, at_):
                return vec[:, L, at_:at_ + NT].unsqueeze(2).broadcast_to([P, NT, T])

            def by_tile(ap):
                return ap.rearrange("p (t n) -> p t n", t=NT)

            def by_chunk(ap):
                return ap.rearrange("p (q n) -> p q n", q=8)

            def norm(n, at_):
                dve.wait_ge(rooted, n + 1)
                root = RSTD_ffn if n % 2 else RSTD
                step(nc.vector.reciprocal(root, root))
                for k in range(KT):
                    g = vec[:, n // 2, at_ + k:at_ + k + 1]
                    last = stt(hT[:, k, :], xT[:, k, :], g, root, ALU.mult, ALU.mult)
                last.then_inc(normed, 1)

            def less_high(dst, src, high_part):
                return tt(dst, src, high_part.bitcast(F32), ALU.subtract)

            def low_in(L, i):
                dve.wait_ge(slab_high, split_before["mix", L] + i + 1)
                less_high(mix_low[i % 3], slab(i % 3), mix_high[i % 3]).then_inc(slab_split, 1)

            def in_slab(L, o):
                dve.wait_ge(proj_act, N_IN * L + o + 1)
                for m in range(2):
                    src = ps[:, o % 4, m * T:(m + 1) * T]
                    if o < 7:
                        t = IN_SLABS[o] // P + m
                        dst = (LO[:, (t - 12) * T:(t - 11) * T] if t >= 12 else (R3, K3, V3)[t // NT][:, t % NT, :])
                        last = stt(dst[:, 1:T], src[:, 0:T - 1], v_at(L, V_MU + t), dst[:, 1:T], ALU.mult, ALU.add)
                if o >= 7:
                    for back in range(1, 4):
                        for m in range(2):
                            src = ps[:, o % 4, m * T:(m + 1) * T]
                            i = 2 * (o - 7) + m
                            dst = QKV[:, i * T + back:(i + 1) * T]
                            last = stt(dst, src[:, 0:T - back], v_at(L, V_CONV + (3 - back) * 12 + i), dst,
                                       ALU.mult, ALU.add)
                            if back < 3:
                                step.mark(last)
                        if back < 3:
                            dve.wait_ge(dve_steps, step.n)
                last.then_inc(proj_dve, 1)
                low_in(L, o + 3)

            def project(L):
                norm(2 * L, V_N1)
                for half in range(2):
                    dve.wait_ge(norm_high, 4 * L + half + 1)
                    cut = slice(4 * half, 4 * half + 4)
                    less_high(mix_norm_low[:, cut, :], hT[:, cut, :], mix_norm_high[:, cut, :]).then_inc(norm_split, 1)
                for i in range(3):
                    low_in(L, i)
                dve.wait_ge(ab_split, 2 * L + 1)
                less_high(w_ab_low[:], w_ab[:], w_ab_high[:]).then_inc(ab_split, 1)
                step.mark(nc.vector.memset(LC[:, :, 0:1], 0.0))
                for o in range(7):
                    in_slab(L, o)
                dve.wait_ge(proj_dve, N_CONV * L + 7)
                tt(by_tile(KK), K3, per_tile(L, V_KK), ALU.mult).then_inc(kk_made, 1)
                in_slab(L, 7)
                in_slab(L, 8)
                dve.wait_ge(decay_sig, L + 1)
                flat = view(o_LC, 1032)
                step(nc.vector.tensor_tensor_scan(flat, restart[:], flat, 0.0, ALU.mult, ALU.add))
                step(nc.vector.tensor_copy(mid, LC[:, :, 64]))
                tt(LC, LC, mid.unsqueeze(2).broadcast_to([P, 8, 129]), ALU.subtract).then_inc(log_decay, 1)
                in_slab(L, 9)
                in_slab(L, 10)
                dve.wait_ge(kk_rooted, L + 1)
                step(nc.vector.reciprocal(SQ, SQ))
                step(tt(KK, KK, SQ, ALU.mult))
                in_slab(L, 11)
                in_slab(L, 12)
                dve.wait_ge(rate_sig, L + 1)
                for t in range(NT):
                    last = ts(SQ[:, t * T:(t + 1) * T], A3[:, t, :], -1.0, v_at(L, V_KA + t), ALU.add, ALU.mult)
                step(last)
                step.mark(stt(by_tile(K3_flat), by_tile(SQ), 1.0, K3, ALU.add, ALU.mult))
                dve.wait_ge(decays, 2 * L + 2)
                stt(AR[:, :, 0, :], by_chunk(KK), -1.0, EP[:, :, 0:P], ALU.mult, ALU.mult)
                tt(AR[:, :, 1, :], by_chunk(view(o_R, 1024)), EP[:, :, 1:129], ALU.mult)
                low_in(L, 16)
                step(tt(BH, by_chunk(KK), by_chunk(view(o_A, 1024)), ALU.mult))
                tt(scol, EP[:, 0::2, P], EM[:, 1::2, 0], ALU.mult)
                tt(BH, BH, EM[:, :, 1:129], ALU.mult)
                tt(KH, by_chunk(K3_flat), EM[:, :, 1:129], ALU.mult).then_inc(rw_ready, 1)
                step(tt(SQ, view(o_R, 1024), K3_flat, ALU.mult))
                tt(by_tile(SQ), by_tile(SQ), per_tile(L, V_RK), ALU.mult).then_inc(rk_ready, 1)
                low_in(L, 17)
                dve.wait_ge(ab_done, L + 1)
                dve.wait_ge(head_in, 16 * 2 * DEPTH)
                ts(g4[:, 0, :], ps[0:GH, 4, 0:T], head_raw[:, 1, L:L + 1], None, ALU.add).then_inc(ab_dve, 1)
                dve.wait_ge(ab_act, 3 * L + 1)
                ts(g4[:, 2, :], g4[:, 1, :], 1.0, None, ALU.add).then_inc(ab_dve, 1)
                dve.wait_ge(ab_dve, 3 * L + 2)
                step.mark(nc.vector.reciprocal(g4[:, 4, :], g4[:, 2, :]))
                dve.wait_ge(ab_act, 3 * L + 2)
                step(ts(g4[:, 2, :], g4[:, 2, :], -1.0, None, ALU.add))
                step(tt(g4[:, 2, :], g4[:, 1, :], g4[:, 2, :], ALU.subtract))
                step(tt(g4[:, 2, :], g4[:, 2, :], g4[:, 4, :], ALU.mult))
                step(tt(g4[:, 2, :], g4[:, 2, :], g4[:, 3, :], ALU.add))
                step(stt(g4[:, 2, :], g4[:, 0, :], 0.0, g4[:, 2, :], ALU.max, ALU.add))
                step(ts(g4[:, 2, :], g4[:, 2, :], minus_a[:, L:L + 1], None, ALU.mult))
                for c in range(2):
                    last = nc.vector.tensor_tensor_scan(GB[:, c * P:(c + 1) * P], ones[0:GH, :],
                                                        g4[:, 2, c * P:(c + 1) * P], 0.0, ALU.mult, ALU.add)
                last.then_inc(ab_dve, 1)
                low_in(L, 18)
                low_in(L, 19)
                dve.wait_ge(rk_summed, L + 1)
                tt(view(o_R, 1024), banks(6, 1024), view(o_V, 1024), ALU.mult).then_inc(bonus_made, 1)
                low_in(L, 20)
                dve.wait_ge(qk_rooted, 2 * L + 1)
                step(nc.vector.reciprocal(QSQ, QSQ))
                tt(KBQ[:, :, 1, :], by_chunk(Q1), by_chunk(QSQ), ALU.mult)
                low_in(L, 21)
                dve.wait_ge(qk_rooted, 2 * L + 2)
                ksq = KSQ.rearrange("p q n -> p (q n)")
                step(nc.vector.reciprocal(ksq, ksq))
                step(tt(K1, K1, ksq, ALU.mult))
                low_in(L, 22)
                dve.wait_ge(spread_kept, L + 1)
                tt(KBQ[:, :, 0, :], by_chunk(K1), by_chunk(view(o_EM, 1024)), ALU.mult)
                dve.wait_ge(silu_done, 3 * L + 3)
                tt(V1, V1, view(o_EM, 1024), ALU.mult).then_inc(vb_made, 1)
                dve.wait_ge(cols_turned, L + 1)
                nc.vector.tensor_copy(gcol, ps[:, 4, 0:2 * GH].rearrange("p (c h) -> p c h", c=2)).then_inc(cols_kept, 1)
                dve.wait_ge(cols_kept, L + 1)
                tt(kdec, BG[:, :, P - 1], gcol[:, 0, :], ALU.subtract).then_inc(kdec_arg, 1)
                for h in range(GH):
                    for c in range(2):
                        last = ts(DD[:, 2 * h + c, :], BG[:, h, c * P:(c + 1) * P], gcol[:, c, h:h + 1], 0.0,
                                  ALU.subtract, ALU.min)
                last.then_inc(dd_made, 1)

            def turn_tokens(L):
                dve.wait_ge(kdec_made, 2 * L + 2)
                dve.wait_ge(gdn_turned, L + 1)
                src = ps[:, 7, :].rearrange("p (h n) -> p h n", h=GH)
                tt(TKN.rearrange("p (h n) -> p h n", h=GH), src, kdec.unsqueeze(2).broadcast_to([P, GH, P]),
                   ALU.mult).then_inc(gdn_keyed, 1)
                late = slice(P, 2 * P)
                kb = KBQ.rearrange("p (h c) s n -> p h c s n", c=2)
                stt(KG.rearrange("p (h n) -> p h n", h=GH), kb[:, :, 1, 0, :], -1.0, EG[:, :, late], ALU.mult, ALU.mult)
                tt(QG.rearrange("p (h n) -> p h n", h=GH), kb[:, :, 1, 1, :], EG[:, :, late], ALU.mult)
                dve.wait_ge(dd_exp, L + 1)
                dve.wait_ge(rw_turned, L + 1)
                tt(DM, DD.unsqueeze(2).broadcast_to([P, 8, 2, P]),
                   later_neg[:].unsqueeze(1).broadcast_to([P, 8, 2, P]), ALU.mult).then_inc(gdn_ready, 1)

            def groups(L):
                for pair in range(3):
                    rw = pair < 2
                    base, _, _ = group_bases(L, pair)
                    steps = R_AT if rw else G_AT
                    if pair == 2:
                        dve.wait_ge(gdn_ready, L + 1)
                    flat_mask = later[:].rearrange("p s n -> p (s n)")

                    def masked(s, dst, b):
                        g = 2 * pair + s
                        src = ps[:, 4 * s + b:4 * s + b + 2, :].rearrange("p b (q n) -> p (b q) n", q=2)
                        if rw:
                            mask = flat_mask.unsqueeze(1).broadcast_to([P, 4, 2 * P])
                        else:
                            mask = DM[:, 4 * (g - 4):4 * (g - 4) + 4, :, :].rearrange("p q s n -> p q (s n)")
                        return tt(dst, src, mask, ALU.mult)

                    for s in range(2):
                        dve.wait_ge(mat_done[s], base + 1)
                        Q, A, Gm = MQ[s][:, :, 0:P], DG[s][:, :, 0:P], DG[s][:, :, P:2 * P]
                        step(masked(s, MQ[s], 0))
                        tt(A, Q, blocks16[:].unsqueeze(1).broadcast_to([P, 4, P]), ALU.mult).then_inc(mat_summed[s], 1)
                        sums = L * (2 * len(R_SUMS) + len(G_SUMS)) + pair * len(R_SUMS)
                        if rw:
                            step.mark(masked(s, MK[s], 2))
                        dve.wait_ge(mat_summed[s], sums + 1)
                        step.mark(tt(Gm, A, ident[:].unsqueeze(1).broadcast_to([P, 4, P]), ALU.add))
                        tt(Q, Q, A, ALU.subtract).then_inc(mat_summed[s], 1)
                    for what in ("gen1", "gen2", "last1", "gen3", "gen4", "last2"):
                        for s in range(2):
                            Gm = DG[s][:, :, P:2 * P]
                            dve.wait_ge(mat_done[s], base + steps[what])
                            tt(Gm, ps[:, 4 * s + 3, :].rearrange("p (q n) -> p q n", q=4), Gm,
                               ALU.add).then_inc(mat_summed[s], 1)
                    if not rw:
                        for s in range(2):
                            g = 2 * pair + s
                            dve.wait_ge(mat_done[s], base + steps["z1"])
                            src = ps[:, 4 * s, 0:2 * P]
                            vb = TVB[:, 1, 2 * (g - 4) * P:(2 * (g - 4) + 2) * P]
                            tt(ZB[s].rearrange("p q n -> p (q n)"), src, vb, ALU.add).then_inc(mat_summed[s], 1)
                    for s in range(2):
                        g = 2 * pair + s
                        dve.wait_ge(mat_done[s], base + steps["o"])
                        if rw:
                            last = nc.vector.tensor_copy(KK[:, g * T:(g + 1) * T], ps[:, 4 * s + 3, 0:T])
                        else:
                            last = nc.vector.tensor_copy(OG[:, (g - 4) * 512:(g - 3) * 512], ps[:, 4 * s + 3, :])
                        last.then_inc(mat_summed[s], 1)

            def finish_mixer(L):
                dve.wait_ge(hn_summed, 3 * L + 1)
                sums = (L + 1) * (2 * len(R_SUMS) + len(G_SUMS))
                dve.wait_ge(mat_summed[0], sums)
                dve.wait_ge(mat_summed[1], sums)
                stt(KK, banks(0, 1024), -1.0 / HD, KK, ALU.mult, ALU.add).then_inc(hn_dve, 1)
                dve.wait_ge(hn_act, 4 * L + 2)
                step(nc.vector.reciprocal(QSQ, QSQ))
                step(tt(OG, OG, QSQ, ALU.mult))
                stt(OG, OG, v_at(L, V_GN), Z, ALU.mult, ALU.mult).then_inc(hn_dve, 1)
                dve.wait_ge(hn_act, 4 * L + 4)
                step(nc.vector.reciprocal(SQ, SQ))
                step(tt(KK, KK, SQ, ALU.mult))
                for t in range(NT):
                    cut = slice(t * T, (t + 1) * T)
                    last = ts(KK[:, cut], KK[:, cut], v_at(L, V_LG + t), v_at(L, V_LB + t), ALU.mult, ALU.add)
                step(last)
                step(tt(KK, KK, view(o_R, 1024), ALU.add))
                tt(KK, KK, G, ALU.mult).then_inc(hn_dve, 1)
                for i in range(2):
                    dve.wait_ge(slab_done, first["mix", L] + N_IN + i + 1)
                    step.mark(tt(YT[:, i * 1024:(i + 1) * 1024], banks(4 + 2 * i, 1024),
                                 GATES[:, 2048 + i * 1024:2048 + (i + 1) * 1024], ALU.mult))
                for i in range(2):
                    dve.wait_ge(slab_done, first["mix", L] + N_IN + i + 3)
                    ya = GATES[:, i * 1024:(i + 1) * 1024]
                    step(tt(ya, banks(2 * i, 1024), ya, ALU.mult))
                    last = tt(YT[:, i * 1024:(i + 1) * 1024], YT[:, i * 1024:(i + 1) * 1024], ya, ALU.add)
                last.then_inc(merged, 1)
                for j in range(4):
                    dve.wait_ge(slab_done, first["mix", L] + N_IN + 4 + j + 1)
                    xs = xT[:, 2 * j:2 * j + 2, :].rearrange("p k n -> p (k n)")
                    tt(xs, ps[:, j, :], xs, ALU.add).then_inc(mixed, 1)

            def dense(L):
                norm(2 * L + 1, V_N2)
                s0 = first["ffn", L]

                def make_low(i):
                    dve.wait_ge(slab_high, split_before["ffn", L] + i + 1)
                    less_high(low[i % FFN_RING], slab(i % FFN_RING), high[i % HIGHS]).then_inc(slab_split, 1)

                for half in range(2):
                    dve.wait_ge(norm_high, 4 * L + 2 + half + 1)
                    cut = slice(4 * half, 4 * half + 4)
                    less_high(hT_low[:, cut, :], hT[:, cut, :], hT_high[:, cut, :]).then_inc(norm_split, 1)
                for i in range(HIGHS):
                    make_low(i)
                for i, (kind, j) in enumerate(FFN_ORDER):
                    if kind == "u":
                        dve.wait_ge(ffn_act, j + 1)
                        dve.wait_ge(slab_done, s0 + i + 1)
                        if j:
                            dve.wait_ge(ffn_split, j)
                        tt(FH, ps[:, 2 * (j % 2) + 1, :], FG[:, j % 2, :], ALU.mult).then_inc(ffn_dve, 1)
                    if i + HIGHS < N_FFN:
                        make_low(i + HIGHS)
                    if kind == "u":
                        dve.wait_ge(ffn_high, j + 1)
                        less_high(FH_low[:, j % 2, :], FH, FH_high[:, j % 2, :]).then_inc(ffn_split, 1)
                dve.wait_ge(slab_done, s0 + N_FFN)
                for j in range(4):
                    xs = xT[:, 2 * j:2 * j + 2, :].rearrange("p k n -> p (k n)")
                    tt(xs, ps[:, 4 + j, :], xs, ALU.add).then_inc(ffn_added, 1)

            def route():
                dve.wait_ge(tok_kept, 1)
                less_high(h_tok_low.rearrange("p a n -> p (a n)"), banks(0, 2048),
                          h_tok_high.rearrange("p a n -> p (a n)")).then_inc(norm_split, 1)
                step.mark(nc.vector.memset(chosen9, 0.0))
                step.mark(nc.vector.memset(pos9, 0.0))
                dve.wait_ge(logits_done, 1)
                step(nc.vector.tensor_copy(logits, ps[:, 0, 0:2 * NE].rearrange("p (a n) -> p a n", a=2)))
                for a in range(2):
                    step(nc.vector.max(top[:, a, :], logits[:, a, :]))
                    step(nc.vector.max_index(topi[:, a, :], top[:, a, :], logits[:, a, :]))
                step(nc.vector.tensor_copy(topi_f, topi[:]))
                tt(g_diff, top[:, :, 1], top[:, :, 0], ALU.subtract).then_inc(diff_made, 1)
                dve.wait_ge(exp_made, 1)
                step(ts(g_first, g_exp, 1.0, None, ALU.add))
                step(nc.vector.reciprocal(g_first, g_first))
                step(tt(g_second, g_exp, g_first, ALU.mult))
                for a in range(2):
                    step.mark(ts(hot1[:, a, :], slots[:, 0:NE], topi_f[:, a, 0:1], None, ALU.is_equal))
                    step(ts(hot2[:, a, :], slots[:, 0:NE], topi_f[:, a, 1:2], None, ALU.is_equal))
                tt(chosen, hot1, hot2, ALU.add).then_inc(routed, 1)
                dve.wait_ge(routed, 1)
                for a in range(2):
                    step.mark(ts(hot1[:, a, :], hot1[:, a, :], g_first[:, a:a + 1], None, ALU.mult))
                    step(ts(hot2[:, a, :], hot2[:, a, :], g_second[:, a:a + 1], None, ALU.mult))
                step.mark(tt(combine, hot1, hot2, ALU.add))
                dve.wait_ge(pos_done, 1)
                step(nc.vector.tensor_copy(pos, ps[:, 1, 0:2 * NE].rearrange("p (a n) -> p a n", a=2)))
                step(nc.vector.reduce_max(most, ps[:, 1, 2 * NE:3 * NE], AX_X))
                ts(over[:], most, float(P), None, ALU.is_gt).then_inc(over_made, 1)

            def experts(lap):
                s0 = first["moe", 1] + lap * NE * N_FFN
                if lap:
                    ts(pos9, pos9, -float(P), None, ALU.add).then_inc(pos_moved, 1)
                    dve.wait_ge(pos_moved, 1)

                def make_hot(e):
                    for a in range(2):
                        last = ts(PT[:, a, :], slots[:], pos9[:, a, bass.ds(e, 1)], chosen9[:, a, bass.ds(e, 1)],
                                  ALU.is_equal, ALU.mult)
                    last.then_inc(hot_made, 1)

                def split_tokens(e):
                    dve.wait_ge(gather_kept, e + (lap * (NE + 1) + 1))
                    less_high(XS_low, ps[:, 0:2, :].rearrange("p b (k n) -> p (b k) n", n=P),
                              XS_high).then_inc(gather_split, 1)

                def add_up(e, halves):
                    for a in halves:
                        dve.wait_ge(scattered, 2 * e + (2 * lap * (NE + 1) + a + 1))
                        tt(x_tok[:, a, :], banks(4 + 2 * a, 1024), x_tok[:, a, :], ALU.add).then_inc(added, 1)

                make_hot(0)
                nc.vector.memset(PC, 0.0)
                nc.vector.memset(YE, 0.0).then_inc(zeroed, 1)
                split_tokens(0)
                with dve.Fori(0, NE) as e:
                    chunks = e * FC + lap * NE * FC

                    def make_low(i):
                        dve.wait_ge(slab_high, e * N_FFN + (split_before["moe", 1] + lap * NE * N_FFN + i + 1))
                        less_high(low[i % FFN_RING], slab(i % FFN_RING), high[i % HIGHS]).then_inc(slab_split, 1)

                    def split_h(j):
                        dve.wait_ge(e_high, chunks + (j + 1))
                        less_high(FH_low[:, j % 2, 0:T], ps[:, 6 + j % 2, 0:T], FH_high[:, j % 2, 0:T]).then_inc(e_split, 1)

                    make_low(0)
                    make_low(1)
                    for a in range(2):
                        last = ts(PTC[:, a, :], slots[:], pos9[:, a, bass.ds(e, 1)], combine[:, a, bass.ds(e, 1)],
                                  ALU.is_equal, ALU.mult)
                    last.then_inc(weights_made, 1)
                    add_up(e, (0,))
                    make_low(2)
                    add_up(e, (1,))
                    for i, (kind, j) in enumerate(FFN_ORDER):
                        if kind == "u":
                            dve.wait_ge(e_act, chunks + (j + 1))
                            dve.wait_ge(slab_done, e * N_FFN + (s0 + i + 1))
                            tt(FH[:, 0:T], ps[:, 4 + j % 2, 0:T], FG[:, j % 2, 0:T], ALU.mult).then_inc(e_dve, 1)
                        if kind == "g" and j:
                            split_h(j - 1)
                        if i + HIGHS < N_FFN:
                            make_low(i + HIGHS)
                        if (kind, j) == ("d", 5):
                            make_hot(e + 1)
                    split_tokens(e + 1)
                    split_h(FC - 1)
                add_up(NE, (0, 1))

            dve.wait_ge(consts_made, 1)
            dve.wait_ge(x_kept, 1)
            for L in range(DEPTH):
                dve.wait_ge(vec_kept, 2 * L + 1)
                ts(one_less_mu[:, L, :], vec[:, L, V_MU:V_MU + 14], -1.0, 1.0, ALU.mult, ALU.add).then_inc(vec_kept, 1)
                project(L)
                turn_tokens(L)
                groups(L)
                finish_mixer(L)
                if L == 0:
                    dense(L)
            norm(3, V_N2)
            route()
            experts(0)
            more = dve.value_load(over[0:1, 0:1])
            with dve.If(more > 0):
                experts(1)
            nc.vector.memset(most, 0.0).then_inc(moe_added, 1)
            dve.wait_ge(fin_in, 16)
            dve.wait_ge(fin_root, 1)
            step(nc.vector.reciprocal(xsum, xsum))
            for a in range(2):
                stt(x_tok_out[:, a, :], x_tok[:, a, :], xsum[:, a:a + 1], fin_g, ALU.mult, ALU.mult).then_inc(fin_made, 1)


_INS = ['x', 'norm1_g', 'w_in', 'tshift_mu', 'w0', 'w_decay_up', 'a0', 'w_iclr_up', 'w_gate_up', 'k_k', 'k_a', 'r_k',
        'lnx_g', 'lnx_b', 'w_pa', 'conv_w', 'a_log', 'dt_bias', 'gdn_norm_g', 'w_pb', 'w_out', 'norm2_g',
        'ffn_w_gate', 'ffn_w_up', 'ffn_w_down', 'moe_router', 'moe_w_gate', 'moe_w_up', 'moe_w_down', 'final_g']
_OUTS = [((1, T, D), 'float32')]


def kernel(**inputs):
    import numpy as _np
    import concourse.bacc as _bacc
    from concourse import mybir as _mybir
    from concourse.bass_utils import run_bass_kernel_spmd as _run

    nc = _bacc.Bacc("TRN2", target_bir_lowering=False, num_devices=1)
    arrays, args = {}, []
    for name in _INS:
        a = _np.ascontiguousarray(inputs[name])
        arrays[f"in_{name}_dram"] = a
        args.append(nc.dram_tensor(f"in_{name}_dram", a.shape, _mybir.dt.from_np(a.dtype), kind="ExternalInput").ap())
    for i, (shape, dtype) in enumerate(_OUTS):
        dt = _mybir.dt.from_np(_np.dtype(dtype))
        args.append(nc.dram_tensor(f"out_{i}_dram", shape, dt, kind="ExternalOutput").ap())
    trunk(nc, *args)
    r = _run(nc, [arrays], core_ids=[0])
    return r.results[0]["out_0_dram"]
```

```python
from contextlib import ExitStack

import concourse.bass as bass
from concourse import mybir

F32 = mybir.dt.float32
F32R = mybir.dt.float32r
BF16 = mybir.dt.bfloat16
I32 = mybir.dt.int32
U32 = mybir.dt.uint32
ALU = mybir.AluOpType
ACT = mybir.ActivationFunctionType
AX_X = mybir.AxisListType.X

P = 128
D = 1024
T = 256
DEPTH = 2
KT = D // P
RW = 512
NT = RW // P
HD = 64
GH = 4
RWKV_COLS = 1792
GDN_BASE = RWKV_COLS
AB_BASE = GDN_BASE + 3 * RW
Z_BASE = AB_BASE + 2 * GH
GATE_BASE = Z_BASE + RW
F = 2816
NE = 8
NORM_EPS = 1e-6
GN_EPS = 64e-5
DECAY_C = 0.6065306597126334

SLAB = 2048
COLS = SLAB // KT
FC = F // COLS
MIX_RING = 3
MIX_EARLY = 11
FFN_RING = 11
HIGHS = 3
IN_SLABS = ([1536] + [512, 768, 0, 256, 1024, 1280] + [GDN_BASE + COLS * i for i in range(6)]
            + [Z_BASE, Z_BASE + COLS] + [GATE_BASE + COLS * i for i in range(8)])
N_IN = len(IN_SLABS)
N_CONV = 13
N_MIX = N_IN + 8
N_FFN = 3 * FC

V_MU, V_W0, V_A0, V_KK, V_KA, V_RK, V_LG, V_LB, V_CONV, V_N1, V_N2, V_GN = (
    0, 14, 18, 22, 26, 30, 34, 38, 42, 90, 98, 106)
N_VEC = 107
NORM_BANK = (7, 7, 7, 0)
VEC_BANK = (6, 0)

MIX0 = MIX_RING * SLAB


def ffn_order():
    order = [("g", 0), ("u", 0)]
    for j in range(1, FC):
        order += [("g", j), ("u", j), ("d", j - 1)]
    return order + [("d", FC - 1)]


FFN_ORDER = ffn_order()
AT = {key: n for n, key in enumerate(FFN_ORDER)}

R_STEPS = ["pair", "dT", "sq", "gen1", "gen2", "last1", "gT", "m", "gen3", "gen4", "last2",
           "z0", "u0", "s", "z1", "u1", "o"]
G_STEPS = [s for s in R_STEPS if s != "z0"]
R_AT = {s: n + 1 for n, s in enumerate(R_STEPS)}
G_AT = {s: n + 1 for n, s in enumerate(G_STEPS)}
R_COPIES = ["dT", "sq", "sqT", "gen1", "gen1T", "gen2T", "gT", "m", "mT", "gen3", "gen3T", "gen4T",
            "z0", "u0", "s", "z1", "u1"]
G_COPIES = [s for s in R_COPIES if s not in ("z0", "z1")]
RC_AT = {s: n + 1 for n, s in enumerate(R_COPIES)}
GC_AT = {s: n + 1 for n, s in enumerate(G_COPIES)}
R_SUMS = ["d", "masked", "base", "gen1", "gen2", "last1", "gen3", "gen4", "last2", "o"]
G_SUMS = ["d", "masked", "base", "gen1", "gen2", "last1", "gen3", "gen4", "last2", "z1", "o"]
RS_AT = {s: n + 1 for n, s in enumerate(R_SUMS)}
GS_AT = {s: n + 1 for n, s in enumerate(G_SUMS)}


class Chain:

    def __init__(self, eng, sem):
        self.eng, self.sem, self.n = eng, sem, 0

    def mark(self, ins):
        self.n += 1
        ins.then_inc(self.sem, 1)

    def __call__(self, ins):
        self.mark(ins)
        self.eng.wait_ge(self.sem, self.n)


def trunk(nc, x, norm1_g, w_in, tshift_mu, w0, w_decay_up, a0, w_iclr_up, w_gate_up, k_k, k_a, r_k, lnx_g, lnx_b,
          w_pa, conv_w, a_log, dt_bias, gdn_norm_g, w_pb, w_out, norm2_g, ffn_w_gate, ffn_w_up, ffn_w_down,
          moe_router, moe_w_gate, moe_w_up, moe_w_down, final_g, out, dbg=None):
    with ExitStack() as ctx:
        def sb(name, shape, dt=F32):
            return ctx.enter_context(nc.sbuf_tensor(name, shape, dt))

        def sem(name):
            return ctx.enter_context(nc.semaphore(name))

        ps = ctx.enter_context(nc.psum_tensor("ps", [P, 8, 512], F32))

        xT = sb("xT", [P, KT, T])
        hT = sb("hT", [P, KT, T])
        hT_at = nc.sbuf_base - 4 * KT * T
        ident = sb("ident", [P, P])
        ones = sb("ones", [P, P])
        head_ones = sb("head_ones", [P, P])
        later = sb("later", [P, 2, P])
        later_neg = sb("later_neg", [P, 2, P])
        blocks16 = sb("blocks16", [P, P])
        sel = sb("sel", [GH, GH, P])
        restart = sb("restart", [P, 8 * 129], BF16)
        slots = sb("slots", [P, P])
        vec_rows = sb("vec_rows", [P, P])
        vec = sb("vec", [P, DEPTH, N_VEC])
        one_less_mu = sb("one_less_mu", [P, DEPTH, 14])
        head_raw = sb("head_raw", [GH, 2, DEPTH])
        minus_a = sb("minus_a", [GH, DEPTH])
        lora_up = sb("lora_up", [P, RW])
        gate_up = sb("gate_up", [P, RW])
        w_ab = sb("w_ab", [P, KT, 2 * GH])
        w_ab_high = sb("w_ab_high", [P, KT, 2 * GH], F32R)
        w_ab_low = sb("w_ab_low", [P, KT, 2 * GH], F32R)
        eps_b = sb("eps_b", [P, 4])
        arena = sb("arena", [P, 44800])
        arena_at = nc.sbuf_base - 4 * 44800

        at = [MIX0]

        def take(n):
            at[0] += n
            return at[0] - n

        def view(off, n, rows=P):
            return arena[0:rows, off:off + n]

        def rounded(name, off, n):
            return nc.alloc_sbuf_tensor_at(name, [P, n], F32R, offset=arena_at + 4 * off)[:]

        o_R, o_K = take(1024), take(1024)
        o_V = take(1024)
        o_LO, o_LC, o_EP, o_EM, o_A = take(512), take(1032), take(1032), take(1032), take(1024)
        o_KK, o_AR, o_BH, o_KH, o_SQ, o_G = take(1024), take(2048), take(1024), take(1024), take(1024), take(1024)
        o_TV, o_TB, o_TK, o_QKV, o_KBQ = take(1024), take(512), take(512), take(3072), take(2048)
        o_Z, o_TVB, o_TKN, o_GB, o_GATES = take(1024), take(1024), take(512), take(512), take(4096)
        R3 = view(o_R, 1024).rearrange("p (t n) -> p t n", t=NT)
        K3_flat = view(o_K, 1024)
        K3 = view(o_K, 1024).rearrange("p (t n) -> p t n", t=NT)
        V3 = view(o_V, 1024).rearrange("p (t n) -> p t n", t=NT)
        LO = view(o_LO, 512)
        LC = view(o_LC, 1032).rearrange("p (q n) -> p q n", q=8)
        EP = view(o_EP, 1032).rearrange("p (q n) -> p q n", q=8)
        EM = view(o_EM, 1032).rearrange("p (q n) -> p q n", q=8)
        A3 = view(o_A, 1024).rearrange("p (t n) -> p t n", t=NT)
        KK = view(o_KK, 1024)
        AR = view(o_AR, 2048).rearrange("p (q s n) -> p q s n", q=8, s=2)
        BH = view(o_BH, 1024).rearrange("p (q n) -> p q n", q=8)
        KH = view(o_KH, 1024).rearrange("p (q n) -> p q n", q=8)
        SQ = view(o_SQ, 1024)
        G = view(o_G, 1024)
        TV = view(o_TV, 1024).rearrange("p (c n) -> p c n", c=2)
        TB = view(o_TB, 512)
        TK = view(o_TK, 512)
        QKV = view(o_QKV, 3072)
        Q1, K1, V1 = view(o_QKV, 1024), view(o_QKV + 1024, 1024), view(o_QKV + 2048, 1024)
        KBQ = view(o_KBQ, 2048).rearrange("p (q s n) -> p q s n", q=8, s=2)
        Z = view(o_Z, 1024)
        TVB = view(o_TVB, 1024).rearrange("p (c n) -> p c n", c=2)
        TKN = view(o_TKN, 512)
        GB = view(o_GB, 512, GH)
        GATES = view(o_GATES, 4096)
        KG = view(o_QKV, 512)
        QG = view(o_QKV + 512, 512)
        OG = V1
        BG = view(o_LC, 1024).rearrange("p (h n) -> p h n", h=GH)
        EG = view(o_A, 1024).rearrange("p (h n) -> p h n", h=GH)
        BB = view(o_EM, 1024).rearrange("p (h n) -> p h n", h=GH)
        DD = view(o_EP, 1024).rearrange("p (q n) -> p q n", q=8)
        DM = view(o_K, 2048).rearrange("p (q s n) -> p q s n", q=8, s=2)
        x_tok_in = view(o_QKV, 2048).rearrange("p (a n) -> p a n", a=2)
        YT = view(o_KBQ, 2048)
        XSQ = view(o_KBQ, 2048)
        small = sb("small", [P, 96])
        mid = small[:, 0:8]
        scol = small[:, 8:12]
        gcol = small[:, 12:20].rearrange("p (c h) -> p c h", c=2)
        kdec = small[:, 20:24]
        norm_root = small[:, 24:26]
        q_root, k_root, gdn_root = small[:, 26:34], small[:, 34:42], small[:, 42:50]
        kk_root, dev_root = small[:, 50:66], small[:, 66:82]

        o = at[0]
        KSQ = view(o, 1024).rearrange("p (q n) -> p q n", q=4)
        g4 = view(o + 1024, 1280, GH).rearrange("p (i n) -> p i n", i=5)
        mix_norm_high = rounded("mix_norm_high", o + 2304, 2048).rearrange("p (k n) -> p k n", k=KT)
        mix_norm_low = nc.alloc_sbuf_tensor_at("mix_norm_low", [P, KT, T], F32R, offset=hT_at)[:]
        mix_high = [rounded(f"mix_high{i}", place_, SLAB) for i, place_ in enumerate((o_TV, o + 4352, o + 6400))]
        fin_high = [mix_high[0], rounded("fin_high1", o, SLAB), rounded("fin_high2", o + 2048, SLAB)]
        KK_high, KK_low = rounded("KK_high", o_SQ, 1024), rounded("KK_low", o_KK, 1024)
        OG_high, OG_low = rounded("OG_high", o + 6144, 1024), rounded("OG_low", o_QKV + 2048, 1024)
        YT_high, YT_low = rounded("YT_high", o + 4096, 2048), rounded("YT_low", o_KBQ, 2048)
        mix_low = {i: rounded(f"mix_low{i}", i * SLAB, SLAB) for i in range(MIX_RING)}
        mix_low[MIX_EARLY] = rounded("mix_low_early", o_KBQ, SLAB)

        MQ, MK, DG, DT, ZB, UB, SB = [], [], [], [], [], [], []
        for s in range(2):
            o = take(1024)
            MQ.append(view(o, 1024).rearrange("p (q n) -> p q n", q=4))
            o = take(1024)
            MK.append(view(o, 1024).rearrange("p (q n) -> p q n", q=4))
            o = take(1024)
            DG.append(view(o, 1024).rearrange("p (q n) -> p q n", q=4))
            o = take(512)
            DT.append(view(o, 512).rearrange("p (q n) -> p q n", q=4))
            o = take(256)
            ZB.append(view(o, 256).rearrange("p (q n) -> p q n", q=2))
            o = take(512)
            UB.append(view(o, 512).rearrange("p (q n) -> p q n", q=4))
            o = take(256)
            SB.append(view(o, 256).rearrange("p (q n) -> p q n", q=2))
        assert at[0] <= 44800, at[0]
        QSQ = view(o_TVB, 1024)

        at[0] = FFN_RING * SLAB
        low = [rounded(f"low{i}", i * SLAB, SLAB) for i in range(FFN_RING)]
        high = [rounded(f"high{i}", take(SLAB), SLAB) for i in range(HIGHS)]
        XSQ_ffn = view(at[0], 2048)
        FG = view(take(2 * 512), 1024).rearrange("p (b n) -> p b n", b=2)
        FH = view(take(512), 512)
        FH_high = rounded("FH_high", take(1024), 1024).rearrange("p (b n) -> p b n", b=2)
        FH_low = rounded("FH_low", take(1024), 1024).rearrange("p (b n) -> p b n", b=2)
        o = take(4096)
        hT_high = rounded("hT_high", o, 2048).rearrange("p (k n) -> p k n", k=KT)
        hT_low = rounded("hT_low", o + 2048, 2048).rearrange("p (k n) -> p k n", k=KT)
        h_tok_high = rounded("h_tok_high", o, 2048).rearrange("p (a n) -> p a n", a=2)
        h_tok_low = rounded("h_tok_low", o + 2048, 2048).rearrange("p (a n) -> p a n", a=2)
        x_tok_out = view(o, 2048).rearrange("p (a n) -> p a n", a=2)
        x_tok = view(take(2048), 2048).rearrange("p (a n) -> p a n", a=2)
        XS_high = rounded("XS_high", take(1024), 1024).rearrange("p (k n) -> p k n", k=KT)
        XS_low = rounded("XS_low", take(1024), 1024).rearrange("p (k n) -> p k n", k=KT)
        PT = rounded("PT", take(256), 256).rearrange("p (a n) -> p a n", a=2)
        PTC = view(take(256), 256).rearrange("p (a n) -> p a n", a=2)
        PC = view(take(256), 256)
        YE = view(take(1024), 1024)
        w_router = view(take(64), 64).rearrange("p (k n) -> p k n", k=KT)
        rt = view(take(256), 256)
        logits = rt[:, 0:16].rearrange("p (a n) -> p a n", a=2)
        top = rt[:, 16:32].rearrange("p (a n) -> p a n", a=2)
        topi_f = rt[:, 32:48].rearrange("p (a n) -> p a n", a=2)
        hot1 = rt[:, 48:64].rearrange("p (a n) -> p a n", a=2)
        hot2 = rt[:, 64:80].rearrange("p (a n) -> p a n", a=2)
        chosen9 = rt[:, 144:162].rearrange("p (a n) -> p a n", a=2)
        pos9 = rt[:, 162:180].rearrange("p (a n) -> p a n", a=2)
        chosen, pos = chosen9[:, :, 0:NE], pos9[:, :, 0:NE]
        combine = rt[:, 96:112].rearrange("p (a n) -> p a n", a=2)
        g_diff, g_exp = rt[:, 128:130], rt[:, 130:132]
        g_first, g_second = rt[:, 132:134], rt[:, 134:136]
        most = rt[:, 136:137]
        xsum = rt[:, 138:140]
        topi = sb("topi", [P, 2, 8], U32)
        over = sb("over", [P, 1], I32)
        fin_g = view(take(1024), 1024)
        x_sq = XSQ_ffn.rearrange("p (a n) -> p a n", a=2)
        assert at[0] <= 44800, at[0]

        slab_in = [sem(f"slab_in{i}") for i in range(FFN_RING + 1)]
        slab_done = sem("slab_done")
        consts_made = sem("consts_made")
        x_in = sem("x_in")
        rows_in = [sem(f"rows_in{L}") for L in range(DEPTH)]
        small_in = [sem(f"small_in{L}") for L in range(DEPTH)]
        head_in = sem("head_in")
        router_in = sem("router_in")
        fin_in = sem("fin_in")
        vec_turned, vec_kept = sem("vec_turned"), sem("vec_kept")
        x_turned, x_kept = sem("x_turned"), sem("x_kept")
        squared, summed, rooted, normed = sem("squared"), sem("summed"), sem("rooted"), sem("normed")
        inverted, root_spread = sem("inverted"), sem("root_spread")
        kk_inverted, kk_spread, kk_used = sem("kk_inverted"), sem("kk_spread"), sem("kk_used")
        qk_inverted, qk_spread, qk_used = sem("qk_inverted"), sem("qk_spread"), sem("qk_used")
        hn_inverted, hn_spread = sem("hn_inverted"), sem("hn_spread")
        proj_act, proj_dve = sem("proj_act"), sem("proj_dve")
        lora_acted, lora_done = sem("lora_acted"), sem("lora_done")
        decay_sig, rate_sig, gate_kept = sem("decay_sig"), sem("rate_sig"), sem("gate_kept")
        kk_made, kk_squared, kk_summed, kk_rooted = sem("kk_made"), sem("kk_squared"), sem("kk_summed"), sem("kk_rooted")
        log_decay, decays = sem("log_decay"), sem("decays")
        rw_ready, rk_ready, rk_summed, bonus_made = sem("rw_ready"), sem("rk_ready"), sem("rk_summed"), sem("bonus_made")
        silu_done, qk_squared, qk_summed = sem("silu_done"), sem("qk_squared"), sem("qk_summed")
        qk_rooted = sem("qk_rooted")
        ab_split = sem("ab_split")
        ab_done, ab_dve, ab_act = sem("ab_done"), sem("ab_dve"), sem("ab_act")
        spread, spread_kept, cols_turned, cols_kept = sem("spread"), sem("spread_kept"), sem("cols_turned"), sem("cols_kept")
        kdec_arg, kdec_made, dd_made, dd_exp = sem("kdec_arg"), sem("kdec_made"), sem("dd_made"), sem("dd_exp")
        vb_made, gdn_ready = sem("vb_made"), sem("gdn_ready")
        rw_turned, rw_kept = sem("rw_turned"), sem("rw_kept")
        gdn_turned, gdn_kept, gdn_keyed = sem("gdn_turned"), sem("gdn_kept"), sem("gdn_keyed")
        mat_done = [sem(f"mat_done{s}") for s in range(2)]
        mat_copied = [sem(f"mat_copied{s}") for s in range(2)]
        mat_summed = [sem(f"mat_summed{s}") for s in range(2)]
        hn_summed, hn_act, hn_dve = sem("hn_summed"), sem("hn_act"), sem("hn_dve")
        merged, mixed = sem("merged"), sem("mixed")
        branch_high, branch_split = sem("branch_high"), sem("branch_split")
        slab_high, slab_split = sem("slab_high"), sem("slab_split")
        norm_high, norm_split = sem("norm_high"), sem("norm_split")
        ffn_act, ffn_dve, ffn_added = sem("ffn_act"), sem("ffn_dve"), sem("ffn_added")
        ffn_high, ffn_split = sem("ffn_high"), sem("ffn_split")
        tok_turned, tok_kept = sem("tok_turned"), sem("tok_kept")
        routed, logits_done, diff_made, exp_made, pos_done, over_made = (
            sem("routed"), sem("logits_done"), sem("diff_made"), sem("exp_made"), sem("pos_done"), sem("over_made"))
        hot_made, gathered, gather_kept = sem("hot_made"), sem("gathered"), sem("gather_kept")
        gather_split, weights_made = sem("gather_split"), sem("weights_made")
        hot_turned, hot_kept = sem("hot_turned"), sem("hot_kept")
        e_turned, e_high, e_split = sem("e_turned"), sem("e_high"), sem("e_split")
        e_act, e_dve, e_out, e_kept = sem("e_act"), sem("e_dve"), sem("e_out"), sem("e_kept")
        scattered, added = sem("scattered"), sem("added")
        zeroed, zero_put = sem("zeroed"), sem("zero_put")
        pos_moved = sem("pos_moved")
        moe_added, fin_sq, fin_root, fin_made, stored = (
            sem("moe_added"), sem("fin_sq"), sem("fin_root"), sem("fin_made"), sem("stored"))
        act_steps, dve_steps, pool_steps = sem("act_steps"), sem("dve_steps"), sem("pool_steps")

        first = {("mix", 0): 0, ("ffn", 0): N_MIX, ("mix", 1): N_MIX + N_FFN, ("moe", 1): 2 * N_MIX + N_FFN}
        place, landed, before = {}, {}, {}
        uses, last_user = [0] * (FFN_RING + 1), [None] * (FFN_RING + 1)
        for phase, n, ring in ((("mix", 0), N_MIX, MIX_RING), (("ffn", 0), N_FFN, FFN_RING),
                               (("mix", 1), N_MIX, MIX_RING), (("moe", 1), N_FFN, FFN_RING)):
            for i in range(n):
                slot, s = i % ring, first[phase] + i
                if phase[0] == "mix":
                    slot = (MIX_EARLY if i % 4 == 3 else i % 4) if i < 16 else (i - 16) % ring
                uses[slot] += 1
                place[s], landed[s], before[s] = slot, 16 * uses[slot], last_user[slot]
                last_user[slot] = s
        E_LAPS = N_FFN // FFN_RING

        split_before = first

        def slab(slot):
            if slot == MIX_EARLY:
                return view(o_KBQ, SLAB)
            return arena[:, slot * SLAB:(slot + 1) * SLAB]

        def by_k(ap, n):
            return ap.rearrange("(k p) n -> p k n", p=P)

        def mix_source(L, i):
            if i < N_IN:
                return by_k(w_in[L, :, IN_SLABS[i]:IN_SLABS[i] + COLS], COLS), KT
            i -= N_IN
            if i < 4:
                w = (w_pa, w_pa, w_pb, w_pb)[i]
                return by_k(w[L, :, 512 * (i % 2):512 * (i % 2) + 512], 512), NT
            i -= 4
            return by_k(w_out[L, :, COLS * i:COLS * i + COLS], COLS), KT

        def ffn_source(wg, wu, wd, kind, j):
            if kind == "d":
                return by_k(wd[COLS * j:COLS * (j + 1), :], D), 2
            return by_k((wg if kind == "g" else wu)[:, COLS * j:COLS * (j + 1)], COLS), KT

        def load_rows(eng, L):
            rows = [(V_MU, tshift_mu[L], 14), (V_W0, w0[L], 4), (V_A0, a0[L], 4), (V_KK, k_k[L], 4),
                    (V_KA, k_a[L], 4), (V_RK, r_k[L], 4), (V_LG, lnx_g[L], 4), (V_LB, lnx_b[L], 4),
                    (V_N1, norm1_g[L], 8), (V_N2, norm2_g[L], 8), (V_GN, gdn_norm_g[L], 1)]
            for r, src, n in rows:
                eng.dma_start(vec_rows[r:r + n, :], src.rearrange("(t p) -> t p", p=P)).then_inc(rows_in[L], 16)
            eng.dma_start(vec_rows[V_CONV:V_CONV + 48, :],
                          conv_w[L].rearrange("j (t p) -> (j t) p", p=P)).then_inc(rows_in[L], 16)

        block = ctx.enter_context(nc.Block())

        @block.sync
        def _(sp):
            xv = x.rearrange("b (a p) d -> p (b a) d", p=P)
            sp.dma_start(x_tok_in, xv).then_inc(x_in, 16)

            def static(s, src, k):
                if before[s] is not None:
                    sp.wait_ge(slab_done, before[s] + 1)
                dst = slab(place[s]).rearrange("p (k n) -> p k n", k=k)
                sp.dma_start(dst, src).then_inc(slab_in[place[s]], 16)

            for L in range(DEPTH):
                for i in range(N_MIX):
                    if i == 3:
                        sp.wait_ge(summed, 2 * L + 1)
                    static(first["mix", L] + i, *mix_source(L, i))
                if L == 0:
                    for i, (kind, j) in enumerate(FFN_ORDER):
                        if i == MIX_RING:
                            sp.wait_ge(mixed, 4 * (L + 1))
                        static(first["ffn", 0] + i, *ffn_source(ffn_w_gate[0], ffn_w_up[0], ffn_w_down[0], kind, j))

            def experts(lap):
                s0 = first["moe", 1]
                with sp.Fori(0, NE) as e:
                    for i, (kind, j) in enumerate(FFN_ORDER):
                        slot = i % FFN_RING
                        sp.wait_ge(slab_done, e * N_FFN + (s0 + lap * NE * N_FFN + i - FFN_RING + 1))
                        src, k = ffn_source(moe_w_gate[0, e], moe_w_up[0, e], moe_w_down[0, e], kind, j)
                        sp.dma_start(slab(slot).rearrange("p (k n) -> p k n", k=k), src).then_inc(slab_in[slot], 16)

            sp.wait_ge(mixed, 8)
            experts(0)
            sp.wait_ge(over_made, 1)
            more = sp.value_load(over[0:1, 0:1])
            with sp.If(more > 0):
                experts(1)

            sp.wait_ge(fin_made, 2)
            ov = out.rearrange("b (a p) d -> p (b a) d", p=P)
            sp.dma_start(ov, x_tok_out).then_inc(stored, 16)
            sp.wait_ge(stored, 16)

        @block.gpsimd
        def _(pool):
            step = Chain(pool, pool_steps)
            keep = nc.gpsimd.affine_select
            step(nc.gpsimd.memset(ident[:], 1.0))
            step(keep(out=ident[:], in_=ident[:], pattern=[[-1, P]], compare_op=ALU.is_equal, fill=0.0,
                      base=0, channel_multiplier=1))
            step(nc.gpsimd.memset(ones[:], 1.0))
            for i, value in enumerate((NORM_EPS, P * 1e-6, GN_EPS, 1.0)):
                step(nc.gpsimd.memset(eps_b[:, i:i + 1], value))
            nc.gpsimd.memset(small[:], 0.0).then_inc(consts_made, 1)
            pool.wait_ge(consts_made, 1)
            for t in (head_ones, later, later_neg, blocks16, sel, restart):
                step(nc.gpsimd.memset(t[:], 0.0 if t is head_ones else 1.0))
            for tab, value in ((later, 1.0), (later_neg, -1.0)):
                step(nc.gpsimd.memset(tab[:, 0, :], value))
                step(keep(out=tab[:, 0, :], in_=tab[:, 0, :], pattern=[[1, P]], compare_op=ALU.is_gt, fill=0.0,
                          base=0, channel_multiplier=-1))
                step(keep(out=tab[:, 1, :], in_=tab[:, 1, :], pattern=[[1, P]], compare_op=ALU.is_ge, fill=0.0,
                          base=0, channel_multiplier=-1))
            b16 = blocks16[:].rearrange("p (b n) -> p b n", n=16)
            step(keep(out=b16, in_=b16, pattern=[[-16, 8], [0, 16]], compare_op=ALU.is_ge, fill=0.0,
                      base=0, channel_multiplier=1))
            step(keep(out=b16, in_=b16, pattern=[[16, 8], [0, 16]], compare_op=ALU.is_ge, fill=0.0,
                      base=15, channel_multiplier=-1))
            step(keep(out=sel[:], in_=sel[:], pattern=[[-1, GH], [0, P]], compare_op=ALU.is_equal, fill=0.0,
                      base=0, channel_multiplier=1))
            r3 = restart[:].rearrange("p (q n) -> p q n", q=8)
            step(nc.gpsimd.memset(r3[:, :, 0:1], 0.0))
            for hh in range(2):
                step(nc.gpsimd.memset(head_ones[64 * hh:64 * hh + 64, 64 * hh:64 * hh + 64], 1.0))
            nc.gpsimd.iota(slots[:], pattern=[[1, P]], base=0, channel_multiplier=0,
                           allow_small_or_imprecise_dtypes=True).then_inc(consts_made, 1)

            for L in range(DEPTH):
                if L:
                    pool.wait_ge(vec_turned, L)
                    load_rows(pool, L)
                if L == 0:
                    for i, src in enumerate((a_log, dt_bias)):
                        for l in range(DEPTH):
                            pool.dma_start(head_raw[:, i, l:l + 1],
                                           src[l].rearrange("(h a) -> h a", a=1)).then_inc(head_in, 16)
                else:
                    pool.wait_ge(lora_done, 3 * L)
                    pool.wait_ge(ab_split, 2 * L)
                pool.dma_start(lora_up[0:64, :], w_decay_up[L]).then_inc(small_in[L], 16)
                pool.dma_start(lora_up[64:128, :], w_iclr_up[L]).then_inc(small_in[L], 16)
                pool.dma_start(gate_up[:], w_gate_up[L]).then_inc(small_in[L], 16)
                pool.dma_start(w_ab[:], by_k(w_in[L, :, AB_BASE:AB_BASE + 2 * GH], 2 * GH)).then_inc(small_in[L], 16)
            pool.wait_ge(mixed, 8)
            pool.dma_start(w_router, by_k(moe_router[0], NE)).then_inc(router_in, 16)
            pool.dma_start(fin_g, final_g.rearrange("(a n) -> a n", a=1).broadcast_to([P, D])).then_inc(fin_in, 16)

        @block.tensor
        def _(pe):
            def mm(out, lhsT, rhs, start=True, stop=True, **kw):
                return nc.tensor.matmul(out, lhsT, rhs, start=start, stop=stop, **kw)

            def turn(out, src):
                n = src.shape[0]
                return nc.tensor.transpose(out, src, ident[0:n, 0:n])

            def split_mm(out, w_high, w_low, x_high, x_low, start=True, stop=True, **kw):
                mm(out, w_high, x_high, start, False, **kw)
                mm(out, w_high, x_low, False, False, **kw)
                return mm(out, w_low, x_high, False, stop, **kw)

            def norm(n):
                squares, bank = XSQ_ffn if n % 2 else XSQ, NORM_BANK[n]
                for k in range(KT):
                    if k % 2 == 0:
                        pe.wait_ge(squared, 4 * n + k // 2 + 1)
                    for a in range(2):
                        last = mm(ps[:, bank, a:a + 1], squares[:, k * T + a * P:k * T + (a + 1) * P], ones[:, 0:1],
                                  k == 0 and a == 0, k == KT - 1, skip_group_check=True)
                last.then_inc(summed, 1)
                pe.wait_ge(inverted, n + 1)
                for a in range(2):
                    last = mm(ps[:, bank, a * P:(a + 1) * P], norm_root[:, a:a + 1].broadcast_to([P, P]), ident[:])
                last.then_inc(root_spread, 1)

            def token_sums(src, bank, heads):
                table = head_ones[:, 0:P:P // heads] if heads > 1 else ones[:, 0:1]
                for q in range(8):
                    last = mm(ps[:, bank, heads * q:heads * (q + 1)], src[:, q * P:(q + 1) * P], table)
                return last

            def spread_roots(roots, banks_):
                for q in range(8):
                    w = (roots[:, q:q + 1].broadcast_to([P, P]) if roots.shape[1] == 8
                         else roots[:, q * P:(q + 1) * P])
                    last = mm(ps[:, banks_[q // 4], (q % 4) * P:(q % 4 + 1) * P], w, ident[:])
                return last

            def in_slab(L, o):
                if o >= 4:
                    if o - 4 < N_CONV:
                        pe.wait_ge(proj_dve, N_CONV * L + o - 3)
                    else:
                        pe.wait_ge(proj_act, N_IN * L + o - 3)
                pe.wait_ge(slab_split, split_before["mix", L] + o + 1)
                wh, wl = (w.rearrange("p (k n) -> p k n", k=KT) for w in (mix_high[o % 3], mix_low[place[first["mix", L] + o]]))
                for m in range(2):
                    cut = slice(m * P, (m + 1) * P)
                    for k in range(KT):
                        if o == 0 and m == 0 and k % 2 == 0:
                            pe.wait_ge(norm_split, 8 * L + k // 2 + 1)
                        last = split_mm(ps[:, o % 4, m * T:(m + 1) * T], wh[:, k, cut], wl[:, k, cut],
                                        mix_norm_high[:, k, :], mix_norm_low[:, k, :], k == 0, k == KT - 1)
                last.then_inc(slab_done, 1)

            def head_sums(table, src, bank):
                for i in range(2):
                    last = mm(ps[:, bank + i, :], table[:], src[:, i * 512:(i + 1) * 512])
                return last

            def project(L):
                norm(2 * L)
                pe.wait_ge(small_in[L], 64)
                pe.wait_ge(consts_made, 2)
                for o in range(9):
                    in_slab(L, o)
                pe.wait_ge(lora_acted, 2 * (L + 1))
                for lo, bank in ((0, 4), (64, 6)):
                    for t in range(NT):
                        last = mm(ps[:, bank + t // 2, (t % 2) * T:(t % 2 + 1) * T],
                                  lora_up[lo:lo + 64, t * P:(t + 1) * P], LO[lo:lo + 64, 0:T])
                    last.then_inc(lora_done, 1)
                in_slab(L, 9)
                in_slab(L, 10)
                pe.wait_ge(kk_squared, L + 1)
                pe.wait_ge(decay_sig, L + 1)
                token_sums(SQ, 4, 2).then_inc(kk_summed, 1)
                in_slab(L, 11)
                in_slab(L, 12)
                pe.wait_ge(rate_sig, L + 1)
                for t in range(NT):
                    last = mm(ps[:, 6 + t // 2, (t % 2) * T:(t % 2 + 1) * T],
                              gate_up[:, t * P:(t + 1) * P], LO[:, T:2 * T])
                last.then_inc(lora_done, 1)
                pe.wait_ge(kk_inverted, L + 1)
                spread_roots(SQ, (4, 5)).then_inc(kk_spread, 1)
                in_slab(L, 13)
                in_slab(L, 14)
                pe.wait_ge(kk_used, L + 1)
                pe.wait_ge(ab_split, 2 * (L + 1))
                for i in range(2):
                    for k in range(KT):
                        last = split_mm(ps[0:GH, 4, i * T:(i + 1) * T], w_ab_high[:, k, i * GH:(i + 1) * GH],
                                        w_ab_low[:, k, i * GH:(i + 1) * GH], mix_norm_high[:, k, :],
                                        mix_norm_low[:, k, :], k == 0, k == KT - 1)
                last.then_inc(ab_done, 1)
                for o in range(15, 17):
                    in_slab(L, o)
                pe.wait_ge(rk_ready, L + 1)
                pe.wait_ge(gate_kept, L + 1)
                head_sums(head_ones, SQ, 6).then_inc(rk_summed, 1)
                in_slab(L, 17)
                pe.wait_ge(qk_squared, 2 * L + 1)
                pe.wait_ge(ab_act, 3 * L + 3)
                pe.wait_ge(ab_dve, 3 * L + 1)
                token_sums(QSQ, 4, 1).then_inc(qk_summed, 1)
                in_slab(L, 18)
                pe.wait_ge(qk_squared, 2 * L + 2)
                pe.wait_ge(bonus_made, L + 1)
                token_sums(KSQ.rearrange("p q n -> p (q n)"), 6, 1).then_inc(qk_summed, 1)
                in_slab(L, 19)
                pe.wait_ge(qk_inverted, 2 * L + 1)
                spread_roots(q_root, (4, 5)).then_inc(qk_spread, 1)
                pe.wait_ge(qk_inverted, 2 * L + 2)
                spread_roots(k_root, (6, 7)).then_inc(qk_spread, 1)
                in_slab(L, 20)
                in_slab(L, 21)
                pe.wait_ge(qk_used, 2 * L + 2)
                pe.wait_ge(ab_dve, 3 * L + 3)
                for h in range(GH):
                    last = mm(ps[:, 4 + h, :], sel[:, h, :], GB)
                last.then_inc(spread, 1)
                in_slab(L, 22)
                pe.wait_ge(spread_kept, L + 1)
                for c in range(2):
                    last = mm(ps[:, 4, c * GH:(c + 1) * GH], GB[:, c * P:(c + 1) * P], ident[0:GH, 0:GH])
                last.then_inc(cols_turned, 1)

            def turn_tokens(L):
                pe.wait_ge(proj_act, N_IN * (L + 1))
                pe.wait_ge(rw_ready, L + 1)
                for c in range(2):
                    for t in range(NT):
                        turn(ps[:, c, t * P:(t + 1) * P], V3[:, t, c * P:(c + 1) * P])
                for bank, src in ((2, BH), (3, KH)):
                    for t in range(NT):
                        last = turn(ps[:, bank, t * P:(t + 1) * P], src[:, 2 * t, :])
                last.then_inc(rw_turned, 1)
                pe.wait_ge(vb_made, L + 1)
                for c in range(2):
                    for h in range(GH):
                        turn(ps[:, 5 + c, h * P:(h + 1) * P], V1[:, h * T + c * P:h * T + (c + 1) * P])
                for h in range(GH):
                    last = turn(ps[:, 7, h * P:(h + 1) * P], K1[:, h * T:h * T + P])
                last.then_inc(gdn_turned, 1)
                pe.wait_ge(rw_kept, L + 1)

            def groups(L):
                for pair in range(3):
                    rw = pair < 2
                    base = L * (2 * len(R_STEPS) + len(G_STEPS)) + pair * len(R_STEPS)
                    cbase = L * (2 * len(R_COPIES) + len(G_COPIES)) + pair * len(R_COPIES)
                    sbase = L * (2 * len(R_SUMS) + len(G_SUMS)) + pair * len(R_SUMS)
                    copies, sums = (RC_AT, RS_AT) if rw else (GC_AT, GS_AT)

                    def copied(s, what):
                        pe.wait_ge(mat_copied[s], cbase + copies[what])

                    def summed_(s, what):
                        pe.wait_ge(mat_summed[s], sbase + sums[what])

                    def products(s, bank, lhs, rhs):
                        for q in range(4):
                            last = mm(ps[:, 4 * s + bank, q * P:(q + 1) * P], lhs(q), rhs(q))
                        return last

                    def doubling(s, square, turned, add):
                        A = lambda q: DG[s][:, q, 0:P]
                        At = lambda q: DT[s][:, q, :]
                        Gm = lambda q: DG[s][:, q, P:2 * P]
                        if square:
                            products(s, 1, At, A)
                        if turned:
                            last = products(s, 2, A, At)
                        if add:
                            last = products(s, 3, At, Gm)
                        last.then_inc(mat_done[s], 1)

                    for s in range(2):
                        g = 2 * pair + s
                        if pair:
                            pbase = sbase - (len(R_SUMS))
                            pe.wait_ge(mat_summed[s], pbase + RS_AT["o"])
                        elif s == 1:
                            pe.wait_ge(gdn_kept, L + 1)
                            pe.wait_ge(gdn_keyed, L + 1)
                            pe.wait_ge(cols_kept, L + 1)
                        if pair == 2 and s == 0:
                            pe.wait_ge(gdn_ready, L + 1)
                        for q in range(4):
                            hh, c = q // 2, q % 2
                            dst = ps[:, 4 * s + q // 2, (q % 2) * T:(q % 2 + 1) * T]
                            if rw:
                                r = slice(64 * hh, 64 * hh + 64)
                                last = mm(dst, BH[r, 2 * g + c, :], AR[r, 2 * g + c, :, :])
                                last = mm(ps[:, 4 * s + 2 + q // 2, (q % 2) * T:(q % 2 + 1) * T],
                                          KH[r, 2 * g + c, :], AR[r, 2 * g + c, :, :])
                            else:
                                h = 2 * (g - 4) + hh
                                last = mm(dst, K1[:, h * T + c * P:h * T + (c + 1) * P], KBQ[:, 2 * h + c, :, :])
                        last.then_inc(mat_done[s], 1)
                    for s in range(2):
                        summed_(s, "d")
                        for q in range(4):
                            last = turn(ps[:, 4 * s, q * P:(q + 1) * P], DG[s][:, q, 0:P])
                        last.then_inc(mat_done[s], 1)
                    for s in range(2):
                        copied(s, "dT")
                        summed_(s, "masked")
                        doubling(s, True, True, False)
                    if not rw:
                        for i in range(2):
                            last = mm(ps[:, 4 * i, :], head_ones[:], KK[:, i * 512:(i + 1) * 512])
                        last.then_inc(hn_summed, 1)
                    for s in range(2):
                        copied(s, "sqT")
                        summed_(s, "base")
                        doubling(s, True, True, True)
                    for s in range(2):
                        copied(s, "gen1T")
                        summed_(s, "gen1")
                        doubling(s, False, True, True)
                    for s in range(2):
                        copied(s, "gen2T")
                        summed_(s, "gen2")
                        doubling(s, False, False, True)
                    if not rw:
                        pe.wait_ge(hn_dve, 4 * L + 1)
                    for s in range(2):
                        summed_(s, "last1")
                        for q in range(4):
                            last = turn(ps[:, 4 * s, q * P:(q + 1) * P], DG[s][:, q, P:2 * P])
                        last.then_inc(mat_done[s], 1)
                    for s in range(2):
                        copied(s, "gT")
                        products(s, 1, lambda q: DT[s][:, q, :], lambda q: MQ[s][:, q, 0:P])
                        products(s, 2, lambda q: MQ[s][:, q, 0:P], lambda q: DT[s][:, q, :]).then_inc(mat_done[s], 1)
                    for s in range(2):
                        copied(s, "mT")
                        doubling(s, True, True, True)
                    if not rw:
                        pe.wait_ge(hn_act, 4 * L + 1)
                        token_sums(SQ, 0, 2).then_inc(hn_summed, 1)
                    for s in range(2):
                        copied(s, "gen3T")
                        summed_(s, "gen3")
                        doubling(s, False, True, True)
                    for s in range(2):
                        copied(s, "gen4T")
                        summed_(s, "gen4")
                        doubling(s, False, False, True)
                    if not rw:
                        pe.wait_ge(hn_inverted, 2 * L + 1)
                        spread_roots(SQ, (0, 4)).then_inc(hn_spread, 1)

                    def heads(s):
                        g = 2 * pair + s
                        for hh in range(2):
                            if rw:
                                yield hh, slice(g * P + HD * hh, g * P + HD * (hh + 1)), slice(HD * hh, HD * (hh + 1)), HD
                            else:
                                h = 2 * (g - 4) + hh
                                yield hh, slice(h * P, (h + 1) * P), slice(0, P), P

                    def solve(s, c, rhs, what):
                        for hh, cols, rows, n in heads(s):
                            last = mm(ps[:, 4 * s + 1, hh * P:hh * P + n], DG[s][:, 2 * hh + c, P:2 * P], rhs(hh, cols, n))
                        last.then_inc(mat_done[s], 1)

                    if rw:
                        for s in range(2):
                            for hh, cols, rows, n in heads(s):
                                last = mm(ps[:, 4 * s + 2 * hh, 0:n], MK[s][:, 2 * hh, 0:P], TV[:, 0, cols])
                            last.then_inc(mat_done[s], 1)
                    for s in range(2):
                        summed_(s, "last2")
                        if rw:
                            copied(s, "z0")
                            solve(s, 0, lambda hh, cols, n: ZB[s][:, hh, 0:n], "u0")
                        else:
                            solve(s, 0, lambda hh, cols, n: TVB[:, 0, cols], "u0")
                    for s in range(2):
                        copied(s, "u0")
                        for hh, cols, rows, n in heads(s):
                            if rw:
                                dst = ps[rows, 4 * s + 2, 0:n]
                                mm(dst, TB[:, cols], UB[s][:, 2 * hh, 0:n], True, False)
                                last = mm(dst, TK[:, cols], TV[:, 0, cols], False, True)
                            else:
                                last = mm(ps[:, 4 * s + 2, hh * P:(hh + 1) * P], TKN[:, cols], UB[s][:, 2 * hh, :])
                        last.then_inc(mat_done[s], 1)
                    if not rw:
                        pe.wait_ge(hn_dve, 4 * L + 2)
                    for s in range(2):
                        g = 2 * pair + s
                        copied(s, "s")
                        for hh, cols, rows, n in heads(s):
                            dst = ps[:, 4 * s + 2 * hh, 0:n] if rw else ps[:, 4 * s, hh * P:hh * P + n]
                            if rw:
                                mm(dst, AR[rows, 2 * g + 1, 0, :], SB[s][rows, 0, 0:n], True, False)
                                last = mm(dst, MK[s][:, 2 * hh + 1, 0:P], TV[:, 1, cols], False, True)
                            else:
                                last = mm(dst, KG[:, cols], SB[s][:, hh, :])
                        last.then_inc(mat_done[s], 1)
                    for s in range(2):
                        if rw:
                            copied(s, "z1")
                        else:
                            summed_(s, "z1")
                        solve(s, 1, lambda hh, cols, n: ZB[s][:, hh, 0:n], "u1")
                    for s in range(2):
                        g = 2 * pair + s
                        copied(s, "u1")
                        for hh, cols, rows, n in heads(s):
                            for c in range(2):
                                q = 2 * hh + c
                                dst = ps[rows, 4 * s + 3, c * P:(c + 1) * P] if rw else \
                                    ps[:, 4 * s + 3, q * P:(q + 1) * P]
                                mm(dst, UB[s][:, q, 0:n], MQ[s][:, q, P:2 * P], True, not rw and c == 0)
                                if rw:
                                    mm(dst, TV[:, c, cols], MK[s][:, q, P:2 * P], False, c == 0)
                                if c == 1:
                                    if rw:
                                        last = mm(dst, SB[s][rows, 0, 0:n], AR[rows, 2 * g + 1, 1, :], False, True)
                                    else:
                                        last = mm(dst, SB[s][:, hh, :], QG[:, cols], False, True)
                        last.then_inc(mat_done[s], 1)

            def out_parts(L, f, k):
                pe.wait_ge(slab_split, split_before["mix", L] + N_IN + f + 1)
                return (w.rearrange("p (k n) -> p k n", k=k)
                        for w in (fin_high[f % 3], mix_low[place[first["mix", L] + N_IN + f]]))

            def finish_mixer(L):
                for s in range(2):
                    pe.wait_ge(mat_summed[s], (L + 1) * (2 * len(R_SUMS) + len(G_SUMS)))
                pe.wait_ge(hn_act, 4 * L + 3)
                token_sums(QSQ, 4, 1).then_inc(hn_summed, 1)
                for i, bank in ((0, 0), (1, 2), (2, 4), (3, 6)):
                    if i == 1:
                        pe.wait_ge(hn_inverted, 2 * L + 2)
                        spread_roots(gdn_root, (4, 5)).then_inc(hn_spread, 1)
                    if i % 2 == 0:
                        pe.wait_ge(branch_split, 4 * L + i // 2 + 1)
                    wh, wl = out_parts(L, i, NT)
                    sh, sl = (KK_high, KK_low) if i < 2 else (OG_high, OG_low)
                    for m in range(4):
                        cut = slice(m * P, (m + 1) * P)
                        for k in range(NT):
                            tok = slice(k * T, (k + 1) * T)
                            last = split_mm(ps[:, bank + m // 2, (m % 2) * T:(m % 2 + 1) * T], wh[:, k, cut], wl[:, k, cut],
                                            sh[:, tok], sl[:, tok], k == 0, k == NT - 1)
                    last.then_inc(slab_done, 1)
                for j, half in ((0, 0), (1, 0), (0, 1), (1, 1), (2, 0), (2, 1), (3, 0), (3, 1)):
                    if j == 0:
                        pe.wait_ge(branch_split, 4 * L + half + 3)
                    wh, wl = out_parts(L, 4 + j, KT)
                    for m in range(2):
                        cut = slice(m * P, (m + 1) * P)
                        for k in range(4 * half, 4 * half + 4):
                            tok = slice(k * T, (k + 1) * T)
                            last = split_mm(ps[:, j, m * T:(m + 1) * T], wh[:, k, cut], wl[:, k, cut],
                                            YT_high[:, tok], YT_low[:, tok], k == 0 and m == 0, k == KT - 1,
                                            skip_group_check=True)
                    if half:
                        last.then_inc(slab_done, 1)

            def dense(L):
                norm(2 * L + 1)
                s0 = first["ffn", L]
                for i, (kind, j) in enumerate(FFN_ORDER):
                    pe.wait_ge(slab_split, split_before["ffn", L] + i + 1)
                    wh, wl = high[i % HIGHS], low[i % FFN_RING]
                    if kind in "gu":
                        if j >= 2:
                            pe.wait_ge(ffn_dve, j - 1)
                        wh, wl = (w.rearrange("p (k n) -> p k n", k=KT) for w in (wh, wl))
                        for m in range(2):
                            cut = slice(m * P, (m + 1) * P)
                            for k in range(KT):
                                if i == 0 and m == 0 and k % 2 == 0:
                                    pe.wait_ge(norm_split, 8 * L + 4 + k // 2 + 1)
                                last = split_mm(ps[:, 2 * (j % 2) + (kind == "u"), m * T:(m + 1) * T],
                                                wh[:, k, cut], wl[:, k, cut], hT_high[:, k, :], hT_low[:, k, :],
                                                k == 0, k == KT - 1)
                    else:
                        pe.wait_ge(ffn_split, j + 1)
                        wh, wl = (w.rearrange("p (k n) -> p k n", k=2) for w in (wh, wl))
                        for m in range(KT):
                            cut = slice(m * P, (m + 1) * P)
                            for k in range(2):
                                tok = slice(k * T, (k + 1) * T)
                                last = split_mm(ps[:, 4 + m // 2, (m % 2) * T:(m % 2 + 1) * T],
                                                wh[:, k, cut], wl[:, k, cut], FH_high[:, j % 2, tok], FH_low[:, j % 2, tok],
                                                j == 0 and k == 0 and m % 2 == 0,
                                                j == FC - 1 and k == 1, skip_group_check=True)
                    last.then_inc(slab_done, 1)

            def gather():
                for k in range(KT):
                    for a in range(2):
                        for part in (h_tok_high, h_tok_low):
                            first_, last_ = a == 0 and part is h_tok_high, a == 1 and part is h_tok_low
                            last = mm(ps[:, k // 4, (k % 4) * P:(k % 4 + 1) * P],
                                      part[:, a, k * P:(k + 1) * P], PT[:, a, :], first_, last_)
                last.then_inc(gathered, 1)

            def scatter():
                for a in range(2):
                    for n in range(2):
                        last = mm(ps[:, 4 + 2 * a + n, :], PC[:, a * P:(a + 1) * P], YE[:, n * 512:(n + 1) * 512])
                    last.then_inc(scattered, 1)

            def turn_h(j):
                for m in range(2):
                    last = turn(ps[:, 6 + j % 2, m * P:(m + 1) * P], FH[:, m * P:(m + 1) * P])
                last.then_inc(e_turned, 1)

            def experts(lap):
                s0 = first["moe", 1] + lap * NE * N_FFN
                pe.wait_ge(hot_made, lap * (NE + 1) + 1)
                gather()
                pe.wait_ge(zeroed, lap + 1)
                for n in range(2):
                    last = mm(ps[:, 2 + n, :], ones[:], YE[:, n * 512:(n + 1) * 512])
                last.then_inc(zero_put, 1)
                with pe.Fori(0, NE) as e:
                    n_e = e + lap * NE
                    chunks = e * FC + lap * NE * FC
                    pe.wait_ge(gather_split, e + (lap * (NE + 1) + 1))
                    for i, (kind, j) in enumerate(FFN_ORDER):
                        if (kind, j) == ("u", 0):
                            pe.wait_ge(e_kept, e + (lap * (NE + 1) + 1))
                            scatter()
                            pe.wait_ge(added, 2 * e + (2 * lap * (NE + 1) + 1))
                        elif kind == "u":
                            if j == 1:
                                pe.wait_ge(weights_made, n_e + 1)
                                pe.wait_ge(added, 2 * e + (2 * lap * (NE + 1) + 2))
                                for a in range(2):
                                    last = turn(ps[:, 7, a * P:(a + 1) * P], PTC[:, a, :])
                                last.then_inc(hot_turned, 1)
                            if j == 2:
                                pe.wait_ge(hot_kept, n_e + 1)
                            pe.wait_ge(e_dve, chunks + j)
                            turn_h(j - 1)
                        elif (kind, j) == ("d", FC - 2):
                            pe.wait_ge(hot_made, e + (lap * (NE + 1) + 2))
                            pe.wait_ge(e_act, chunks + FC)
                            gather()
                            pe.wait_ge(e_dve, chunks + FC)
                            turn_h(FC - 1)
                        pe.wait_ge(slab_split, e * N_FFN + (split_before["moe", 1] + lap * NE * N_FFN + i + 1))
                        wh, wl = high[i % HIGHS], low[i % FFN_RING]
                        if kind in "gu":
                            if kind == "g" and j >= 2:
                                pe.wait_ge(e_dve, chunks + (j - 1))
                            wh, wl = (w.rearrange("p (k n) -> p k n", k=KT) for w in (wh, wl))
                            for k in range(KT):
                                last = split_mm(ps[:, j % 2 + 4 * (kind == "u"), 0:COLS],
                                                XS_high[:, k, :], XS_low[:, k, :], wh[:, k, :], wl[:, k, :],
                                                k == 0, k == KT - 1)
                        else:
                            pe.wait_ge(e_split, chunks + (j + 1))
                            wh, wl = (w.rearrange("p (k n) -> p k n", k=2) for w in (wh, wl))
                            for k in range(2):
                                hcut = slice(k * P, (k + 1) * P)
                                for n in range(2):
                                    cut = slice(n * 512, (n + 1) * 512)
                                    last = split_mm(ps[:, 2 + n, :], FH_high[:, j % 2, hcut], FH_low[:, j % 2, hcut],
                                                    wh[:, k, cut], wl[:, k, cut],
                                                    j == 0 and k == 0, j == FC - 1 and k == 1)
                        last.then_inc(slab_done, 1)
                pe.wait_ge(e_kept, (lap + 1) * (NE + 1))
                scatter()

            pe.wait_ge(consts_made, 1)
            pe.wait_ge(x_in, 16)
            for k in range(KT):
                for a in range(2):
                    last = turn(ps[:, k // 2, (k % 2) * T + a * P:(k % 2) * T + (a + 1) * P],
                                x_tok_in[:, a, k * P:(k + 1) * P])
            last.then_inc(x_turned, 1)
            for L in range(DEPTH):
                pe.wait_ge(rows_in[L], 16 * 12)
                turn(ps[:, VEC_BANK[L], 0:N_VEC], vec_rows[0:N_VEC, :]).then_inc(vec_turned, 1)
                project(L)
                turn_tokens(L)
                groups(L)
                finish_mixer(L)
                if L == 0:
                    dense(L)
            norm(3)
            def turn_channels(src):
                for k in range(KT):
                    for a in range(2):
                        last = turn(ps[:, 4 + 2 * a + k // 4, (k % 4) * P:(k % 4 + 1) * P], src[:, k, a * P:(a + 1) * P])
                last.then_inc(tok_turned, 1)

            turn_channels(xT)
            pe.wait_ge(normed, 16)
            pe.wait_ge(router_in, 16)
            for a in range(2):
                for k in range(KT):
                    last = mm(ps[:, 0, a * NE:(a + 1) * NE], hT[:, k, a * P:(a + 1) * P], w_router[:, k, :],
                              k == 0, k == KT - 1)
            last.then_inc(logits_done, 1)
            pe.wait_ge(tok_kept, 1)
            turn_channels(hT)
            pe.wait_ge(routed, 1)
            mm(ps[:, 1, 0:NE], later[:, 0, :], chosen[:, 0, :])
            mm(ps[:, 1, NE:2 * NE], later[:, 0, :], chosen[:, 1, :], True, False)
            mm(ps[:, 1, NE:2 * NE], ones[:], chosen[:, 0, :], False, True)
            mm(ps[:, 1, 2 * NE:3 * NE], ones[:], chosen[:, 0, :], True, False)
            mm(ps[:, 1, 2 * NE:3 * NE], ones[:], chosen[:, 1, :], False, True).then_inc(pos_done, 1)
            pe.wait_ge(norm_split, 13)
            experts(0)
            pe.wait_ge(over_made, 1)
            more = pe.value_load(over[0:1, 0:1])
            with pe.If(more > 0):
                experts(1)

        def banks(a, n):
            return ps[:, a:a + (n + 511) // 512, :].rearrange("p b n -> p (b n)")[:, 0:n]

        def group_bases(L, pair):
            return (L * (2 * len(R_STEPS) + len(G_STEPS)) + pair * len(R_STEPS),
                    L * (2 * len(R_COPIES) + len(G_COPIES)) + pair * len(R_COPIES),
                    L * (2 * len(R_SUMS) + len(G_SUMS)) + pair * len(R_SUMS))

        @block.scalar
        def _(act):
            step = Chain(act, act_steps)
            run = nc.scalar.activation

            def norm(n, ready, count, meanwhile=None):
                squares = XSQ_ffn if n % 2 else XSQ
                for q in range(4):
                    act.wait_ge(ready, count + q + 1)
                    run(squares[:, q * 512:(q + 1) * 512], xT[:, 2 * q:2 * q + 2, :], ACT.Square).then_inc(squared, 1)
                    if meanwhile and q == (2 if n % 2 else 3):
                        meanwhile()
                act.wait_ge(summed, n + 1)
                run(norm_root, ps[:, NORM_BANK[n], 0:2], ACT.Sqrt, bias=eps_b[:, 0:1],
                    scale=1.0 / D).then_inc(rooted, 1)

            def high_norm(n, dst):
                for q in range(4):
                    act.wait_ge(normed, 4 * n + q + 1)
                    run(dst[:, 2 * q:2 * q + 2, :], hT[:, 2 * q:2 * q + 2, :], ACT.Copy).then_inc(norm_high, 1)

            def high_in(L, i):
                s = first["mix", L] + i
                act.wait_ge(slab_in[place[s]], landed[s])
                if i >= 3:
                    act.wait_ge(slab_done, s - 3 + 1)
                run(mix_high[i % 3], slab(place[s]), ACT.Copy).then_inc(slab_high, 1)

            def high_out(L, f):
                s = first["mix", L] + N_IN + f
                act.wait_ge(slab_in[place[s]], landed[s])
                if f >= 3:
                    act.wait_ge(slab_done, s - 3 + 1)
                run(fin_high[f % 3], slab(place[s]), ACT.Copy).then_inc(slab_high, 1)

            def in_slab(L, o):
                act.wait_ge(slab_done, first["mix", L] + o + 1)
                src = ps[:, o % 4, :]
                if o < N_CONV:
                    for m in range(2):
                        if o < 7:
                            t = IN_SLABS[o] // P + m
                            dst, scale = shifted(t), one_less_mu[:, L, t:t + 1]
                        else:
                            i = 2 * (o - 7) + m
                            dst, scale = QKV[:, i * T:(i + 1) * T], vec[:, L, V_CONV + 36 + i:V_CONV + 37 + i]
                        last = run(dst, src[:, m * T:(m + 1) * T], ACT.Copy, scale=scale)
                elif o < 15:
                    last = run(Z[:, (o - 13) * 512:(o - 12) * 512], src, ACT.Silu)
                else:
                    last = run(GATES[:, (o - 15) * 512:(o - 14) * 512], src, ACT.Sigmoid)
                last.then_inc(proj_act, 1)
                if o + 3 < N_IN:
                    high_in(L, o + 3)

            def project(L):
                norm(2 * L, ffn_added if L else x_kept, 0, lambda: high_in(L, 0))
                high_norm(2 * L, mix_norm_high)
                high_in(L, 1)
                high_in(L, 2)
                act.wait_ge(small_in[L], 64)
                run(w_ab_high[:], w_ab[:], ACT.Copy).then_inc(ab_split, 1)
                for o in range(3):
                    in_slab(L, o)
                act.wait_ge(proj_dve, N_CONV * L + 1)
                run(LO[0:64, 0:T], LO[0:64, 0:T], ACT.Tanh).then_inc(lora_acted, 1)
                run(LO[:, T:2 * T], LO[:, T:2 * T], ACT.Sigmoid).then_inc(lora_acted, 1)
                for o in range(3, 9):
                    in_slab(L, o)
                act.wait_ge(lora_done, 3 * L + 1)
                for t in range(NT):
                    src = ps[:, 4 + t // 2, (t % 2) * T:(t % 2 + 1) * T].rearrange("p (c n) -> p c n", c=2)
                    last = run(LC[:, 2 * t:2 * t + 2, 1:129], src, ACT.Sigmoid, bias=vec[:, L, V_W0 + t:V_W0 + t + 1])
                last.then_inc(decay_sig, 1)
                act.wait_ge(lora_done, 3 * L + 2)
                for t in range(NT):
                    last = run(A3[:, t, :], ps[:, 6 + t // 2, (t % 2) * T:(t % 2 + 1) * T], ACT.Sigmoid,
                               bias=vec[:, L, V_A0 + t:V_A0 + t + 1])
                last.then_inc(rate_sig, 1)
                act.wait_ge(kk_made, L + 1)
                run(SQ, KK, ACT.Square).then_inc(kk_squared, 1)
                in_slab(L, 9)
                in_slab(L, 10)
                act.wait_ge(log_decay, L + 1)
                run(view(o_EP, 1032), view(o_LC, 1032), ACT.Exp, scale=-DECAY_C).then_inc(decays, 1)
                run(view(o_EM, 1032), view(o_LC, 1032), ACT.Exp, scale=DECAY_C).then_inc(decays, 1)
                act.wait_ge(kk_summed, L + 1)
                run(kk_root, ps[:, 4, 0:16], ACT.Sqrt, bias=eps_b[:, 0:1]).then_inc(kk_rooted, 1)
                in_slab(L, 11)
                in_slab(L, 12)
                act.wait_ge(lora_done, 3 * L + 3)
                run(G, banks(6, 1024), ACT.Copy).then_inc(gate_kept, 1)
                in_slab(L, 13)
                act.wait_ge(proj_dve, N_CONV * (L + 1))
                for i in range(3):
                    last = run(QKV[:, i * 1024:(i + 1) * 1024], QKV[:, i * 1024:(i + 1) * 1024], ACT.Silu)
                    last.then_inc(silu_done, 1)
                in_slab(L, 14)
                in_slab(L, 15)
                act.wait_ge(ab_dve, 3 * L + 1)
                step(run(g4[:, 1, :], g4[:, 0, :], ACT.Abs))
                run(g4[:, 1, :], g4[:, 1, :], ACT.Exp, scale=-1.0).then_inc(ab_act, 1)
                act.wait_ge(ab_dve, 3 * L + 2)
                run(g4[:, 3, :], g4[:, 2, :], ACT.Ln).then_inc(ab_act, 1)
                run(GB[:, T:2 * T], ps[0:GH, 4, T:2 * T], ACT.Sigmoid).then_inc(ab_act, 1)
                act.wait_ge(silu_done, 3 * L + 2)
                run(QSQ, Q1, ACT.Square).then_inc(qk_squared, 1)
                run(KSQ, K1.rearrange("p (q n) -> p q n", q=4), ACT.Square).then_inc(qk_squared, 1)
                in_slab(L, 16)
                in_slab(L, 17)
                act.wait_ge(qk_summed, 2 * L + 1)
                run(q_root, ps[:, 4, 0:8], ACT.Sqrt, bias=eps_b[:, 1:2], scale=float(P)).then_inc(qk_rooted, 1)
                in_slab(L, 18)
                act.wait_ge(qk_summed, 2 * L + 2)
                run(k_root, ps[:, 6, 0:8], ACT.Sqrt, bias=eps_b[:, 0:1]).then_inc(qk_rooted, 1)
                in_slab(L, 19)
                in_slab(L, 20)
                in_slab(L, 21)
                act.wait_ge(spread, L + 1)
                act.wait_ge(rw_ready, L + 1)
                step(run(BG, ps[:, 4:8, 0:T], ACT.Copy))
                run(BB, ps[:, 4:8, T:2 * T], ACT.Copy).then_inc(spread_kept, 1)
                in_slab(L, 22)
                run(EG, BG, ACT.Exp).then_inc(kdec_made, 1)
                act.wait_ge(kdec_arg, L + 1)
                run(kdec, kdec, ACT.Exp).then_inc(kdec_made, 1)
                act.wait_ge(dd_made, L + 1)
                run(DD, DD, ACT.Exp).then_inc(dd_exp, 1)

            def turn_tokens(L):
                act.wait_ge(rw_turned, L + 1)
                run(TV, ps[:, 0:2, :], ACT.Copy)
                run(TB, ps[:, 2, :], ACT.Copy)
                run(TK, ps[:, 3, :], ACT.Copy).then_inc(rw_kept, 1)
                act.wait_ge(gdn_turned, L + 1)
                run(TVB, ps[:, 5:7, :], ACT.Copy).then_inc(gdn_kept, 1)

            def groups(L):
                for pair in range(3):
                    rw = pair < 2
                    base, _, _ = group_bases(L, pair)
                    steps = R_AT if rw else G_AT

                    def copy(s, what, dst, src, scale=None):
                        act.wait_ge(mat_done[s], base + steps[what])
                        if scale is None:
                            run(dst, src, ACT.Copy).then_inc(mat_copied[s], 1)
                        else:
                            run(dst, src, ACT.Copy, scale=scale).then_inc(mat_copied[s], 1)

                    def bank(s, b):
                        return ps[:, 4 * s + b, :].rearrange("p (q n) -> p q n", q=4)

                    def turned(s, what):
                        copy(s, what, DT[s], bank(s, 0))

                    def both(s, what):
                        if what not in ("gen2", "gen4"):
                            copy(s, what, DG[s][:, :, 0:P], bank(s, 1))
                        copy(s, what, DT[s], bank(s, 2))

                    for what in ("dT", "sq", "gen1", "gen2", "gT", "m", "gen3", "gen4"):
                        for s in range(2):
                            if what == "sq":
                                act.wait_ge(mat_summed[s], group_bases(L, pair)[2] + RS_AT["base"])
                            (turned if what in ("dT", "gT") else both)(s, what)
                        if not rw and what == "gen2":
                            act.wait_ge(hn_dve, 4 * L + 1)
                            run(SQ, KK, ACT.Square).then_inc(hn_act, 1)
                        if not rw and what == "gT":
                            high_out(L, 0)
                        if not rw and what == "gen3":
                            act.wait_ge(hn_summed, 3 * L + 2)
                            run(dev_root, ps[:, 0, 0:16], ACT.Sqrt, bias=eps_b[:, 2:3],
                                scale=1.0 / HD).then_inc(hn_act, 1)
                    n = HD if rw else P

                    def narrow(s, b):
                        return ps[:, 4 * s + b, 0:2 * P].rearrange("p (q n) -> p q n", q=2)[:, :, 0:n]

                    if rw:
                        for s in range(2):
                            copy(s, "z0", ZB[s][:, :, 0:n], ps[:, 4 * s:4 * s + 3:2, 0:n])
                    for s in range(2):
                        copy(s, "u0", UB[s].rearrange("p (h c) n -> p h c n", c=2)[:, :, 0, 0:n], narrow(s, 1))
                    for s in range(2):
                        if rw:
                            g = 2 * pair + s
                            copy(s, "s", SB[s][:, 0, 0:HD], ps[:, 4 * s + 2, 0:HD], scol[:, g:g + 1])
                        else:
                            copy(s, "s", SB[s], narrow(s, 2))
                    if rw:
                        for s in range(2):
                            copy(s, "z1", ZB[s][:, :, 0:n], ps[:, 4 * s:4 * s + 3:2, 0:n])
                    for s in range(2):
                        copy(s, "u1", UB[s].rearrange("p (h c) n -> p h c n", c=2)[:, :, 1, 0:n], narrow(s, 1))

            def finish_mixer(L):
                act.wait_ge(hn_dve, 4 * L + 3)
                run(KK_high, KK, ACT.Copy).then_inc(branch_high, 1)
                sums = (L + 1) * (2 * len(R_SUMS) + len(G_SUMS))
                act.wait_ge(mat_summed[0], sums)
                act.wait_ge(mat_summed[1], sums)
                run(QSQ, OG, ACT.Square).then_inc(hn_act, 1)
                act.wait_ge(hn_summed, 3 * L + 3)
                run(gdn_root, ps[:, 4, 0:8], ACT.Sqrt, bias=eps_b[:, 0:1], scale=1.0 / P).then_inc(hn_act, 1)
                high_out(L, 1)
                high_out(L, 2)
                act.wait_ge(hn_dve, 4 * L + 4)
                run(OG_high, OG, ACT.Copy).then_inc(branch_high, 1)
                high_out(L, 3)
                high_out(L, 4)
                for half in range(2):
                    if half:
                        high_out(L, 6)
                    cut = slice(half * 1024, (half + 1) * 1024)
                    act.wait_ge(merged, 2 * L + half + 1)
                    run(YT_high[:, cut], YT[:, cut], ACT.Copy).then_inc(branch_high, 1)
                    if not half:
                        high_out(L, 5)
                high_out(L, 7)

            def dense(L):
                s0 = first["ffn", L]

                def make_high(i):
                    act.wait_ge(slab_in[place[s0 + i]], landed[s0 + i])
                    if i >= HIGHS:
                        act.wait_ge(slab_done, s0 + i - HIGHS + 1)
                    run(high[i % HIGHS], slab(place[s0 + i]), ACT.Copy).then_inc(slab_high, 1)

                norm(2 * L + 1, mixed, 4 * L, lambda: make_high(0))
                high_norm(2 * L + 1, hT_high)
                make_high(1)
                make_high(2)
                for i, (kind, j) in enumerate(FFN_ORDER):
                    if kind == "g":
                        act.wait_ge(slab_done, s0 + i + 1)
                        if j >= 2:
                            act.wait_ge(ffn_dve, j - 1)
                        run(FG[:, j % 2, :], ps[:, 2 * (j % 2), :], ACT.Silu).then_inc(ffn_act, 1)
                    if i + HIGHS < N_FFN:
                        make_high(i + HIGHS)
                    if kind == "u":
                        act.wait_ge(ffn_dve, j + 1)
                        run(FH_high[:, j % 2, :], FH, ACT.Copy).then_inc(ffn_high, 1)

            def experts(lap):
                s0 = first["moe", 1] + lap * NE * N_FFN

                def keep_tokens(e):
                    act.wait_ge(gathered, e + (lap * (NE + 1) + 1))
                    run(XS_high, ps[:, 0:2, :].rearrange("p b (k n) -> p (b k) n", n=P), ACT.Copy).then_inc(gather_kept, 1)

                keep_tokens(0)
                act.wait_ge(zero_put, lap + 1)
                with act.Fori(0, NE) as e:
                    n_e = e + lap * NE
                    chunks = e * FC + lap * NE * FC

                    def make_high(i):
                        slot = i % FFN_RING
                        act.wait_ge(slab_in[slot], e * (16 * E_LAPS)
                                    + (16 * (uses[slot] - E_LAPS + i // FFN_RING + 1 + lap * NE * E_LAPS)))
                        act.wait_ge(slab_done, e * N_FFN + (s0 + i - HIGHS + 1))
                        run(high[i % HIGHS], slab(slot), ACT.Copy).then_inc(slab_high, 1)

                    def keep_h(j):
                        act.wait_ge(e_turned, chunks + (j + 1))
                        run(FH_high[:, j % 2, 0:T], ps[:, 6 + j % 2, 0:T], ACT.Copy).then_inc(e_high, 1)

                    make_high(0)
                    make_high(1)
                    act.wait_ge(slab_done, e * N_FFN + s0)
                    run(YE, banks(2, 1024), ACT.Copy).then_inc(e_kept, 1)
                    make_high(2)
                    for i, (kind, j) in enumerate(FFN_ORDER):
                        if kind == "g":
                            act.wait_ge(slab_done, e * N_FFN + (s0 + i + 1))
                            if j >= 2:
                                act.wait_ge(e_dve, chunks + (j - 1))
                            run(FG[:, j % 2, 0:T], ps[:, j % 2, 0:T], ACT.Silu).then_inc(e_act, 1)
                            if j:
                                keep_h(j - 1)
                        if i + HIGHS < N_FFN:
                            make_high(i + HIGHS)
                        if (kind, j) == ("g", 1):
                            act.wait_ge(hot_turned, n_e + 1)
                            run(PC, ps[:, 7, 0:2 * P], ACT.Copy).then_inc(hot_kept, 1)
                    keep_tokens(e + 1)
                    keep_h(FC - 1)
                act.wait_ge(slab_done, s0 + NE * N_FFN)
                run(YE, banks(2, 1024), ACT.Copy).then_inc(e_kept, 1)

            def shifted(t):
                if t >= 12:
                    return LO[:, (t - 12) * T:(t - 11) * T]
                return (R3, K3, V3)[t // NT][:, t % NT, :]

            load_rows(act, 0)
            act.wait_ge(consts_made, 1)
            act.wait_ge(x_turned, 1)
            for q in range(4):
                run(xT[:, 2 * q:2 * q + 2, :], ps[:, q, :].rearrange("p (k n) -> p k n", k=2), ACT.Copy).then_inc(x_kept, 1)
            for L in range(DEPTH):
                act.wait_ge(vec_turned, L + 1)
                run(vec[:, L, :], ps[:, VEC_BANK[L], 0:N_VEC], ACT.Copy).then_inc(vec_kept, 1)
                act.wait_ge(vec_kept, 2 * L + 2)
                if L == 0:
                    act.wait_ge(head_in, 16 * 2 * DEPTH)
                    step(run(minus_a[:], head_raw[:, 0, :], ACT.Exp))
                    run(minus_a[:], minus_a[:], ACT.Copy, scale=-1.0)
                project(L)
                turn_tokens(L)
                groups(L)
                finish_mixer(L)
                if L == 0:
                    dense(L)
            norm(3, mixed, 4)
            act.wait_ge(tok_turned, 1)
            run(x_tok.rearrange("p a n -> p (a n)"), banks(4, 2048), ACT.Copy).then_inc(tok_kept, 1)
            act.wait_ge(tok_turned, 2)
            run(h_tok_high.rearrange("p a n -> p (a n)"), banks(4, 2048), ACT.Copy).then_inc(tok_kept, 1)
            act.wait_ge(diff_made, 1)
            run(g_exp, g_diff, ACT.Exp).then_inc(exp_made, 1)
            experts(0)
            act.wait_ge(over_made, 1)
            more = act.value_load(over[0:1, 0:1])
            with act.If(more > 0):
                experts(1)
            act.wait_ge(moe_added, 1)
            for a in range(2):
                step(run(x_sq[:, a, :], x_tok[:, a, :], ACT.Square, accum_out=xsum[:, a:a + 1]))
            run(xsum, xsum, ACT.Sqrt, bias=eps_b[:, 0:1], scale=1.0 / D).then_inc(fin_root, 1)

        @block.vector
        def _(dve):
            step = Chain(dve, dve_steps)
            tt, ts, stt = nc.vector.tensor_tensor, nc.vector.tensor_scalar, nc.vector.scalar_tensor_tensor

            def v_at(L, at_, n=1):
                return vec[:, L, at_:at_ + n]

            def per_tile(L, at_):
                return vec[:, L, at_:at_ + NT].unsqueeze(2).broadcast_to([P, NT, T])

            def by_channel(dst, roots):
                return nc.vector.tensor_copy(dst.rearrange("p (q n) -> p q n", n=HD),
                                             roots.unsqueeze(2).broadcast_to([P, 16, HD]))

            def by_tile(ap):
                return ap.rearrange("p (t n) -> p t n", t=NT)

            def by_chunk(ap):
                return ap.rearrange("p (q n) -> p q n", q=8)

            def less_high(dst, src, high_part):
                return tt(dst, src, high_part.bitcast(F32), ALU.subtract)

            def norm(n, at_, high_part=None, low_part=None):
                dve.wait_ge(rooted, n + 1)
                nc.vector.reciprocal(norm_root, norm_root).then_inc(inverted, 1)
                dve.wait_ge(root_spread, n + 1)
                root = ps[:, NORM_BANK[n], 0:T]

                def low(q):
                    dve.wait_ge(norm_high, 4 * n + q + 1)
                    cut = slice(2 * q, 2 * q + 2)
                    less_high(low_part[:, cut, :], hT[:, cut, :], high_part[:, cut, :]).then_inc(norm_split, 1)

                for q in range(4):
                    for k in (2 * q, 2 * q + 1):
                        g = vec[:, n // 2, at_ + k:at_ + k + 1]
                        last = stt(hT[:, k, :], xT[:, k, :], g, root, ALU.mult, ALU.mult)
                    last.then_inc(normed, 1)
                    if high_part is not None and q:
                        low(q - 1)
                if high_part is not None:
                    low(3)

            def low_in(L, i):
                dve.wait_ge(slab_high, split_before["mix", L] + i + 1)
                at_ = place[first["mix", L] + i]
                less_high(mix_low[at_], slab(at_), mix_high[i % 3]).then_inc(slab_split, 1)

            def low_out(L, f):
                dve.wait_ge(slab_high, split_before["mix", L] + N_IN + f + 1)
                at_ = place[first["mix", L] + N_IN + f]
                less_high(mix_low[at_], slab(at_), fin_high[f % 3]).then_inc(slab_split, 1)

            def in_slab(L, o):
                dve.wait_ge(proj_act, N_IN * L + o + 1)
                for m in range(2):
                    src = ps[:, o % 4, m * T:(m + 1) * T]
                    if o < 7:
                        t = IN_SLABS[o] // P + m
                        dst = (LO[:, (t - 12) * T:(t - 11) * T] if t >= 12 else (R3, K3, V3)[t // NT][:, t % NT, :])
                        last = stt(dst[:, 1:T], src[:, 0:T - 1], v_at(L, V_MU + t), dst[:, 1:T], ALU.mult, ALU.add)
                if o >= 7:
                    for back in range(1, 4):
                        for m in range(2):
                            src = ps[:, o % 4, m * T:(m + 1) * T]
                            i = 2 * (o - 7) + m
                            dst = QKV[:, i * T + back:(i + 1) * T]
                            last = stt(dst, src[:, 0:T - back], v_at(L, V_CONV + (3 - back) * 12 + i), dst,
                                       ALU.mult, ALU.add)
                            if back < 3:
                                step.mark(last)
                        if back < 3:
                            dve.wait_ge(dve_steps, step.n)
                last.then_inc(proj_dve, 1)
                low_in(L, o + 3)

            def project(L):
                low_in(L, 0)
                norm(2 * L, V_N1, mix_norm_high, mix_norm_low)
                low_in(L, 1)
                low_in(L, 2)
                dve.wait_ge(consts_made, 2)
                dve.wait_ge(ab_split, 2 * L + 1)
                less_high(w_ab_low[:], w_ab[:], w_ab_high[:]).then_inc(ab_split, 1)
                step.mark(nc.vector.memset(LC[:, :, 0:1], 0.0))
                for o in range(7):
                    in_slab(L, o)
                dve.wait_ge(proj_dve, N_CONV * L + 7)
                tt(by_tile(KK), K3, per_tile(L, V_KK), ALU.mult).then_inc(kk_made, 1)
                in_slab(L, 7)
                in_slab(L, 8)
                dve.wait_ge(decay_sig, L + 1)
                flat = view(o_LC, 1032)
                step(nc.vector.tensor_tensor_scan(flat, restart[:], flat, 0.0, ALU.mult, ALU.add))
                step(nc.vector.tensor_copy(mid, LC[:, :, 64]))
                tt(LC, LC, mid.unsqueeze(2).broadcast_to([P, 8, 129]), ALU.subtract).then_inc(log_decay, 1)
                in_slab(L, 9)
                in_slab(L, 10)
                dve.wait_ge(kk_rooted, L + 1)
                step(nc.vector.reciprocal(kk_root, kk_root))
                by_channel(SQ, kk_root).then_inc(kk_inverted, 1)
                in_slab(L, 11)
                in_slab(L, 12)
                dve.wait_ge(kk_spread, L + 1)
                tt(KK, KK, banks(4, 1024), ALU.mult).then_inc(kk_used, 1)
                dve.wait_ge(kk_used, L + 1)
                dve.wait_ge(rate_sig, L + 1)
                for t in range(NT):
                    last = ts(SQ[:, t * T:(t + 1) * T], A3[:, t, :], -1.0, v_at(L, V_KA + t), ALU.add, ALU.mult)
                step(last)
                step.mark(stt(by_tile(K3_flat), by_tile(SQ), 1.0, K3, ALU.add, ALU.mult))
                dve.wait_ge(decays, 2 * L + 2)
                stt(AR[:, :, 0, :], by_chunk(KK), -1.0, EP[:, :, 0:P], ALU.mult, ALU.mult)
                tt(AR[:, :, 1, :], by_chunk(view(o_R, 1024)), EP[:, :, 1:129], ALU.mult)
                low_in(L, 16)
                step(tt(BH, by_chunk(KK), by_chunk(view(o_A, 1024)), ALU.mult))
                tt(scol, EP[:, 0::2, P], EM[:, 1::2, 0], ALU.mult)
                tt(BH, BH, EM[:, :, 1:129], ALU.mult)
                tt(KH, by_chunk(K3_flat), EM[:, :, 1:129], ALU.mult).then_inc(rw_ready, 1)
                step(tt(SQ, view(o_R, 1024), K3_flat, ALU.mult))
                tt(by_tile(SQ), by_tile(SQ), per_tile(L, V_RK), ALU.mult).then_inc(rk_ready, 1)
                low_in(L, 17)
                low_in(L, 18)
                dve.wait_ge(ab_done, L + 1)
                dve.wait_ge(head_in, 16 * 2 * DEPTH)
                ts(g4[:, 0, :], ps[0:GH, 4, 0:T], head_raw[:, 1, L:L + 1], None, ALU.add).then_inc(ab_dve, 1)
                dve.wait_ge(ab_act, 3 * L + 1)
                ts(g4[:, 2, :], g4[:, 1, :], 1.0, None, ALU.add).then_inc(ab_dve, 1)
                dve.wait_ge(ab_dve, 3 * L + 2)
                step.mark(nc.vector.reciprocal(g4[:, 4, :], g4[:, 2, :]))
                dve.wait_ge(ab_act, 3 * L + 2)
                step(ts(g4[:, 2, :], g4[:, 2, :], -1.0, None, ALU.add))
                step(tt(g4[:, 2, :], g4[:, 1, :], g4[:, 2, :], ALU.subtract))
                step(tt(g4[:, 2, :], g4[:, 2, :], g4[:, 4, :], ALU.mult))
                step(tt(g4[:, 2, :], g4[:, 2, :], g4[:, 3, :], ALU.add))
                step(stt(g4[:, 2, :], g4[:, 0, :], 0.0, g4[:, 2, :], ALU.max, ALU.add))
                step(ts(g4[:, 2, :], g4[:, 2, :], minus_a[:, L:L + 1], None, ALU.mult))
                for c in range(2):
                    last = nc.vector.tensor_tensor_scan(GB[:, c * P:(c + 1) * P], ones[0:GH, :],
                                                        g4[:, 2, c * P:(c + 1) * P], 0.0, ALU.mult, ALU.add)
                last.then_inc(ab_dve, 1)
                low_in(L, 19)
                dve.wait_ge(rk_summed, L + 1)
                tt(view(o_R, 1024), banks(6, 1024), view(o_V, 1024), ALU.mult).then_inc(bonus_made, 1)
                low_in(L, 20)
                dve.wait_ge(qk_rooted, 2 * L + 1)
                nc.vector.reciprocal(q_root, q_root).then_inc(qk_inverted, 1)
                low_in(L, 21)
                dve.wait_ge(qk_rooted, 2 * L + 2)
                nc.vector.reciprocal(k_root, k_root).then_inc(qk_inverted, 1)
                dve.wait_ge(qk_spread, 2 * L + 1)
                tt(KBQ[:, :, 1, :], by_chunk(Q1), by_chunk(banks(4, 1024)), ALU.mult).then_inc(qk_used, 1)
                low_in(L, 22)
                dve.wait_ge(qk_spread, 2 * L + 2)
                tt(K1, K1, banks(6, 1024), ALU.mult).then_inc(qk_used, 1)
                dve.wait_ge(qk_used, 2 * L + 2)
                dve.wait_ge(spread_kept, L + 1)
                tt(KBQ[:, :, 0, :], by_chunk(K1), by_chunk(view(o_EM, 1024)), ALU.mult)
                dve.wait_ge(silu_done, 3 * L + 3)
                tt(V1, V1, view(o_EM, 1024), ALU.mult).then_inc(vb_made, 1)
                dve.wait_ge(cols_turned, L + 1)
                nc.vector.tensor_copy(gcol, ps[:, 4, 0:2 * GH].rearrange("p (c h) -> p c h", c=2)).then_inc(cols_kept, 1)
                dve.wait_ge(cols_kept, L + 1)
                tt(kdec, BG[:, :, P - 1], gcol[:, 0, :], ALU.subtract).then_inc(kdec_arg, 1)
                for h in range(GH):
                    for c in range(2):
                        last = ts(DD[:, 2 * h + c, :], BG[:, h, c * P:(c + 1) * P], gcol[:, c, h:h + 1], 0.0,
                                  ALU.subtract, ALU.min)
                last.then_inc(dd_made, 1)

            def turn_tokens(L):
                dve.wait_ge(kdec_made, 2 * L + 2)
                dve.wait_ge(gdn_turned, L + 1)
                src = ps[:, 7, :].rearrange("p (h n) -> p h n", h=GH)
                tt(TKN.rearrange("p (h n) -> p h n", h=GH), src, kdec.unsqueeze(2).broadcast_to([P, GH, P]),
                   ALU.mult).then_inc(gdn_keyed, 1)

            def ready_gdn(L):
                late = slice(P, 2 * P)
                kb = KBQ.rearrange("p (h c) s n -> p h c s n", c=2)
                stt(KG.rearrange("p (h n) -> p h n", h=GH), kb[:, :, 1, 0, :], -1.0, EG[:, :, late], ALU.mult, ALU.mult)
                tt(QG.rearrange("p (h n) -> p h n", h=GH), kb[:, :, 1, 1, :], EG[:, :, late], ALU.mult)
                dve.wait_ge(dd_exp, L + 1)
                dve.wait_ge(rw_turned, L + 1)
                tt(DM, DD.unsqueeze(2).broadcast_to([P, 8, 2, P]),
                   later_neg[:].unsqueeze(1).broadcast_to([P, 8, 2, P]), ALU.mult).then_inc(gdn_ready, 1)

            def groups(L):
                for pair in range(3):
                    rw = pair < 2
                    base, _, _ = group_bases(L, pair)
                    steps = R_AT if rw else G_AT
                    if pair == 2:
                        dve.wait_ge(gdn_ready, L + 1)
                    flat_mask = later[:].rearrange("p s n -> p (s n)")

                    def masked(s, dst, b):
                        g = 2 * pair + s
                        src = ps[:, 4 * s + b:4 * s + b + 2, :].rearrange("p b (q n) -> p (b q) n", q=2)
                        if rw:
                            mask = flat_mask.unsqueeze(1).broadcast_to([P, 4, 2 * P])
                        else:
                            mask = DM[:, 4 * (g - 4):4 * (g - 4) + 4, :, :].rearrange("p q s n -> p q (s n)")
                        return tt(dst, src, mask, ALU.mult)

                    for s in range(2):
                        dve.wait_ge(mat_done[s], base + 1)
                        Q, A, Gm = MQ[s][:, :, 0:P], DG[s][:, :, 0:P], DG[s][:, :, P:2 * P]
                        step(masked(s, MQ[s], 0))
                        tt(A, Q, blocks16[:].unsqueeze(1).broadcast_to([P, 4, P]), ALU.mult).then_inc(mat_summed[s], 1)
                        if rw:
                            masked(s, MK[s], 2).then_inc(mat_summed[s], 1)
                    for s in range(2):
                        Q, A, Gm = MQ[s][:, :, 0:P], DG[s][:, :, 0:P], DG[s][:, :, P:2 * P]
                        sums = L * (2 * len(R_SUMS) + len(G_SUMS)) + pair * len(R_SUMS)
                        dve.wait_ge(mat_summed[s], sums + 1)
                        last = tt(Gm, A, ident[:].unsqueeze(1).broadcast_to([P, 4, P]), ALU.add)
                        if rw:
                            step.mark(last)
                        else:
                            last.then_inc(mat_summed[s], 1)
                        tt(Q, Q, A, ALU.subtract).then_inc(mat_summed[s], 1)
                    if pair == 0:
                        ready_gdn(L)
                    for what in ("gen1", "gen2", "last1", "gen3", "gen4", "last2"):
                        if not rw and what == "gen1":
                            dve.wait_ge(hn_summed, 3 * L + 1)
                            for i in range(2):
                                half = KK[:, i * 512:(i + 1) * 512]
                                last = stt(half, ps[:, 4 * i, :], -1.0 / HD, half, ALU.mult, ALU.add)
                            last.then_inc(hn_dve, 1)
                        if not rw and what == "gen4":
                            dve.wait_ge(hn_act, 4 * L + 2)
                            step(nc.vector.reciprocal(dev_root, dev_root))
                            by_channel(SQ, dev_root).then_inc(hn_inverted, 1)
                        if not rw and what == "gen3":
                            low_out(L, 0)
                        for s in range(2):
                            Gm = DG[s][:, :, P:2 * P]
                            dve.wait_ge(mat_done[s], base + steps[what])
                            tt(Gm, ps[:, 4 * s + 3, :].rearrange("p (q n) -> p q n", q=4), Gm,
                               ALU.add).then_inc(mat_summed[s], 1)
                    if not rw:
                        dve.wait_ge(hn_spread, 2 * L + 1)
                        for i in range(2):
                            half = KK[:, i * 512:(i + 1) * 512]
                            last = tt(half, half, ps[:, 4 * i, :], ALU.mult)
                        last.then_inc(hn_dve, 1)
                        dve.wait_ge(hn_dve, 4 * L + 2)
                        for t in range(NT):
                            cut = slice(t * T, (t + 1) * T)
                            step.mark(ts(KK[:, cut], KK[:, cut], v_at(L, V_LG + t), v_at(L, V_LB + t),
                                         ALU.mult, ALU.add))
                    if not rw:
                        dve.wait_ge(dve_steps, step.n)
                        step.mark(tt(KK, KK, view(o_R, 1024), ALU.add))
                        for s in range(2):
                            g = 2 * pair + s
                            dve.wait_ge(mat_done[s], base + steps["z1"])
                            src = ps[:, 4 * s, 0:2 * P]
                            vb = TVB[:, 1, 2 * (g - 4) * P:(2 * (g - 4) + 2) * P]
                            tt(ZB[s].rearrange("p q n -> p (q n)"), src, vb, ALU.add).then_inc(mat_summed[s], 1)
                        dve.wait_ge(dve_steps, step.n)
                        tt(KK, KK, G, ALU.mult).then_inc(hn_dve, 1)
                    for s in range(2):
                        g = 2 * pair + s
                        dve.wait_ge(mat_done[s], base + steps["o"])
                        if rw:
                            last = nc.vector.tensor_copy(KK[:, g * T:(g + 1) * T], ps[:, 4 * s + 3, 0:T])
                        else:
                            last = nc.vector.tensor_copy(OG[:, (g - 4) * 512:(g - 3) * 512], ps[:, 4 * s + 3, :])
                        last.then_inc(mat_summed[s], 1)

            def finish_mixer(L):
                def branch_low(n, dst, src, high_part):
                    dve.wait_ge(branch_high, 4 * L + n + 1)
                    less_high(dst, src, high_part).then_inc(branch_split, 1)

                branch_low(0, KK_low, KK, KK_high)
                dve.wait_ge(hn_act, 4 * L + 4)
                nc.vector.reciprocal(gdn_root, gdn_root).then_inc(hn_inverted, 1)
                low_out(L, 1)
                low_out(L, 2)
                dve.wait_ge(hn_spread, 2 * L + 2)
                step(tt(OG, OG, banks(4, 1024), ALU.mult))
                stt(OG, OG, v_at(L, V_GN), Z, ALU.mult, ALU.mult).then_inc(hn_dve, 1)
                branch_low(1, OG_low, OG, OG_high)
                for i in range(2):
                    dve.wait_ge(slab_done, first["mix", L] + N_IN + i + 1)
                    step.mark(tt(YT[:, i * 1024:(i + 1) * 1024], banks(2 * i, 1024),
                                 GATES[:, i * 1024:(i + 1) * 1024], ALU.mult))
                    if i == 0:
                        low_out(L, 3)
                for i in range(2):
                    dve.wait_ge(slab_done, first["mix", L] + N_IN + i + 3)
                    cut = slice(i * 1024, (i + 1) * 1024)
                    yb = GATES[:, 2048 + i * 1024:2048 + (i + 1) * 1024]
                    step(tt(yb, banks(4 + 2 * i, 1024), yb, ALU.mult))
                    tt(YT[:, cut], YT[:, cut], yb, ALU.add).then_inc(merged, 1)
                    if i == 0:
                        low_out(L, 4)
                    branch_low(2 + i, YT_low[:, cut], YT[:, cut], YT_high[:, cut])
                    low_out(L, 5 + i)
                for j in range(4):
                    dve.wait_ge(slab_done, first["mix", L] + N_IN + 4 + j + 1)
                    xs = xT[:, 2 * j:2 * j + 2, :].rearrange("p k n -> p (k n)")
                    tt(xs, ps[:, j, :], xs, ALU.add).then_inc(mixed, 1)
                    if j == 0:
                        low_out(L, 7)

            def dense(L):
                s0 = first["ffn", L]

                def make_low(i):
                    dve.wait_ge(slab_high, split_before["ffn", L] + i + 1)
                    less_high(low[i % FFN_RING], slab(i % FFN_RING), high[i % HIGHS]).then_inc(slab_split, 1)

                make_low(0)
                norm(2 * L + 1, V_N2, hT_high, hT_low)
                make_low(1)
                make_low(2)
                for i, (kind, j) in enumerate(FFN_ORDER):
                    if kind == "u":
                        dve.wait_ge(ffn_act, j + 1)
                        dve.wait_ge(slab_done, s0 + i + 1)
                        if j:
                            dve.wait_ge(ffn_split, j)
                        tt(FH, ps[:, 2 * (j % 2) + 1, :], FG[:, j % 2, :], ALU.mult).then_inc(ffn_dve, 1)
                    if i + HIGHS < N_FFN:
                        make_low(i + HIGHS)
                    if kind == "u":
                        dve.wait_ge(ffn_high, j + 1)
                        less_high(FH_low[:, j % 2, :], FH, FH_high[:, j % 2, :]).then_inc(ffn_split, 1)
                dve.wait_ge(slab_done, s0 + N_FFN)
                for j in range(4):
                    xs = xT[:, 2 * j:2 * j + 2, :].rearrange("p k n -> p (k n)")
                    tt(xs, ps[:, 4 + j, :], xs, ALU.add).then_inc(ffn_added, 1)

            def no_output():
                nc.vector.memset(PC, 0.0)
                nc.vector.memset(YE, 0.0).then_inc(zeroed, 1)

            def route():
                no_output()
                step.mark(nc.vector.memset(chosen9, 0.0))
                step.mark(nc.vector.memset(pos9, 0.0))
                dve.wait_ge(logits_done, 1)
                step(nc.vector.tensor_copy(logits, ps[:, 0, 0:2 * NE].rearrange("p (a n) -> p a n", a=2)))
                for a in range(2):
                    step(nc.vector.max(top[:, a, :], logits[:, a, :]))
                    step(nc.vector.max_index(topi[:, a, :], top[:, a, :], logits[:, a, :]))
                step(nc.vector.tensor_copy(topi_f, topi[:]))
                tt(g_diff, top[:, :, 1], top[:, :, 0], ALU.subtract).then_inc(diff_made, 1)
                for a in range(2):
                    step.mark(ts(hot1[:, a, :], slots[:, 0:NE], topi_f[:, a, 0:1], None, ALU.is_equal))
                    step(ts(hot2[:, a, :], slots[:, 0:NE], topi_f[:, a, 1:2], None, ALU.is_equal))
                tt(chosen, hot1, hot2, ALU.add).then_inc(routed, 1)
                dve.wait_ge(tok_kept, 2)
                less_high(h_tok_low.rearrange("p a n -> p (a n)"), banks(4, 2048),
                          h_tok_high.rearrange("p a n -> p (a n)")).then_inc(norm_split, 1)
                dve.wait_ge(exp_made, 1)
                step(ts(g_first, g_exp, 1.0, None, ALU.add))
                step(nc.vector.reciprocal(g_first, g_first))
                step(tt(g_second, g_exp, g_first, ALU.mult))
                dve.wait_ge(routed, 1)
                for a in range(2):
                    step.mark(ts(hot1[:, a, :], hot1[:, a, :], g_first[:, a:a + 1], None, ALU.mult))
                    step(ts(hot2[:, a, :], hot2[:, a, :], g_second[:, a:a + 1], None, ALU.mult))
                step.mark(tt(combine, hot1, hot2, ALU.add))
                dve.wait_ge(pos_done, 1)
                step(nc.vector.tensor_copy(pos, ps[:, 1, 0:2 * NE].rearrange("p (a n) -> p a n", a=2)))
                step(nc.vector.reduce_max(most, ps[:, 1, 2 * NE:3 * NE], AX_X))
                ts(over[:], most, float(P), None, ALU.is_gt).then_inc(over_made, 1)

            def experts(lap):
                s0 = first["moe", 1] + lap * NE * N_FFN
                if lap:
                    no_output()
                    ts(pos9, pos9, -float(P), None, ALU.add).then_inc(pos_moved, 1)
                    dve.wait_ge(pos_moved, 1)

                def make_hot(e):
                    for a in range(2):
                        last = ts(PT[:, a, :], slots[:], pos9[:, a, bass.ds(e, 1)], chosen9[:, a, bass.ds(e, 1)],
                                  ALU.is_equal, ALU.mult)
                    last.then_inc(hot_made, 1)

                def split_tokens(e):
                    dve.wait_ge(gather_kept, e + (lap * (NE + 1) + 1))
                    less_high(XS_low, ps[:, 0:2, :].rearrange("p b (k n) -> p (b k) n", n=P),
                              XS_high).then_inc(gather_split, 1)

                def add_up(e, halves):
                    for a in halves:
                        dve.wait_ge(scattered, 2 * e + (2 * lap * (NE + 1) + a + 1))
                        tt(x_tok[:, a, :], banks(4 + 2 * a, 1024), x_tok[:, a, :], ALU.add).then_inc(added, 1)

                make_hot(0)
                split_tokens(0)
                with dve.Fori(0, NE) as e:
                    chunks = e * FC + lap * NE * FC

                    def make_low(i):
                        dve.wait_ge(slab_high, e * N_FFN + (split_before["moe", 1] + lap * NE * N_FFN + i + 1))
                        less_high(low[i % FFN_RING], slab(i % FFN_RING), high[i % HIGHS]).then_inc(slab_split, 1)

                    def split_h(j):
                        dve.wait_ge(e_high, chunks + (j + 1))
                        less_high(FH_low[:, j % 2, 0:T], ps[:, 6 + j % 2, 0:T], FH_high[:, j % 2, 0:T]).then_inc(e_split, 1)

                    make_low(0)
                    make_low(1)
                    for a in range(2):
                        last = ts(PTC[:, a, :], slots[:], pos9[:, a, bass.ds(e, 1)], combine[:, a, bass.ds(e, 1)],
                                  ALU.is_equal, ALU.mult)
                    last.then_inc(weights_made, 1)
                    add_up(e, (0,))
                    make_low(2)
                    add_up(e, (1,))
                    for i, (kind, j) in enumerate(FFN_ORDER):
                        if kind == "u":
                            dve.wait_ge(e_act, chunks + (j + 1))
                            dve.wait_ge(slab_done, e * N_FFN + (s0 + i + 1))
                            tt(FH[:, 0:T], ps[:, 4 + j % 2, 0:T], FG[:, j % 2, 0:T], ALU.mult).then_inc(e_dve, 1)
                        if kind == "g" and j:
                            split_h(j - 1)
                        if i + HIGHS < N_FFN:
                            make_low(i + HIGHS)
                        if (kind, j) == ("d", 5):
                            make_hot(e + 1)
                    split_tokens(e + 1)
                    split_h(FC - 1)
                add_up(NE, (0, 1))

            dve.wait_ge(consts_made, 1)
            dve.wait_ge(x_kept, 4)
            for L in range(DEPTH):
                dve.wait_ge(vec_kept, 2 * L + 1)
                ts(one_less_mu[:, L, :], vec[:, L, V_MU:V_MU + 14], -1.0, 1.0, ALU.mult, ALU.add).then_inc(vec_kept, 1)
                project(L)
                turn_tokens(L)
                groups(L)
                finish_mixer(L)
                if L == 0:
                    dense(L)
            norm(3, V_N2)
            route()
            experts(0)
            more = dve.value_load(over[0:1, 0:1])
            with dve.If(more > 0):
                experts(1)
            nc.vector.memset(most, 0.0).then_inc(moe_added, 1)
            dve.wait_ge(fin_in, 16)
            dve.wait_ge(fin_root, 1)
            step(nc.vector.reciprocal(xsum, xsum))
            for a in range(2):
                stt(x_tok_out[:, a, :], x_tok[:, a, :], xsum[:, a:a + 1], fin_g, ALU.mult, ALU.mult).then_inc(fin_made, 1)


_INS = ['x', 'norm1_g', 'w_in', 'tshift_mu', 'w0', 'w_decay_up', 'a0', 'w_iclr_up', 'w_gate_up', 'k_k', 'k_a', 'r_k',
        'lnx_g', 'lnx_b', 'w_pa', 'conv_w', 'a_log', 'dt_bias', 'gdn_norm_g', 'w_pb', 'w_out', 'norm2_g',
        'ffn_w_gate', 'ffn_w_up', 'ffn_w_down', 'moe_router', 'moe_w_gate', 'moe_w_up', 'moe_w_down', 'final_g']
_OUTS = [((1, T, D), 'float32')]


def kernel(**inputs):
    import numpy as _np
    import concourse.bacc as _bacc
    from concourse import mybir as _mybir
    from concourse.bass_utils import run_bass_kernel_spmd as _run

    nc = _bacc.Bacc("TRN2", target_bir_lowering=False, num_devices=1)
    arrays, args = {}, []
    for name in _INS:
        a = _np.ascontiguousarray(inputs[name])
        arrays[f"in_{name}_dram"] = a
        args.append(nc.dram_tensor(f"in_{name}_dram", a.shape, _mybir.dt.from_np(a.dtype), kind="ExternalInput").ap())
    for i, (shape, dtype) in enumerate(_OUTS):
        dt = _mybir.dt.from_np(_np.dtype(dtype))
        args.append(nc.dram_tensor(f"out_{i}_dram", shape, dt, kind="ExternalOutput").ap())
    trunk(nc, *args)
    r = _run(nc, [arrays], core_ids=[0])
    return r.results[0]["out_0_dram"]
```
